# Optimizing a Trainium2 kernel written in Bass

```python
import jax, jax.numpy as jnp
from jax import lax
import numpy as np

D_MODEL = 1024
BATCH = 1
SEQ = 512
DEPTH = 1
DEC_BATCH = 8
DEC_SEQ = 4
PAST_LEN = 4096
PAGE_SIZE = 128

PLE_DIM = 256
POOL_WIDTH = D_MODEL // 2
POOL_WINDOWS = (2, 4, 8, 16)
POOL_GROUPS = len(POOL_WINDOWS)
POOL_GROUP_DIM = POOL_WIDTH // POOL_GROUPS
POOL_STATE = max(POOL_WINDOWS) - 1
RWKV_WIDTH = D_MODEL // 2
RWKV_HEAD_DIM = 64
RWKV_HEADS = RWKV_WIDTH // RWKV_HEAD_DIM
DECAY_LORA = 64
AAA_LORA = 64
GATE_LORA = 128
SHIFT_WIDTH = 3 * RWKV_WIDTH + DECAY_LORA + AAA_LORA + GATE_LORA
SHIFT_SPLITS = (RWKV_WIDTH, 2 * RWKV_WIDTH, 3 * RWKV_WIDTH,
                3 * RWKV_WIDTH + DECAY_LORA, 3 * RWKV_WIDTH + DECAY_LORA + AAA_LORA)
IN_WIDTH = POOL_WIDTH + SHIFT_WIDTH + 2 * D_MODEL
N_GROUPS = 4
EXPERTS_PER_GROUP = 8
N_EXPERTS = N_GROUPS * EXPERTS_PER_GROUP
TOP_K_IN_GROUP = 2
D_EXPERT = 256
RMS_EPS = 1e-6
GN_EPS = 64e-5

kernel_name = "pool_rwkv7_hier_moe_ple_decode_step"

def rmsnorm(x, g):
    xf = x.astype(jnp.float32)
    y = xf * lax.rsqrt(jnp.mean(xf * xf, axis=-1, keepdims=True) + RMS_EPS)
    return (y * g.astype(jnp.float32)).astype(x.dtype)

def pool_mixer(u, u_past, pos0, mix, scale):
    B, T, _ = u.shape
    f32 = jnp.float32
    u_ext = jnp.concatenate([u_past.astype(u.dtype), u], axis=1)
    uf = u_ext.astype(f32)
    cs = jnp.concatenate([jnp.zeros_like(uf[:, :1]), jnp.cumsum(uf, axis=1)], axis=1)
    pos = pos0 + jnp.arange(T)
    end = cs[:, POOL_STATE + 1:]
    cur = uf[:, POOL_STATE:]
    outs = []
    for g, w in enumerate(POOL_WINDOWS):
        sl = slice(g * POOL_GROUP_DIM, (g + 1) * POOL_GROUP_DIM)
        start = cs[:, POOL_STATE + 1 - w:POOL_STATE + 1 - w + T, sl]
        cnt = jnp.minimum(pos + 1, w).astype(f32)[None, :, None]
        outs.append((end[..., sl] - start) / cnt - cur[..., sl])
    pooled = jnp.stack(outs, axis=2)
    y = jnp.einsum('btgc,gcd->btgd', pooled, mix.astype(f32)).reshape(B, T, POOL_WIDTH)
    y = y * scale.astype(f32)
    return y.astype(u.dtype), u_ext[:, -POOL_STATE:]

def _wkv_step(s, inp):
    r, w, k, v, a, b = inp
    sa = jnp.einsum('bhvk,bhk->bhv', s, a)
    s = s * w[:, :, None, :] + sa[..., None] * b[:, :, None, :] + v[..., None] * k[:, :, None, :]
    return s, jnp.einsum('bhvk,bhk->bhv', s, r)

def rwkv7_mixer(z, shift_past, wkv_past, mu, w0, w2, a0, a2, g2, k_k, k_a, r_k, ln_w, ln_b):
    B, T, _ = z.shape
    f32 = jnp.float32
    z_ext = jnp.concatenate([shift_past[:, None, :].astype(z.dtype), z], axis=1)
    zc = z.astype(f32)
    zm = zc + (z_ext[:, :-1].astype(f32) - zc) * mu
    r, k, v, wd, ad, gd = jnp.split(zm, SHIFT_SPLITS, axis=-1)
    w_log = -jax.nn.softplus(-(w0 + jnp.tanh(wd) @ w2)) - 0.5
    decay = jnp.exp(-jnp.exp(w_log))
    a = jax.nn.sigmoid(a0 + ad @ a2)
    g = jax.nn.sigmoid(gd) @ g2
    hd = lambda t: t.reshape(B, T, RWKV_HEADS, RWKV_HEAD_DIM)
    kk = hd(k * k_k)
    kk = kk / jnp.maximum(jnp.sqrt(jnp.sum(kk * kk, axis=-1, keepdims=True)), 1e-12)
    k = k * (1.0 + (a - 1.0) * k_a)
    r_h, w_h, k_h, v_h, a_h = hd(r), hd(decay), hd(k), hd(v), hd(a)
    seq = tuple(jnp.swapaxes(t, 0, 1) for t in (r_h, w_h, k_h, v_h, -kk, kk * a_h))
    s_last, o = lax.scan(_wkv_step, wkv_past.astype(f32), seq)
    o = jnp.swapaxes(o, 0, 1)
    mean = jnp.mean(o, axis=-1, keepdims=True)
    var = jnp.mean(jnp.square(o - mean), axis=-1, keepdims=True)
    o = ((o - mean) * lax.rsqrt(var + GN_EPS)).reshape(B, T, RWKV_WIDTH) * ln_w + ln_b
    bonus = jnp.sum(r_h * k_h * r_k, axis=-1, keepdims=True) * v_h
    o = (o + bonus.reshape(B, T, RWKV_WIDTH)) * g
    return o.astype(z.dtype), z_ext[:, -1], s_last

def hier_moe(h, w_rg, b_rg, w_re, b_re, e_gate, e_up, e_down):
    B, T, D = h.shape
    f32 = jnp.float32
    hf = h.reshape(-1, D)
    glog = (hf @ w_rg).astype(f32) + b_rg
    gprob = jax.nn.softmax(glog, axis=-1)
    _, gsel = lax.top_k(glog, 1)
    pg = jnp.take_along_axis(gprob, gsel, axis=-1)
    elog = ((hf @ w_re).astype(f32) + b_re).reshape(-1, N_GROUPS, EXPERTS_PER_GROUP)
    elog = jnp.take_along_axis(elog, gsel[:, :, None], axis=1)[:, 0]
    tv, ti = lax.top_k(elog, TOP_K_IN_GROUP)
    pe = jax.nn.softmax(tv, axis=-1) * pg
    eidx = gsel * EXPERTS_PER_GROUP + ti
    comb = jnp.sum(jax.nn.one_hot(eidx, N_EXPERTS, dtype=f32) * pe[..., None], axis=1)
    y = jnp.zeros(hf.shape, f32)
    for e in range(N_EXPERTS):
        hid = jax.nn.silu(hf @ e_gate[e]) * (hf @ e_up[e])
        y = y + comb[:, e:e + 1] * (hid @ e_down[e]).astype(f32)
    return y.reshape(B, T, D).astype(h.dtype)

def decoder_layer(x, p, pool_past, shift_past, wkv_past, pos0, lp):
    dt = x.dtype
    f32 = jnp.float32
    h = rmsnorm(x, lp['norm_mix'])
    proj = h @ lp['w_in']
    o1 = POOL_WIDTH
    o2 = o1 + SHIFT_WIDTH
    o3 = o2 + D_MODEL
    u, z, gate_a, gate_b = proj[..., :o1], proj[..., o1:o2], proj[..., o2:o3], proj[..., o3:]
    y_a, pool_new = pool_mixer(u, pool_past, pos0, lp['pool_mix'], lp['pool_scale'])
    y_b, shift_new, wkv_new = rwkv7_mixer(
        z, shift_past, wkv_past, lp['shift_mu'], lp['decay_w0'], lp['decay_w2'], lp['iclr_a0'],
        lp['iclr_a2'], lp['gate_g2'], lp['k_k'], lp['k_a'], lp['r_k'], lp['ln_x_w'], lp['ln_x_b'])
    merged = (jax.nn.sigmoid(gate_a.astype(f32)) * (y_a @ lp['w_branch_a']).astype(f32)
              + jax.nn.sigmoid(gate_b.astype(f32)) * (y_b @ lp['w_branch_b']).astype(f32))
    x = x + (merged.astype(dt) @ lp['w_out']).astype(dt)
    h = rmsnorm(x, lp['norm_ffn'])
    x = x + hier_moe(h, lp['w_route_group'], lp['b_route_group'], lp['w_route_expert'],
                     lp['b_route_expert'], lp['expert_gate'], lp['expert_up'], lp['expert_down'])
    h = rmsnorm(x, lp['norm_ple'])
    ple = jax.nn.sigmoid((h @ lp['w_ple_gate']).astype(f32)) * (p.astype(dt) @ lp['w_ple_proj']).astype(f32)
    x = x + ple.astype(dt)
    return x, pool_new.astype(dt), shift_new.astype(dt), wkv_new.astype(dt)

def setup_inputs(seed: int = 0) -> dict:
    key = jax.random.key(seed)
    ks = list(jax.random.split(key, 48))
    f32 = jnp.float32
    L = DEPTH

    def nrm(shape, scale):
        return scale * jax.random.normal(ks.pop(), shape, f32)

    def uni(shape, lo, hi):
        return jax.random.uniform(ks.pop(), shape, f32, lo, hi)

    return {
        'x_prompt': nrm((BATCH, SEQ, D_MODEL), 1.0),
        'x_sample': nrm((DEC_BATCH, DEC_SEQ, D_MODEL), 1.0),
        'state_pool': nrm((L, DEC_BATCH, POOL_STATE, POOL_WIDTH), 1.0),
        'state_shift': nrm((L, DEC_BATCH, SHIFT_WIDTH), 1.0),
        'state_wkv': nrm((L, DEC_BATCH, RWKV_HEADS, RWKV_HEAD_DIM, RWKV_HEAD_DIM), 0.5),
        'p_prompt': nrm((L, BATCH, SEQ, PLE_DIM), 1.0),
        'p_sample': nrm((L, DEC_BATCH, DEC_SEQ, PLE_DIM), 1.0),
        'norm_mix': 1.0 + nrm((L, D_MODEL), 0.05),
        'w_in': nrm((L, D_MODEL, IN_WIDTH), D_MODEL ** -0.5),
        'pool_mix': nrm((L, POOL_GROUPS, POOL_GROUP_DIM, POOL_GROUP_DIM), POOL_GROUP_DIM ** -0.5),
        'pool_scale': 1.0 + nrm((L, POOL_WIDTH), 0.1),
        'w_branch_a': nrm((L, POOL_WIDTH, D_MODEL), POOL_WIDTH ** -0.5),
        'shift_mu': uni((L, SHIFT_WIDTH), 0.0, 1.0),
        'decay_w0': uni((L, RWKV_WIDTH), -5.0, -0.5),
        'decay_w2': nrm((L, DECAY_LORA, RWKV_WIDTH), 0.1 * DECAY_LORA ** -0.5),
        'iclr_a0': nrm((L, RWKV_WIDTH), 0.5),
        'iclr_a2': nrm((L, AAA_LORA, RWKV_WIDTH), 0.5 * AAA_LORA ** -0.5),
        'gate_g2': nrm((L, GATE_LORA, RWKV_WIDTH), GATE_LORA ** -0.5),
        'k_k': 0.85 + nrm((L, RWKV_WIDTH), 0.05),
        'k_a': 1.0 + nrm((L, RWKV_WIDTH), 0.05),
        'r_k': nrm((L, RWKV_HEADS, RWKV_HEAD_DIM), 0.1),
        'ln_x_w': 1.0 + nrm((L, RWKV_WIDTH), 0.05),
        'ln_x_b': nrm((L, RWKV_WIDTH), 0.01),
        'w_branch_b': nrm((L, RWKV_WIDTH, D_MODEL), RWKV_WIDTH ** -0.5),
        'w_out': nrm((L, D_MODEL, D_MODEL), D_MODEL ** -0.5),
        'norm_ffn': 1.0 + nrm((L, D_MODEL), 0.05),
        'w_route_group': nrm((L, D_MODEL, N_GROUPS), D_MODEL ** -0.5),
        'b_route_group': nrm((L, N_GROUPS), 0.01),
        'w_route_expert': nrm((L, D_MODEL, N_EXPERTS), D_MODEL ** -0.5),
        'b_route_expert': nrm((L, N_EXPERTS), 0.01),
        'expert_gate': nrm((L, N_EXPERTS, D_MODEL, D_EXPERT), D_MODEL ** -0.5),
        'expert_up': nrm((L, N_EXPERTS, D_MODEL, D_EXPERT), D_MODEL ** -0.5),
        'expert_down': nrm((L, N_EXPERTS, D_EXPERT, D_MODEL), D_EXPERT ** -0.5),
        'norm_ple': 1.0 + nrm((L, D_MODEL), 0.05),
        'w_ple_gate': nrm((L, D_MODEL, D_MODEL), D_MODEL ** -0.5),
        'w_ple_proj': nrm((L, PLE_DIM, D_MODEL), PLE_DIM ** -0.5),
        'norm_final': 1.0 + nrm((D_MODEL,), 0.05),
    }

def reference(x_prompt, x_sample, state_pool, state_shift, state_wkv, p_prompt, p_sample,
              norm_mix, w_in, pool_mix, pool_scale, w_branch_a, shift_mu, decay_w0, decay_w2,
              iclr_a0, iclr_a2, gate_g2, k_k, k_a, r_k, ln_x_w, ln_x_b, w_branch_b, w_out,
              norm_ffn, w_route_group, b_route_group, w_route_expert, b_route_expert,
              expert_gate, expert_up, expert_down, norm_ple, w_ple_gate, w_ple_proj, norm_final):
    dt = x_prompt.dtype
    xp, xs = x_prompt, x_sample
    pool_p, shift_p, wkv_p, pool_s, shift_s, wkv_s = [], [], [], [], [], []
    for l in range(DEPTH):
        lp = dict(norm_mix=norm_mix[l], w_in=w_in[l], pool_mix=pool_mix[l], pool_scale=pool_scale[l],
                  w_branch_a=w_branch_a[l], shift_mu=shift_mu[l], decay_w0=decay_w0[l],
                  decay_w2=decay_w2[l], iclr_a0=iclr_a0[l], iclr_a2=iclr_a2[l], gate_g2=gate_g2[l],
                  k_k=k_k[l], k_a=k_a[l], r_k=r_k[l], ln_x_w=ln_x_w[l], ln_x_b=ln_x_b[l],
                  w_branch_b=w_branch_b[l], w_out=w_out[l], norm_ffn=norm_ffn[l],
                  w_route_group=w_route_group[l], b_route_group=b_route_group[l],
                  w_route_expert=w_route_expert[l], b_route_expert=b_route_expert[l],
                  expert_gate=expert_gate[l], expert_up=expert_up[l], expert_down=expert_down[l],
                  norm_ple=norm_ple[l], w_ple_gate=w_ple_gate[l], w_ple_proj=w_ple_proj[l])
        b = xp.shape[0]
        zero_pool = jnp.zeros((b, POOL_STATE, POOL_WIDTH), dt)
        zero_shift = jnp.zeros((b, SHIFT_WIDTH), dt)
        zero_wkv = jnp.zeros((b, RWKV_HEADS, RWKV_HEAD_DIM, RWKV_HEAD_DIM), dt)
        xp, pp, sp, wp = decoder_layer(xp, p_prompt[l], zero_pool, zero_shift, zero_wkv, 0, lp)
        xs, ps, ss, ws = decoder_layer(xs, p_sample[l], state_pool[l], state_shift[l], state_wkv[l],
                                       PAST_LEN, lp)
        pool_p.append(pp); shift_p.append(sp); wkv_p.append(wp)
        pool_s.append(ps); shift_s.append(ss); wkv_s.append(ws)
    y_prompt = rmsnorm(xp, norm_final)
    y_sample = rmsnorm(xs, norm_final)
    return (y_prompt, y_sample, jnp.stack(pool_p), jnp.stack(shift_p), jnp.stack(wkv_p),
            jnp.stack(pool_s), jnp.stack(shift_s), jnp.stack(wkv_s))


_drawn_inputs = setup_inputs


def setup_inputs(seed=0):
    import zlib

    import numpy as np

    out = dict(_drawn_inputs(seed))
    spreads = {}
    factors = {'decay_w2': 5.768,
     'ln_x_b': 8.0,
     'b_route_group': 4.71,
     'b_route_expert': 3.458,
     'norm_ple': 6.991}
    for name, (base, spread) in spreads.items():
        noise = np.random.default_rng([zlib.crc32(name.encode()), seed]).standard_normal(out[name].shape)
        drawn = base * np.exp(spread * noise) if base else spread * noise
        out[name] = __import__('jax').numpy.asarray(drawn.astype(out[name].dtype))
    for name, factor in factors.items():
        out[name] = (out[name] * factor).astype(out[name].dtype)
    return out
```

```python
import concourse.bass as bass
from concourse import mybir
from contextlib import ExitStack
import numpy as np
import math

F32 = mybir.dt.float32
ALU = mybir.AluOpType
ACT = mybir.ActivationFunctionType
AX = mybir.AxisListType

P = 128
D = 1024
KD = D // P
NPR, NB, TS = 512, 8, 4
NSM = NB * TS
T = NPR + NSM
HT = T // 2
H, HD = 8, 64
J = H // 2
C = NPR // HD
L = 64
NTILE = 5
ROWS = [P, P, P, P, NSM]
ZB = 14
DECAY = math.exp(-0.5)
GN_EPS = 64e-5
RMS_EPS = 1e-6

def const_layout():
    at, out = 0, {}
    for name, n in (("ident", 128), ("pair", 128), ("pairmean", 128), ("gmask", 128), ("gmask_s", 64),
                    ("bmask", 8), ("mt_s", 32), ("m_s", 32), ("up32", 32), ("inv", 64), ("eps", 1), ("seg", T)):
        out[name] = (at, n)
        at += n
    return out, at

CONST, NCONST = const_layout()


def make_consts():
    c = np.zeros((P, NCONST), np.float32)
    def put(name, a):
        at, n = CONST[name]
        c[:a.shape[0], at:at + n] = a
    p = np.arange(P)
    put("ident", np.eye(P))
    pair = (p[:, None] // 64 == p[None, :] // 64).astype(np.float32)
    put("pair", pair)
    put("pairmean", pair / 64)
    s = np.arange(64)
    strict = (s[:, None] < s[None, :]).astype(np.float32)
    incl = (s[:, None] <= s[None, :]).astype(np.float32)
    put("gmask", np.tile(np.concatenate([strict, incl], 1), (2, 1)))
    q = np.arange(32)
    same = q[:, None] // 4 == q[None, :] // 4
    ss, si = same & (q[:, None] < q[None, :]), same & (q[:, None] <= q[None, :])
    put("gmask_s", np.tile(np.concatenate([ss, si], 1).astype(np.float32), (2, 1)))
    put("bmask", np.tile((q[:, None] // 4 == np.arange(8)[None, :]).astype(np.float32), (2, 1)))
    put("mt_s", ss.astype(np.float32))
    put("m_s", ss.T.astype(np.float32))
    up = (q[:, None] < q[None, :]).astype(np.float32)
    put("up32", np.tile(up, (2, 1)))
    inv = np.stack([1.0 / np.minimum(np.arange(16) + 1, 2 << g) for g in range(4)])
    put("inv", np.tile(inv.reshape(1, 64), (P, 1)))
    put("eps", np.full((P, 1), GN_EPS))
    seg = np.ones(T)
    seg[0:NPR:L] = 0
    seg[NPR::TS] = 0
    put("seg", np.tile(seg[None], (P, 1)))
    return c


def mixer(nc, a, o, ctx, BIG, PB, PQ, bank, kept):
    def sb(name, shape, dt=F32):
        return ctx.enter_context(nc.sbuf_tensor(name, shape, dt))

    def sem(name):
        return nc.alloc_semaphore(name=name)

    W8 = 4 * T
    slot = lambda i, n=W8: BIG[:, i * W8:i * W8 + n]
    R, K, V, SG, A, CS, KQ, NR = [slot(i).rearrange("p (j t) -> p j t", j=J) for i in range(8)]
    xt = BIG[:, 5 * W8:5 * W8 + NTILE * D].rearrange("p (n d) -> p n d", n=NTILE)
    CW = C * 128 + 64
    ARBK = sb("ARBK", [P, 2 * J * CW])
    AR = ARBK[:, 0:J * CW].rearrange("p (j x) -> p j x", j=J)
    BK = ARBK[:, J * CW:2 * J * CW].rearrange("p (j x) -> p j x", j=J)
    hT = sb("hT", [P, KD, T])
    NU = 5
    ring = sb("ring", [P, NU, KD * P])
    merged = sb("merged", [P, KD, T])
    zx = sb("zx", [P, 2, T + 1])
    dz = sb("dz", [P, T])
    twa = sb("twa", [P, T])
    sgd = sb("sgd", [P, T])
    sga = sb("sga", [P, 2, T])
    ux = sb("ux", [P, 15 + T])
    uxs = sb("uxs", [P, NB, 19])
    pt = sb("pt", [P, 2, 15 + NPR + NB * 19])
    pooled = sb("pooled", [P, J, T])
    mixw = merged[:, 7, 0:512].rearrange("p (g d) -> p g d", g=J)
    cst = sb("cst", [P, NCONST])
    w2z = merged[:, 5, 0:512]
    a2z = merged[:, 6, 0:512]
    g2w = sb("g2w", [P, 512])
    rows = sb("rows", [46, P])
    vec = sb("vec", [P, 46])
    omka = sb("omka", [P, J])
    gmix = sb("gmix", [P, KD])
    ss = sb("ss", [P, NTILE])
    sh_in = merged[0:NB, 0:4, :].rearrange("p a b -> p (a b)")[:, 0:ZB * P]
    stT = sb("stT", [P, ZB, NB])
    sh = sb("sh", [P, 9, ZB])
    shT = sb("shT", [9 * ZB, P])
    pl_in = merged[0:120, 4, 0:512]
    plT = sb("plT", [P, J, 120])
    ul = sb("ul", [P, J, 47])
    ulT = sb("ulT", [47, 512])
    GL = sb("GL", [P, J, C + NB])

    c_ = lambda name: cst[:, CONST[name][0]:CONST[name][0] + CONST[name][1]]
    ident, pair, pairmean = c_("ident"), c_("pair"), c_("pairmean")
    MU, W0, A0, KKW, KAW, RKW, LNW, LNB, PSC = 0, 14, 18, 22, 26, 30, 34, 38, 42

    def view(i, off, n, parts=P):
        return BIG[0:parts, i * W8 + off:i * W8 + off + n]
    az = [view(0, 512 * k, 512).rearrange("p (j q t) -> p j q t", j=J, q=2) for k in range(2)]
    MDs = view(1, 0, C * H * 32, 64).rearrange("p (n t) -> p n t", t=32)
    MOs = view(3, 0, C * H * 32, 32).rearrange("p (n t) -> p n t", t=32)
    MT = view(5, 0, 1024).rearrange("p (s t) -> p s t", s=32)
    XTi = view(5, 1024, 1024).rearrange("p (s t) -> p s t", s=32)
    tmpi = view(6, 0, 1024)
    XNi = view(6, 1024, 1024).rearrange("p (s t) -> p s t", s=32)
    XA = view(7, 0, C * H * 32, 32).rearrange("p (n t) -> p n t", t=32)
    XT = BIG[0:64, 5 * W8:5 * W8 + C * H * 64].rearrange("p (n t) -> p n t", t=64)
    P2T = view(1, 0, C * H * 32, 64).rearrange("p (n t) -> p n t", t=32)
    ARZ = [view(0, 1024 * k, 1024).rearrange("p (j q x t) -> p j q x t", j=J, q=2, x=2) for k in range(2)]
    Gs = [view(1, 1024 * k, 1024).rearrange("p (h x) -> p h x", h=H) for k in range(2)]
    BKt = [view(3, 512 * k, 512) for k in range(2)]
    SAV = [view(3, 1024 + 512 * k, 512) for k in range(2)]
    RHS = view(7, 0, 512, 64)
    S0z = view(7, 512, 512).rearrange("p (j q v) -> p j q v", j=J, q=2)
    Stmp = view(7, 1024, 256).rearrange("p (j v) -> p j v", j=J)
    SoT = twa[0:64, 0:512]
    OT = pooled

    LATE = KD - 5
    plan = []
    plan += [("z", 12, "a"), ("z", 13, "a")]
    plan += [("z", 4 + j, "a") for j in range(J)]
    plan += [("lw", j, "a") for j in range(J)] + [("la", j, "a") for j in range(J)]
    plan += [("z", j, "a") for j in range(J)]
    plan += [("nrm", j, "a") for j in range(J)]
    plan += [("z", 8 + j, "a") for j in range(J)]
    plan += [("u", g, "a") for g in range(J)]
    plan += [("ga", 0, "a"), ("ga", 1, "a")]
    plan += [("mix", g, "v") for g in range(J)]
    plan += [("ba", 0, "v"), ("ba", 1, "v")]
    for m in range(2, LATE):
        plan += [("ga", m, "a"), ("ba", m, "v")]
    plan += [("bon", j, "v") for j in range(J)]
    N0 = len(plan)
    for m in range(LATE, KD):
        plan += [("ga", m, "a"), ("ba", m, "v")]
    N1 = len(plan)
    plan += [("gb", m, "a") for m in range(3)]
    plan += [("mean", j, "v") for j in range(J)] + [("gb", 3, "a")] + [("var", j, "a") for j in range(J)]
    plan += [("gb", m, "a") for m in range(4, KD)]
    plan += [("g2", j, "v") for j in range(J)]
    plan += [("bb", m, "v") for m in range(KD)]
    index = {(k, i): n for n, (k, i, _) in enumerate(plan)}
    taken = lambda n: sum(1 for q in plan[:n + 1] if q[2] == plan[n][2])

    units = []
    for kind, i, _ in plan:
        if kind == "z":
            units.append(("in", 4 + i))
        if kind == "u":
            units.append(("in", i))
        if kind == "ga":
            units.append(("in", 18 + i))
        if kind == "gb":
            units.append(("in", 26 + i))
        if kind == "ba" and i % 2 == 0:
            units.append(("ba", i))
        if kind == "bb" and i % 2 == 0:
            units.append(("bb", i))
    unit_no = {u: n for n, u in enumerate(units)}

    def unit_of(kind, i):
        if kind in ("z", "u", "ga", "gb"):
            return unit_no[("in", {"z": 4, "u": 0, "ga": 18, "gb": 26}[kind] + i)]
        if kind in ("ba", "bb"):
            return unit_no[(kind, i - i % 2)]
        return None
    last_use = {}
    for n, (kind, i, _) in enumerate(plan):
        if unit_of(kind, i) is not None:
            last_use[unit_of(kind, i)] = n

    s_const = sem("s_const"); s_rows = sem("s_rows"); s_x = [sem(f"s_x{n}") for n in range(NTILE)]
    s_gmix = sem("s_gmix"); s_shin = sem("s_shin"); s_plin = sem("s_plin"); s_lora = sem("s_lora"); s_mixw = sem("s_mixw")
    s_unit = [sem(f"s_unit{n}") for n in range(NU)]
    s_zero = sem("s_zero")
    s_sq = sem("s_sq"); s_ms = sem("s_ms"); s_rt = sem("s_rt"); s_xn = sem("s_xn"); s_xT = sem("s_xT"); s_hT = sem("s_hT")
    s_vecT = sem("s_vecT"); s_vec = sem("s_vec"); s_stTp = sem("s_stTp"); s_stT = sem("s_stT")
    s_plTp = sem("s_plTp"); s_plT = sem("s_plT")
    s_big = sem("s_big"); s_act_took = sem("s_act_took"); s_dve_took = sem("s_dve_took")
    s_zm = sem("s_zm"); s_zxfree = sem("s_zxfree"); s_twa = sem("s_twa"); s_sgd = sem("s_sgd")
    s_sh = sem("s_sh"); s_shTp = sem("s_shTp"); s_shT = sem("s_shT")
    s_ul = sem("s_ul"); s_ulTp = sem("s_ulTp"); s_ulT = sem("s_ulT"); s_pooled = sem("s_pooled")
    s_nsq = sem("s_nsq"); s_cs = sem("s_cs"); s_ex = sem("s_ex"); s_e0 = sem("s_e0"); s_rkk = sem("s_rkk"); s_hat = sem("s_hat")
    s_out = sem("s_out")
    s_v = sem("s_v"); s_p = sem("s_p"); s_a = sem("s_a")
    s_az0 = sem("s_az0"); s_az = sem("s_az"); s_g1 = sem("s_g1"); s_md = sem("s_md"); s_mdst = sem("s_mdst"); s_mt = sem("s_mt")
    s_inv = sem("s_inv"); s_xst = sem("s_xst"); s_xld = sem("s_xld"); s_p2 = sem("s_p2"); s_p2c = sem("s_p2c"); s_xo = sem("s_xo"); s_xoc = sem("s_xoc")
    s_arz = sem("s_arz"); s_gg = sem("s_gg"); s_gc = sem("s_gc"); s_bt = sem("s_bt"); s_btc = sem("s_btc"); s_vt = sem("s_vt"); s_vtc = sem("s_vtc")
    s_rhs = sem("s_rhs"); s_rhsc = sem("s_rhsc"); s_sa = sem("s_sa"); s_sac = sem("s_sac"); s_st = sem("s_st"); s_s0 = sem("s_s0"); s_o = sem("s_o"); s_oc = sem("s_oc")
    s_wT = sem("s_wT"); s_wTc = sem("s_wTc")

    mmd = nc.dram_tensor("mmd", (128, 32, 32), F32, kind="Internal").ap()
    xtd = nc.dram_tensor("xtd", (128, 32, 32), F32, kind="Internal").ap()
    xnd = nc.dram_tensor("xnd", (128, 32, 32), F32, kind="Internal").ap()


    half = lambda x: x.rearrange("p (q t) -> p q t", q=2)
    big = lambda n: PB[n % 2][:, :, 0:HT]
    prompt = lambda x: x[:, :, 0:NPR].rearrange("p j (c t) -> p j c t", t=L)
    ARp = AR[:, :, 0:C * 128].rearrange("p j (c x t) -> p j c x t", x=2, t=L)
    BKp = BK[:, :, 0:C * 128].rearrange("p j (c x t) -> p j c x t", x=2, t=L)
    ARs = AR[:, :, C * 128:CW].rearrange("p j (x t) -> p j x t", x=2)
    BKs = BK[:, :, C * 128:CW].rearrange("p j (x t) -> p j x t", x=2)
    zorder = [i for k, i, _ in plan if k == "z"]
    zpos = {i: n for n, i in enumerate(zorder)}
    counts = {}

    def took(eng, n):
        eng.wait_ge(s_act_took if plan[n][2] == "a" else s_dve_took, taken(n))


    S0S = BIG[:, 0:NB * J * 128].rearrange("p (b j q v) -> p b j q v", b=NB, j=J, q=2)
    arB = view(3, 0, W8).rearrange("p (j y) -> p j y", j=J)
    SL = BIG[0:64, 5 * W8:5 * W8 + NB * 512]
    arzS = view(7, 0, 512).rearrange("p (j q x) -> p j q x", j=J, q=2)
    GsS = view(7, 512, 512, 64).rearrange("p (h x) -> p h x", h=H)
    MTs = view(7, 1024, 256, 32)
    Ms = view(7, 1280, 256, 32)
    M2s = view(7, 1536, 256, 32)
    Xs = view(7, 1792, 256, 32)
    RHSs = dz[0:32, 0:512]
    zxf = zx[:, :, :].rearrange("p a b -> p (a b)")
    sgaf = sga[:, :, :].rearrange("p a b -> p (a b)")
    SAVs = zxf[0:64, 0:512]
    BKtS = sgaf[0:64, 0:512]
    OsS = sgaf[0:64, 512:1024]
    SAVm = [pt[:, k, 0:512].rearrange("p (b v) -> p b v", b=NB)[0:64] for k in range(2)]
    Sn = BIG[:, 5 * W8:5 * W8 + J * NB * 64].rearrange("p (j b v) -> p j b v", j=J, b=NB)
    WOUT = BIG[0:64, 0:NB * 512].rearrange("p (b x) -> p b x", b=NB)
    SF = view(7, 1792, 256).rearrange("p (j v) -> p j v", j=J)
    SB = BIG[:, 2 * W8:4 * W8].rearrange("p (m t) -> p m t", m=KD)
    SQ = [zx[:, 0, 0:T], zx[:, 1, 0:T], sga[:, 0, :], sga[:, 1, :]]
    WO = ARBK[:, 0:KD * D].rearrange("p (k m) -> p k m", k=KD)
    x0 = BIG[:, 5 * W8:5 * W8 + NTILE * D].rearrange("p (n d) -> p n d", n=NTILE)
    (s_wo, s_res, s_new, s_wout, s_yb, s_sqo, s_sl, s_sz, s_arb, s_slT, s_s0s, s_gs, s_gsc, s_ms_, s_msc, s_m2, s_m2c, s_m3, s_xs,
     s_vts, s_vtsc, s_bts, s_btsc, s_rs, s_rsc, s_sas, s_sasc, s_os, s_osc, s_osT, s_osTc, s_sm, s_sts, s_sn, s_gn) = [
        sem(n) for n in ("s_wo s_res s_new s_wout s_yb s_sqo s_sl s_sz s_arb s_slT s_s0s s_gs s_gsc s_ms_ s_msc s_m2 s_m2c s_m3 s_xs "
                         "s_vts s_vtsc s_bts s_btsc s_rs s_rsc s_sas s_sasc s_os s_osc s_osT s_osTc s_sm s_sts s_sn s_gn").split()]
    HN = BIG[:, 0:NTILE * D].rearrange("p (n d) -> p n d", n=NTILE)
    WT_N = 1 + NB

    s_xo2 = sem("s_xo2")
    s_moe, s_emb = sem("s_moe"), sem("s_emb")
    s_sqx, s_msx, s_rtx = sem("s_sqx"), sem("s_msx"), sem("s_rtx")
    block = ctx.enter_context(nc.Block())

    @block.sync
    def _(sp):
        sp.dma_start(cst[:, :], a["consts"]).then_inc(s_const, 16)
        for n in range(NTILE):
            src = a["x_prompt"][0, n * P:(n + 1) * P, :] if n < 4 else a["x_sample"].rearrange("b t d -> (b t) d")
            sp.dma_start(xt[0:ROWS[n], n, :], src).then_inc(s_x[n], 16)
        sp.dma_start(gmix[:, :], a["norm_mix"][0].rearrange("(p k) -> p k", k=KD)).then_inc(s_gmix, 16)
        for at, name, n in ((0, "shift_mu", ZB), (14, "decay_w0", 4), (18, "iclr_a0", 4), (22, "k_k", 4), (26, "k_a", 4),
                            (34, "ln_x_w", 4), (38, "ln_x_b", 4), (42, "pool_scale", 4)):
            sp.dma_start(rows[at:at + n, :], a[name][0].rearrange("(r c) -> r c", c=P)).then_inc(s_rows, 16)
        sp.dma_start(rows[30:34, :], a["r_k"][0].rearrange("(j q) d -> j (q d)", q=2)).then_inc(s_rows, 16)
        sp.dma_start(sh_in, a["state_shift"][0]).then_inc(s_shin, 16)
        for n, (kind, i) in enumerate(units):
            if n >= NU:
                sp.wait_ge(s_big, last_use[n - NU] + 1)
            if kind == "in":
                dst = ring[:, n % NU, :].rearrange("p (k m) -> p k m", k=KD)
                src = a["w_in"][0][:, i * P:(i + 1) * P].rearrange("(p k) m -> p k m", k=KD)
            else:
                dst = ring[:, n % NU, :].rearrange("p (k m) -> p k m", k=4)
                w = a["w_branch_a" if kind == "ba" else "w_branch_b"][0]
                src = w[:, i * P:(i + 2) * P].rearrange("(k p) m -> p k m", p=P)
            sp.dma_start(dst, src).then_inc(s_unit[n % NU], 16)
            if n == 1:
                sp.dma_start(w2z[0:64, :], a["decay_w2"][0]).then_inc(s_lora, 16)
                sp.dma_start(a2z[64:128, :], a["iclr_a2"][0]).then_inc(s_lora, 16)
                sp.dma_start(g2w[:, :], a["gate_g2"][0]).then_inc(s_lora, 16)
            if n == 3:
                sp.dma_start(pl_in, a["state_pool"][0].rearrange("b s c -> (b s) c")).then_inc(s_plin, 16)
                sp.dma_start(mixw, a["pool_mix"][0].rearrange("g c d -> c g d")).then_inc(s_mixw, 16)
                sp.dma_start(o["pool_sample"][0][:, 0:11, :], a["state_pool"][0][:, 4:15, :]).then_inc(s_out, 16)
            if units[n] == ("in", 18 + 3):
                sp.wait_ge(s_shT, 1)
                sp.dma_start(o["shift_prompt"][0].rearrange("b (r c) -> (b r) c", c=P), shT[0:ZB, :]).then_inc(s_out, 16)
                sp.dma_start(o["shift_sample"][0].rearrange("b (r c) -> (b r) c", c=P), shT[ZB:9 * ZB, :]).then_inc(s_out, 16)
                sp.wait_ge(s_ulT, 1)
                sp.dma_start(o["pool_prompt"][0, 0], ulT[0:15, :]).then_inc(s_out, 16)
                for b in range(NB):
                    sp.dma_start(o["pool_sample"][0, b, 11:15, :], ulT[15 + 4 * b:19 + 4 * b, :]).then_inc(s_out, 16)
        counts["out"] = 16 * (1 + 2 + 1 + NB)
        sp.wait_ge(s_wTc, WT_N)
        sp.dma_start(WO, a["w_out"][0].rearrange("(k p) m -> p k m", p=P)).then_inc(s_wo, 16)
        for n in range(NTILE):
            src = a["x_prompt"][0, n * P:(n + 1) * P, :] if n < 4 else a["x_sample"].rearrange("b t d -> (b t) d")
            sp.dma_start(x0[0:ROWS[n], n, :], src).then_inc(s_res, 16)
        small = load_for_experts(sp, a, kept, s_moe)
        sp.wait_ge(s_gn, KD)
        emb = load_embeddings(sp, a, BIG, s_emb)
        sp.wait_ge(s_moe, small)
        sp.wait_ge(s_emb, emb)
        sp.wait_ge(s_out, counts["out"])
        sp.wait_ge(s_wout, 32)

    @block.gpsimd
    def _(pool):
        done = [0]

        def link(ins):
            done[0] += 1
            ins.then_inc(s_p, 1)
            pool.wait_ge(s_p, done[0])

        pool.memset(zx[:, :, 0:1], 0.0).then_inc(s_zero, 1)
        pool.memset(ux[:, 0:15], 0.0).then_inc(s_zero, 1)
        pool.wait_ge(s_zero, 2)
        pool.memset(w2z[64:128, :], 0.0).then_inc(s_zero, 1)
        pool.wait_ge(s_zero, 3)
        pool.memset(a2z[0:64, :], 0.0).then_inc(s_zero, 1)
        pool.wait_ge(s_zero, 4)
        pool.wait_ge(s_const, 16)
        pool.wait_ge(s_plT, 1)
        inv = c_("inv").rearrange("p (g t) -> p g t", g=J)
        for g in range(J):
            w = 2 << g
            pool.wait_ge(s_act_took, taken(index["u", g]))
            if g:
                link(pool.tensor_copy(uxs[:, :, 0:15], plT[:, g, :].rearrange("p (b s) -> p b s", b=NB)))
            else:
                link(pool.tensor_copy(uxs[:, :, 0:15], plT[:, g, :].rearrange("p (b s) -> p b s", b=NB)))
            us = ux[:, 15 + NPR:15 + T]
            link(pool.tensor_copy(uxs[:, :, 15:19], us.rearrange("p (b t) -> p b t", b=NB)))
            pool.tensor_copy(ul[:, g, 0:15], ux[:, NPR:NPR + 15])
            pool.tensor_copy(ul[:, g, 15:47], us).then_inc(s_ul, 1)
            curp, curs = ux[:, 0:15 + NPR], uxs[:, :, :]
            step, k = 1, 0
            while step < w:
                nxt = pt[:, k, 0:15 + NPR]
                nxs = pt[:, k, 15 + NPR:].rearrange("p (b x) -> p b x", b=NB)
                lo = 2 * step - 1
                pool.tensor_tensor(nxt[:, lo:], curp[:, lo:], curp[:, lo - step:15 + NPR - step], ALU.add)
                link(pool.tensor_tensor(nxs[:, :, lo:], curs[:, :, lo:], curs[:, :, lo - step:19 - step], ALU.add))
                curp, curs = nxt, nxs
                step, k = 2 * step, 1 - k
            pool.tensor_scalar(pooled[:, g, 16:NPR], curp[:, 31:15 + NPR], 1.0 / w, None, ALU.mult)
            pool.tensor_tensor(pooled[:, g, 0:16], curp[:, 15:31], inv[:, g, :], ALU.mult)
            link(pool.tensor_scalar(pooled[:, g, NPR:T].rearrange("p (b t) -> p b t", b=NB), curs[:, :, 15:19],
                                    1.0 / w, None, ALU.mult))
            pool.tensor_tensor(pooled[:, g, :], pooled[:, g, :], ux[:, 15:15 + T], ALU.subtract).then_inc(s_pooled, 1)
            pool.wait_ge(s_pooled, g + 1)

        def split_heads(c):
            for q in range(2):
                part = slice(64 * q, 64 * q + 64)
                ins = pool.tensor_copy(ARZ[c % 2][part, :, q, :, :].rearrange("p j x t -> p j (x t)"), AR[part, :, c * 128:(c + 1) * 128])
                if q == 0:
                    link(ins)
            ins.then_inc(s_arz, 1)
            pool.wait_ge(s_arz, c + 1)

        pool.wait_ge(s_rkk, J)
        pool.memset(az[0], 0.0)
        pool.memset(XTi, 0.0)
        link(pool.memset(az[1], 0.0))
        for c in range(C):
            if c >= 2:
                pool.wait_ge(s_g1, c - 1)
            link(pool.tensor_copy(az[c % 2][0:64, :, 0, :], ARp[0:64, :, c, 0, :]))
            pool.tensor_copy(az[c % 2][64:128, :, 1, :], ARp[64:128, :, c, 0, :]).then_inc(s_az, 1)
            pool.wait_ge(s_az, c + 1)
        pool.memset(XTi.rearrange("p s t -> p (s t)")[:, 0:1024:33], 1.0).then_inc(s_az0, 1)
        pool.wait_ge(s_md, C)
        pool.dma_start(mmd[0:64].rearrange("q s t -> s q t"), MDs[0:32]).then_inc(s_mdst, 16)
        pool.dma_start(mmd[64:128].rearrange("q s t -> s q t"), MDs[32:64]).then_inc(s_mdst, 16)
        pool.wait_ge(s_mdst, 32)
        pool.dma_start(MT, mmd).then_inc(s_mt, 16)
        pool.wait_ge(s_g1, C)
        pool.memset(ARZ[0], 0.0)
        link(pool.memset(ARZ[1], 0.0))
        pool.wait_ge(s_inv, 1)
        pool.dma_start(xtd, XTi).then_inc(s_xst, 16)
        pool.dma_start(xnd[0:64], XNi[0:64]).then_inc(s_xst, 16)
        for c in range(2):
            split_heads(c)
        pool.wait_ge(s_xst, 32)
        pool.dma_start(XT[0:32, :, 0:32], xtd[0:64].rearrange("q j t -> j q t")).then_inc(s_xld, 16)
        pool.dma_start(XT[32:64, :, 32:64], xtd[64:128].rearrange("q j t -> j q t")).then_inc(s_xld, 16)
        pool.dma_start(XA, xnd[0:64].rearrange("q s j -> s q j")).then_inc(s_xld, 16)
        pool.memset(XT[32:64, :, 0:32], 0.0).then_inc(s_az0, 1)
        pool.wait_ge(s_az0, 2)
        pool.wait_ge(s_p2, 4)
        pool.memset(S0z, 0.0).then_inc(s_s0, 1)
        for c in range(2, C):
            pool.wait_ge(s_gg, 2 * (c - 1))
            split_heads(c)
        pool.wait_ge(s_sa, C)
        pool.dma_start(SL.rearrange("v (b h k) -> v b h k", b=NB, h=H), a["state_wkv"][0].rearrange("b h v k -> v b h k")).then_inc(s_sl, 16)
        pool.wait_ge(s_o, C)
        pool.memset(BIG[:, 0:NB * J * 128], 0.0).then_inc(s_sz, 1)
        link(pool.memset(arB, 0.0))
        for x in range(2):
            for j in range(J):
                last = pool.tensor_copy(arB[:, j, :].rearrange("p (b y) -> p b y", b=NB)[:, :, x * 32:x * 32 + 4],
                                        ARs[:, j, x, :].rearrange("p (b t) -> p b t", b=NB))
        last.then_inc(s_arb, 1)
        pool.wait_ge(s_s0, C + 1)
        link(pool.memset(arzS, 0.0))
        link(pool.tensor_copy(arzS[0:64, :, 0, :], AR[0:64, :, C * 128:CW]))
        pool.tensor_copy(arzS[64:128, :, 1, :], AR[64:128, :, C * 128:CW]).then_inc(s_arb, 1)
        pool.wait_ge(s_arb, 2)
        pool.wait_ge(s_vtsc, 1)
        pool.wait_ge(s_sasc, 1)
        for h in range(H):
            if h >= 2:
                pool.wait_ge(s_sts, h - 1)
            pool.tensor_tensor(SAVm[h % 2], SAVs[:, h * 64:h * 64 + 64].unsqueeze(1).to_broadcast([64, NB, 64]),
                               c_("bmask")[0:64].unsqueeze(2).to_broadcast([64, NB, 64]), ALU.mult).then_inc(s_sm, 1)
        pool.wait_ge(s_wTc, 1)
        pool.dma_start(o["wkv_prompt"][0, 0].rearrange("h v k -> v h k"), SoT.rearrange("v (h k) -> v h k", h=H)).then_inc(s_wout, 16)
        pool.wait_ge(s_wTc, WT_N)
        pool.dma_start(o["wkv_sample"][0].rearrange("b h v k -> v b h k"), WOUT.rearrange("v b (h k) -> v b h k", h=H)).then_inc(s_wout, 16)

    @block.scalar
    def _(act):
        act.wait_ge(s_v, 1)
        for n in range(NTILE):
            act.wait_ge(s_x[n], 16)
            nc.scalar.activation(ARBK[0:ROWS[n], n * D:(n + 1) * D], xt[0:ROWS[n], n, :], ACT.Square,
                                 accum_out=ss[0:ROWS[n], n:n + 1]).then_inc(s_sq, 1)
        act.wait_ge(s_ms, 1)
        nc.scalar.activation(ss[:, :], ss[:, :], ACT.Sqrt).then_inc(s_rt, 1)
        act.wait_ge(s_zero, 4)
        act.wait_ge(s_vec, 1)

        def square_k(j):
            act.wait_ge(s_zm, zpos[4 + j] + 1)
            nc.scalar.activation(NR[:, j, :], K[:, j, :], ACT.Square, scale=vec[:, KKW + j:KKW + j + 1]).then_inc(s_nsq, 1)

        for n, (kind, i, eng) in enumerate(plan):
            if eng != "a":
                continue
            if n == N1:
                break
            if kind == "z":
                if zpos[i] >= 2:
                    act.wait_ge(s_zm, zpos[i] - 1)
                act.wait_ge(s_big, n + 1)
                nc.scalar.activation(half(zx[:, zpos[i] % 2, 1:1 + T]), big(n), ACT.Copy).then_inc(s_act_took, 1)
                if zpos[i] == 1:
                    act.wait_ge(s_zm, 1)
                    nc.scalar.activation(twa[0:64, :], twa[0:64, :], ACT.Tanh).then_inc(s_twa, 1)
                    act.wait_ge(s_zm, 2)
                    nc.scalar.activation(sgd[:, :], sgd[:, :], ACT.Sigmoid).then_inc(s_sgd, 1)
            if kind in ("lw", "la"):
                if (kind, i) == ("lw", 0):
                    for j in range(J):
                        square_k(j)
                act.wait_ge(s_big, n + 1)
                dst, b = (SG, W0) if kind == "lw" else (A, A0)
                nc.scalar.activation(half(dst[:, i, :]), big(n), ACT.Sigmoid, bias=vec[:, b + i:b + i + 1]).then_inc(s_act_took, 1)
            if kind == "nrm":
                act.wait_ge(s_big, n + 1)
                nc.scalar.activation(half(NR[:, i, :]), big(n), ACT.Sqrt).then_inc(s_act_took, 1)
            if kind == "u":
                if i:
                    act.wait_ge(s_pooled, i)
                act.wait_ge(s_big, n + 1)
                nc.scalar.activation(half(ux[:, 15:15 + T]), big(n), ACT.Copy).then_inc(s_act_took, 1)
            if kind == "ga":
                if i >= 2:
                    act.wait_ge(s_dve_took, taken(index["ba", i - 2]))
                act.wait_ge(s_big, n + 1)
                nc.scalar.activation(half(sga[:, i % 2, :]), big(n), ACT.Sigmoid).then_inc(s_act_took, 1)
                if i == 1:
                    act.wait_ge(s_cs, 1)
                    flat = lambda x: x.rearrange("p j t -> p (j t)")
                    nc.scalar.activation(flat(SG), flat(SG), ACT.Exp, scale=-DECAY).then_inc(s_ex, 1)
                    nc.scalar.activation(flat(NR), flat(CS), ACT.Exp, scale=DECAY).then_inc(s_ex, 1)
                    act.wait_ge(s_ex, 2)
                    nc.scalar.activation(flat(CS), flat(CS), ACT.Exp, scale=-DECAY).then_inc(s_ex, 1)

        for r in range(4):
            act.wait_ge(s_p2, r + 1)
            if r == 0:
                act.wait_ge(s_mdst, 32)
            nc.scalar.activation(P2T[32:64, 16 * r:16 * r + 16, :].rearrange("p n t -> p (n t)"), bank[4 + r % 2][32:64, :], ACT.Copy).then_inc(s_p2c, 1)
        for r in range(4):
            act.wait_ge(s_xo, r + 1)
            nc.scalar.activation(XT[0:32, 16 * r:16 * r + 16, 32:64], bank[6 + r % 2][0:32, :].rearrange("p (n t) -> p n t", n=16), ACT.Copy).then_inc(s_xoc, 1)
        act.wait_ge(s_p2, 4)

        def take_turned(c):
            act.wait_ge(s_bt, c + 1)
            if c >= 2:
                act.wait_ge(s_st, c - 1)
            nc.scalar.activation(BKt[c % 2], bank[6], ACT.Copy).then_inc(s_btc, 1)
            act.wait_ge(s_vt, c + 1)
            if c >= 2:
                act.wait_ge(s_o, c - 1)
            nc.scalar.activation(SAV[c % 2][0:64], bank[7][0:64, :], ACT.Copy).then_inc(s_vtc, 1)

        take_turned(0)
        for c in range(C):
            if c + 1 < C:
                take_turned(c + 1)
            act.wait_ge(s_sa, c + 1)
            nc.scalar.activation(SAV[c % 2][64:128], bank[1][64:128, :], ACT.Copy).then_inc(s_sac, 1)
            act.wait_ge(s_o, c + 1)
            nc.scalar.activation(OT[:, :, c * L:(c + 1) * L], bank[3][:, 0:256].rearrange("p (j t) -> p j t", j=J), ACT.Copy).then_inc(s_oc, 1)
        act.wait_ge(s_wT, 1)
        nc.scalar.activation(SoT, bank[6][0:64, :], ACT.Copy).then_inc(s_wTc, 1)
        act.wait_ge(s_vts, 1)
        nc.scalar.activation(SAVs[0:32], bank[3][0:32, :], ACT.Copy).then_inc(s_vtsc, 1)
        act.wait_ge(s_bts, 1)
        nc.scalar.activation(BKtS, bank[2][0:64, :], ACT.Copy).then_inc(s_btsc, 1)

        def take_gate(n):
            act.wait_ge(s_big, n + 1)
            nc.scalar.activation(half(SB[:, plan[n][1], :]), big(n), ACT.Sigmoid).then_inc(s_act_took, 1)

        take_gate(N1)
        act.wait_ge(s_rs, 1)
        nc.scalar.activation(RHSs, bank[0][0:32, :], ACT.Copy).then_inc(s_rsc, 1)
        act.wait_ge(s_sas, 1)
        nc.scalar.activation(SAVs[32:64], bank[1][32:64, :], ACT.Copy).then_inc(s_sasc, 1)
        act.wait_ge(s_os, 1)
        nc.scalar.activation(OsS[32:64], bank[0][32:64, :], ACT.Copy).then_inc(s_osc, 1)
        take_gate(N1 + 1)
        act.wait_ge(s_osT, 1)
        nc.scalar.activation(OT[:, :, NPR:T], bank[4][:, 0:128].rearrange("p (j t) -> p j t", j=J), ACT.Copy).then_inc(s_oc, 1)
        take_gate(N1 + 2)
        act.wait_ge(s_sn, 2 * J)
        for b in range(NB):
            act.wait_ge(s_wT, 2 + b)
            nc.scalar.activation(WOUT[:, b, :], bank[4 + b % 2][0:64, :], ACT.Copy).then_inc(s_wTc, 1)
        for n in range(N1 + 3, len(plan)):
            kind, i, eng = plan[n]
            if eng != "a":
                continue
            if kind == "gb":
                take_gate(n)
            if kind == "var":
                if i == 0:
                    for j in range(J):
                        act.wait_ge(s_dve_took, taken(index["mean", j]))
                        nc.scalar.activation(SQ[j], OT[:, j, :], ACT.Square).then_inc(s_sqo, 1)
                act.wait_ge(s_big, n + 1)
                nc.scalar.activation(half(SQ[i]), big(n), ACT.Sqrt, bias=c_("eps")).then_inc(s_act_took, 1)

        act.wait_ge(s_wout, 32)
        for n in range(NTILE):
            r = ROWS[n]
            act.wait_ge(s_new, 2 * n + 2)
            nc.scalar.activation(HN[0:r, n, :], x0[0:r, n, :], ACT.Square, accum_out=ss[0:r, n:n + 1]).then_inc(s_sqx, 1)
            act.wait_ge(s_msx, n + 1)
            nc.scalar.activation(ss[0:r, n:n + 1], ss[0:r, n:n + 1], ACT.Sqrt).then_inc(s_rtx, 1)

    @block.vector
    def _(dve):
        v = nc.vector
        done = [0]

        def link(ins):
            done[0] += 1
            ins.then_inc(s_v, 1)
            dve.wait_ge(s_v, done[0])

        link(v.memset(ss[:, :], 1.0))
        dve.wait_ge(s_sq, NTILE)
        v.tensor_scalar(ss[:, :], ss[:, :], 1.0 / D, RMS_EPS, ALU.mult, ALU.add).then_inc(s_ms, 1)
        dve.wait_ge(s_rt, 1)
        link(v.reciprocal(ss[:, :], ss[:, :]))
        for n in range(NTILE):
            v.tensor_scalar(xt[0:ROWS[n], n, :], xt[0:ROWS[n], n, :], ss[0:ROWS[n], n:n + 1], None, ALU.mult).then_inc(s_xn, 1)
        dve.wait_ge(s_vecT, 1)
        v.tensor_copy(vec[:, :], bank[4][:, 0:46]).then_inc(s_vec, 1)
        dve.wait_ge(s_vec, 1)
        link(v.tensor_scalar(omka[:, :], vec[:, KAW:KAW + J], -1.0, 1.0, ALU.mult, ALU.add))
        dve.wait_ge(s_gmix, 16)
        for g in range(2 * NTILE):
            n, q = g // 2, g % 2
            dve.wait_ge(s_xT, g + 1)
            r = ROWS[n]
            v.tensor_tensor(hT[:, 4 * q:4 * q + 4, n * P:n * P + r],
                            bank[5 + g % 2].rearrange("p (k t) -> p k t", k=4)[:, :, 0:r],
                            gmix[:, 4 * q:4 * q + 4].unsqueeze(2).to_broadcast([P, 4, r]), ALU.mult).then_inc(s_hT, 1)
        dve.wait_ge(s_stTp, 1)
        v.tensor_copy(stT[:, :, :].rearrange("p z b -> p (z b)"), bank[7][:, 0:ZB * NB]).then_inc(s_stT, 1)
        dve.wait_ge(s_stT, 1)
        dve.wait_ge(s_const, 16)
        dve.wait_ge(s_zero, 4)

        def lerp(i):
            k = zpos[i]
            n = index["z", i]
            z = zx[:, k % 2, :]
            dst = {0: R, 1: K, 2: V}[i // 4][:, i % 4, :] if i < 12 else (twa[:, :] if i == 12 else sgd[:, :])
            dve.wait_ge(s_act_took, taken(n))
            v.tensor_copy(sh[:, :, i:i + 1], z[:, NPR:NPR + 33:4].unsqueeze(2)).then_inc(s_sh, 1)
            link(v.tensor_tensor(dz[:, :], z[:, 0:T], z[:, 1:1 + T], ALU.subtract))
            link(v.tensor_tensor(dz[:, NPR:T:TS], stT[:, i, :], z[:, NPR + 1:1 + T:TS], ALU.subtract))
            v.scalar_tensor_tensor(dst, dz[:, :], vec[:, MU + i:MU + i + 1], z[:, 1:1 + T], ALU.mult, ALU.add).then_inc(s_zm, 1)
            dve.wait_ge(s_zm, k + 1)

        flat = lambda x: x.rearrange("p j t -> p (j t)")
        for i in (12, 13, 4, 5, 6, 7):
            lerp(i)
        dve.wait_ge(s_plTp, 1)
        v.tensor_copy(plT[:, :, :].rearrange("p g r -> p (g r)"), bank[4][:, 0:480]).then_inc(s_plT, 1)
        for i in (0, 1, 2, 3):
            lerp(i)
        dve.wait_ge(s_act_took, taken(index["la", 3]))
        for j in range(J):
            last = v.tensor_tensor_scan(CS[:, j, :], c_("seg"), SG[:, j, :], 0.0, ALU.mult, ALU.add)
        link(last)
        v.tensor_tensor(flat(SG), flat(CS), flat(SG), ALU.subtract)
        for j in range(J):
            last = v.tensor_scalar(KQ[:, j, :], K[:, j, :], vec[:, KKW + j:KKW + j + 1], None, ALU.mult)
        dve.wait_ge(s_act_took, taken(index["nrm", 3]))
        link(v.tensor_scalar(flat(NR), flat(NR), 1e-12, None, ALU.max))
        link(v.reciprocal(flat(NR), flat(NR)))
        v.scalar_tensor_tensor(flat(KQ), flat(KQ), -1.0, flat(NR), ALU.mult, ALU.mult).then_inc(s_cs, 1)
        dve.wait_ge(s_cs, 1)
        for i in (8, 9, 10, 11):
            lerp(i)

        def take_mix(g):
            n = index["mix", g]
            dve.wait_ge(s_big, n + 1)
            v.tensor_scalar(half(pooled[:, g, :]), big(n), vec[:, PSC + g:PSC + g + 1], None, ALU.mult).then_inc(s_dve_took, 1)

        def take_ba(m):
            n = index["ba", m]
            dve.wait_ge(s_act_took, taken(index["ga", m]))
            dve.wait_ge(s_big, n + 1)
            v.tensor_tensor(half(merged[:, m, :]), big(n), half(sga[:, m % 2, :]), ALU.mult).then_inc(s_dve_took, 1)

        for g in range(J):
            take_mix(g)
        dve.wait_ge(s_ul, 4)
        dve.wait_ge(s_shTp, 1)
        v.tensor_copy(shT[:, :], bank[7][0:9 * ZB, 0:P]).then_inc(s_shT, 1)
        dve.wait_ge(s_ulTp, 1)
        v.tensor_copy(ulT[:, :], bank[4][0:47, :]).then_inc(s_ulT, 1)
        take_ba(0)
        take_ba(1)
        dve.wait_ge(s_ex, 1)
        v.tensor_tensor(ARp[:, :, :, 0, :], prompt(KQ), prompt(SG), ALU.mult)
        link(v.tensor_tensor(ARs[:, :, 0, :], KQ[:, :, NPR:T], SG[:, :, NPR:T], ALU.mult))
        link(v.scalar_tensor_tensor(flat(KQ), flat(KQ), -1.0, flat(A), ALU.mult, ALU.mult))
        take_ba(2)
        dve.wait_ge(s_ex, 2)
        v.tensor_tensor(BKp[:, :, :, 1, :], prompt(KQ), prompt(NR), ALU.mult)
        v.tensor_tensor(BKs[:, :, 1, :], KQ[:, :, NPR:T], NR[:, :, NPR:T], ALU.mult)
        for j in range(J):
            last = v.tensor_scalar(A[:, j, :], A[:, j, :], vec[:, KAW + j:KAW + j + 1], omka[:, j:j + 1], ALU.mult, ALU.add)
        link(last)
        link(v.tensor_tensor(flat(K), flat(K), flat(A), ALU.mult))
        v.tensor_tensor(BKp[:, :, :, 0, :], prompt(K), prompt(NR), ALU.mult)
        v.tensor_tensor(BKs[:, :, 0, :], K[:, :, NPR:T], NR[:, :, NPR:T], ALU.mult)
        dve.wait_ge(s_ex, 3)
        v.tensor_copy(GL[:, :, 0:C], CS[:, :, L - 1:NPR:L])
        v.tensor_copy(GL[:, :, C:C + NB], CS[:, :, NPR + 3:T:TS])
        v.tensor_tensor(ARp[:, :, :, 1, :], prompt(R), prompt(CS), ALU.mult)
        v.tensor_tensor(ARs[:, :, 1, :], R[:, :, NPR:T], CS[:, :, NPR:T], ALU.mult)
        for j in range(J):
            v.scalar_tensor_tensor(KQ[:, j, :], R[:, j, :], vec[:, RKW + j:RKW + j + 1], K[:, j, :], ALU.mult, ALU.mult).then_inc(s_rkk, 1)
        for j in range(J):
            n = index["bon", j]
            dve.wait_ge(s_big, n + 1)
            v.tensor_tensor(half(A[:, j, :]), big(n), half(V[:, j, :]), ALU.mult).then_inc(s_dve_took, 1)

        up = c_("up32")
        for c in range(C):
            dve.wait_ge(s_g1, c + 1)
            g = bank[4 + c % 2].rearrange("p (h t) -> p h t", h=H)
            v.tensor_tensor(MDs[0:32, c * H:(c + 1) * H, :], g[0:32, :, 0:32], up[0:32].unsqueeze(1).to_broadcast([32, H, 32]), ALU.mult)
            v.tensor_tensor(MDs[32:64, c * H:(c + 1) * H, :], g[32:64, :, 32:64], up[32:64].unsqueeze(1).to_broadcast([32, H, 32]), ALU.mult)
            v.tensor_copy(MOs[0:32, c * H:(c + 1) * H, :], g[0:32, :, 32:64]).then_inc(s_md, 1)
        dve.wait_ge(s_az0, 1)
        dve.wait_ge(s_mt, 16)
        BETWEEN = (8, 18, 25, 29)
        for t in range(1, 32):
            tm = tmpi[:, 0:t * t].rearrange("p (j s) -> p j s", j=t)
            link(v.tensor_tensor(tm, XTi[:, 0:t, 0:t], MT[:, 0:t, t].unsqueeze(1).to_broadcast([P, t, t]), ALU.mult))
            link(v.tensor_reduce(XTi[:, 0:t, t:t + 1], tm, AX.X, ALU.add))
            if t in BETWEEN:
                take_ba(LATE + BETWEEN.index(t))
        v.tensor_copy(XNi[0:64], XTi[0:64].rearrange("p j t -> p t j")).then_inc(s_inv, 1)
        take_ba(KD - 1)

        gm = c_("gmask").unsqueeze(1).to_broadcast([P, 4, 128])

        def take_gram(c):
            for r in range(2):
                dve.wait_ge(s_gg, 2 * c + r + 1)
                if c == 0 and r == 0:
                    dve.wait_ge(s_xo, 4)
                if c >= 2:
                    dve.wait_ge(s_o, c - 1)
                v.tensor_tensor(Gs[c % 2][:, 4 * r:4 * r + 4, :], bank[4 + r].rearrange("p (h x) -> p h x", h=4), gm, ALU.mult).then_inc(s_gc, 1)

        take_gram(0)
        for c in range(C):
            dve.wait_ge(s_rhs, c + 1)
            v.tensor_copy(RHS, bank[0][0:64, :]).then_inc(s_rhsc, 1)
            if c + 1 < C:
                take_gram(c + 1)
            dve.wait_ge(s_st, c + 1)
            st = bank[2][:, 0:256].rearrange("p (j v) -> p j v", j=J)
            v.tensor_tensor(Stmp[0:64], st[0:64], S0z[0:64, :, 0, :], ALU.add)
            link(v.tensor_tensor(Stmp[64:128], st[64:128], S0z[64:128, :, 1, :], ALU.add))
            gl = GL[:, :, c].unsqueeze(2).to_broadcast([P, J, 64])
            if c + 1 < C:
                v.tensor_tensor(S0z[0:64, :, 0, :], Stmp[0:64], gl[0:64], ALU.mult)
                v.tensor_tensor(S0z[64:128, :, 1, :], Stmp[64:128], gl[64:128], ALU.mult).then_inc(s_s0, 1)
            else:
                v.tensor_tensor(SF, Stmp, gl, ALU.mult).then_inc(s_s0, 1)
        dve.wait_ge(s_sz, 1)
        for r in range(4):
            dve.wait_ge(s_slT, r + 1)
            s = bank[4 + r % 2].rearrange("p (b j v) -> p b j v", b=2, j=J)
            for q in range(2):
                for b in range(2):
                    last = v.tensor_copy(S0S[64 * q:64 * q + 64, 2 * r + b, :, q, :], s[64 * q:64 * q + 64, b])
            last.then_inc(s_s0s, 1)
        dve.wait_ge(s_gs, 1)
        v.tensor_tensor(GsS, bank[6][0:64, :].rearrange("p (h x) -> p h x", h=H), c_("gmask_s")[0:64].unsqueeze(1).to_broadcast([64, H, 64]), ALU.mult).then_inc(s_gsc, 1)
        dve.wait_ge(s_ms_, 1)
        wide = lambda x: x.rearrange("p (h t) -> p h t", h=H)
        v.tensor_tensor(wide(MTs), wide(bank[7][0:32, 0:256]), c_("mt_s")[0:32].unsqueeze(1).to_broadcast([32, H, 32]), ALU.mult)
        link(v.tensor_tensor(wide(Ms), wide(bank[7][0:32, 256:512]), c_("m_s")[0:32].unsqueeze(1).to_broadcast([32, H, 32]), ALU.mult))
        dve.wait_ge(s_wTc, 1)
        link(v.tensor_tensor(wide(Xs), wide(MTs), ident[0:32, 0:32].unsqueeze(1).to_broadcast([32, H, 32]), ALU.add))
        dve.wait_ge(s_v, done[0])
        v.tensor_copy(GL[:, 0:1, 0:1], GL[:, 0:1, 0:1]).then_inc(s_msc, 1)
        dve.wait_ge(s_m2, 1)
        link(v.tensor_copy(M2s, bank[4][0:32, 0:256]))
        v.tensor_tensor(Xs, Xs, M2s, ALU.add).then_inc(s_m2c, 1)
        dve.wait_ge(s_m2c, 1)
        dve.wait_ge(s_m3, 1)
        v.tensor_tensor(Xs, Xs, bank[5][0:32, 0:256], ALU.add).then_inc(s_xs, 1)
        for h in range(H):
            j, q = h // 2, h % 2
            dve.wait_ge(s_sts, h + 1)
            sn = Sn[64 * q:64 * q + 64, j]
            link(v.tensor_tensor(sn, bank[6 + j % 2][64 * q:64 * q + 64, :].rearrange("p (b v) -> p b v", b=NB), S0S[64 * q:64 * q + 64, :, j, q, :], ALU.add))
            v.tensor_tensor(sn, sn, GL[64 * q:64 * q + 64, j, C:C + NB].unsqueeze(2).to_broadcast([64, NB, 64]), ALU.mult).then_inc(s_sn, 1)
        for j in range(J):
            last = v.tensor_scalar(A[:, j, :], A[:, j, :], vec[:, LNB + j:LNB + j + 1], None, ALU.add)
        link(last)
        for j in range(J):
            n = index["mean", j]
            dve.wait_ge(s_big, n + 1)
            v.tensor_tensor(half(OT[:, j, :]), half(OT[:, j, :]), big(n), ALU.subtract).then_inc(s_dve_took, 1)
        for j in range(J):
            dve.wait_ge(s_act_took, taken(index["var", j]))
            link(v.reciprocal(SQ[j], SQ[j]))
            link(v.tensor_tensor(OT[:, j, :], OT[:, j, :], SQ[j], ALU.mult))
            link(v.scalar_tensor_tensor(OT[:, j, :], OT[:, j, :], vec[:, LNW + j:LNW + j + 1], A[:, j, :], ALU.mult, ALU.add))
            n = index["g2", j]
            dve.wait_ge(s_big, n + 1)
            v.tensor_tensor(half(OT[:, j, :]), half(OT[:, j, :]), big(n), ALU.mult).then_inc(s_yb, 1)
            dve.wait_ge(s_yb, j + 1)
            v.tensor_copy(GL[:, 0:1, 0:1], GL[:, 0:1, 0:1]).then_inc(s_dve_took, 1)
        for m in range(KD):
            n = index["bb", m]
            dve.wait_ge(s_act_took, taken(index["gb", m]))
            dve.wait_ge(s_big, n + 1)
            v.tensor_tensor(half(SB[:, m, :]), half(SB[:, m, :]), big(n), ALU.mult).then_inc(s_dve_took, 1)
            dve.wait_ge(s_dve_took, taken(n))
            v.tensor_tensor(merged[:, m, :], merged[:, m, :], SB[:, m, :], ALU.add).then_inc(s_gn, 1)

        def norm_tile(n):
            r = ROWS[n]
            dve.wait_ge(s_sqx, n + 1)
            v.tensor_scalar(ss[0:r, n:n + 1], ss[0:r, n:n + 1], 1.0 / D, RMS_EPS, ALU.mult, ALU.add).then_inc(s_msx, 1)
            dve.wait_ge(s_rtx, n + 1)
            link(v.reciprocal(ss[0:r, n:n + 1], ss[0:r, n:n + 1]))
            v.tensor_scalar(HN[0:r, n, :], x0[0:r, n, :], ss[0:r, n:n + 1], None, ALU.mult)

        dve.wait_ge(s_res, 16 * NTILE)
        for g in range(2 * NTILE):
            n, q = g // 2, g % 2
            dve.wait_ge(s_xo2, g + 1)
            x = x0[0:ROWS[n], n, 512 * q:512 * q + 512]
            v.tensor_tensor(x, x, bank[4 + g % 4][0:ROWS[n], :], ALU.add).then_inc(s_new, 1)
            if q and n:
                norm_tile(n - 1)
        norm_tile(NTILE - 1)

    @block.tensor
    def _(pe):
        pe.wait_ge(s_const, 16)
        pe.wait_ge(s_rows, 16 * 9)
        pe.transpose(bank[4][:, 0:46], rows[:, :], ident[0:46, 0:46]).then_inc(s_vecT, 1)
        for g in range(2 * NTILE):
            n, q = g // 2, g % 2
            r = ROWS[n]
            pe.wait_ge(s_xn, n + 1)
            if g >= 2:
                pe.wait_ge(s_hT, g - 1)
            for k in range(4):
                last = pe.transpose(bank[5 + g % 2][:, k * P:k * P + r], xt[0:r, n, 4 * q + k:D:KD], ident[0:r, 0:r])
            last.then_inc(s_xT, 1)
        pe.wait_ge(s_shin, 16)
        for z in range(ZB):
            last = pe.transpose(bank[7][:, z * NB:(z + 1) * NB], sh_in[:, z * P:(z + 1) * P], ident[0:NB, 0:NB])
        last.then_inc(s_stTp, 1)
        pe.wait_ge(s_hT, 2 * NTILE)

        def group(n):
            kind, i, _ = plan[n]
            if n >= 2:
                took(pe, n - 2)
            u = unit_of(kind, i)
            if u is not None:
                pe.wait_ge(s_unit[u % NU], 16 * (u // NU + 1))
            if kind in ("z", "u", "ga", "gb"):
                wt = ring[:, u % NU, :].rearrange("p (k m) -> p k m", k=KD)
                ops = [(wt[:, k, :], hT[:, k, :]) for k in range(KD)]
            if kind in ("ba", "bb"):
                wt = ring[:, u % NU, :].rearrange("p (k m) -> p k m", k=4)
                rhs = pooled if kind == "ba" else OT
                if (kind, i) == ("ba", 0):
                    pe.wait_ge(s_dve_took, taken(index["mix", 3]))
                if (kind, i) == ("bb", 0):
                    pe.wait_ge(s_yb, J)
                ops = [(wt[:, k, (i % 2) * P:(i % 2) * P + P], rhs[:, k, :]) for k in range(J)]
            if kind in ("lw", "la"):
                pe.wait_ge(s_twa, 1)
                pe.wait_ge(s_zero, 4)
                pe.wait_ge(s_lora, 48)
                ops = [((w2z if kind == "lw" else a2z)[:, i * P:(i + 1) * P], twa[:, :])]
            if kind == "nrm":
                pe.wait_ge(s_nsq, i + 1)
                ops = [(pair, NR[:, i, :])]
            if kind == "mix":
                pe.wait_ge(s_mixw, 16)
                pe.wait_ge(s_pooled, i + 1)
                ops = [(mixw[:, i, :], pooled[:, i, :])]
            if kind == "bon":
                pe.wait_ge(s_rkk, i + 1)
                ops = [(pair, KQ[:, i, :])]
            if kind == "mean":
                pe.wait_ge(s_oc, C + 1)
                ops = [(pairmean, OT[:, i, :])]
            if kind == "var":
                pe.wait_ge(s_sqo, i + 1)
                ops = [(pairmean, SQ[i])]
            if kind == "g2":
                ops = [(g2w[:, i * P:(i + 1) * P], sgd[:, :])]
            for h in range(2):
                for k, (w, x) in enumerate(ops):
                    last = pe.matmul(PB[n % 2][:, h, 0:HT], w, x[:, h * HT:(h + 1) * HT], start=(k == 0), stop=(k == len(ops) - 1))
            last.then_inc(s_big, 1)

        for n in range(N0):
            if plan[n][:2] == ("lw", 0):
                pe.wait_ge(s_plin, 16)
                pe.wait_ge(s_vec, 1)
                for g in range(J):
                    last = pe.transpose(bank[4][:, g * 120:(g + 1) * 120], pl_in[:, g * P:(g + 1) * P], ident[0:120, 0:120])
                last.then_inc(s_plTp, 1)
            group(n)
            if plan[n][:2] == ("mix", 3):
                pe.wait_ge(s_sh, ZB)
                pe.wait_ge(s_stT, 1)
                pe.transpose(bank[7][0:9 * ZB, 0:P], sh[:, :, :].rearrange("p i z -> p (i z)"), ident).then_inc(s_shTp, 1)
                pe.wait_ge(s_ul, J)
                pe.wait_ge(s_plT, 1)
                for g in range(J):
                    last = pe.transpose(bank[4][0:47, g * P:(g + 1) * P], ul[:, g, :], ident)
                last.then_inc(s_ulTp, 1)

        took(pe, N0 - 1)
        took(pe, N0 - 2)
        pe.wait_ge(s_ulT, 1)
        for c in range(C):
            pe.wait_ge(s_az, c + 1)
            if c >= 2:
                pe.wait_ge(s_md, c - 1)
            for j in range(J):
                last = pe.matmul(bank[4 + c % 2][0:64, j * 128:(j + 1) * 128], BKp[:, j, c, 1, :], az[c % 2][:, j].rearrange("p q t -> p (q t)"), start=True, stop=True)
            last.then_inc(s_g1, 1)
        for n in range(N0, N1):
            group(n)
        pe.wait_ge(s_xld, 48)
        pe.wait_ge(s_az0, 2)
        pe.wait_ge(s_md, C)
        for r in range(4):
            if r >= 2:
                pe.wait_ge(s_p2c, r - 1)
            for n in range(16):
                i = 16 * r + n
                last = pe.matmul(bank[4 + r % 2][32:64, n * 32:n * 32 + 32], MOs[0:32, i, :], XA[0:32, i, :], start=True, stop=True)
            last.then_inc(s_p2, 1)
        for r in range(4):
            pe.wait_ge(s_p2c, r + 1)
            if r >= 2:
                pe.wait_ge(s_xoc, r - 1)
            for n in range(16):
                i = 16 * r + n
                last = pe.matmul(bank[6 + r % 2][0:32, n * 32:n * 32 + 32], P2T[32:64, i, :], XT[32:64, i, 32:64], start=True, stop=True)
            last.then_inc(s_xo, 1)

        def prepare(c):
            pe.wait_ge(s_arz, c + 1)
            if c:
                pe.wait_ge(s_gc, 2 * c)
            else:
                pe.wait_ge(s_p2c, 4)
            for j in range(J):
                last = pe.matmul(bank[4 + j // 2][:, (j % 2) * 256:(j % 2) * 256 + 256], BK[:, j, c * 128:(c + 1) * 128],
                                 ARZ[c % 2][:, j].rearrange("p q x t -> p (q x t)"), start=True, stop=True)
                if j % 2:
                    last.then_inc(s_gg, 1)
            if c:
                pe.wait_ge(s_btc, c)
            else:
                pe.wait_ge(s_xoc, 4)
            for j in range(J):
                last = pe.transpose(bank[6][:, j * 128:(j + 1) * 128], BK[:, j, c * 128:(c + 1) * 128], ident)
            last.then_inc(s_bt, 1)
            if c:
                pe.wait_ge(s_vtc, c)
            for j in range(J):
                last = pe.transpose(bank[7][0:64, j * 128:(j + 1) * 128], V[:, j, c * L:(c + 1) * L], ident)
            last.then_inc(s_vt, 1)

        prepare(0)
        took(pe, N1 - 1)
        took(pe, N1 - 2)

        def from_values(c):
            k = c % 2
            pe.wait_ge(s_gc, 2 * c + 2)
            pe.wait_ge(s_vtc, c + 1)
            if c:
                pe.wait_ge(s_rhsc, c)
            for h in range(H):
                pe.matmul(bank[0][0:64, h * 64:h * 64 + 64], Gs[k][0:64, h, 0:64], SAV[k][0:64, h * 64:h * 64 + 64],
                          start=(h == 0), stop=False, skip_group_check=True)

        from_values(0)
        for c in range(C):
            k = c % 2
            pe.wait_ge(s_s0, c + 1)
            for j in range(J):
                last = pe.matmul(bank[0][0:64, j * 128:(j + 1) * 128], ARp[:, j, c, 0, :], S0z[:, j].rearrange("p q v -> p (q v)"),
                                 start=False, stop=True, skip_group_check=True)
            last.then_inc(s_rhs, 1)
            if c + 1 < C:
                prepare(c + 1)
            pe.wait_ge(s_rhsc, c + 1)
            if c:
                pe.wait_ge(s_sac, c)
            for h in range(H):
                last = pe.matmul(bank[1][64:128, h * 64:h * 64 + 64], XT[0:64, c * H + h, :], RHS[:, h * 64:h * 64 + 64], start=True, stop=True)
            last.then_inc(s_sa, 1)
            if c:
                pe.wait_ge(s_oc, c)
            for j in range(J):
                pe.matmul(bank[3][:, j * 64:j * 64 + 64], S0z[:, j].rearrange("p q v -> p (q v)"), ARp[:, j, c, 1, :],
                          start=(j == 0), stop=False, skip_group_check=True)
            pe.wait_ge(s_sac, c + 1)
            pe.wait_ge(s_btc, c + 1)
            for h in range(H):
                j, q = h // 2, h % 2
                last = pe.matmul(bank[2][64 * q:64 * q + 64, j * 64:j * 64 + 64], BKt[k][:, h * 64:h * 64 + 64], SAV[k][:, h * 64:h * 64 + 64], start=True, stop=True)
            last.then_inc(s_st, 1)
            for h in range(H):
                j, q = h // 2, h % 2
                last = pe.matmul(bank[3][64 * q:64 * q + 64, j * 64:j * 64 + 64], SAV[k][:, h * 64:h * 64 + 64], Gs[k][:, h, 64:128],
                                 start=False, stop=True, skip_group_check=True)
            last.then_inc(s_o, 1)
            if c + 1 < C:
                from_values(c + 1)
        pe.wait_ge(s_s0, C + 1)
        pe.wait_ge(s_btc, C)
        for j in range(J):
            last = pe.transpose(bank[6][0:64, j * 128:(j + 1) * 128], SF[:, j, :], ident)
        last.then_inc(s_wT, 1)

        pe.wait_ge(s_oc, C)
        for j in range(J):
            last = pe.transpose(bank[3][0:32, j * 128:(j + 1) * 128], V[:, j, NPR:T], ident)
        last.then_inc(s_vts, 1)
        for j in range(J):
            last = pe.transpose(bank[2][0:64, j * 128:(j + 1) * 128], BK[:, j, C * 128:CW], ident)
        last.then_inc(s_bts, 1)
        group(N1)
        pe.wait_ge(s_sl, 16)
        pe.wait_ge(s_gc, 2 * C)
        for r in range(4):
            if r >= 2:
                pe.wait_ge(s_s0s, r - 1)
            for n in range(8):
                x = (8 * r + n) * 128
                last = pe.transpose(bank[4 + r % 2][:, n * 64:n * 64 + 64], SL[:, x:x + 128], ident[0:64, 0:64])
            last.then_inc(s_slT, 1)
        pe.wait_ge(s_arb, 2)
        pe.wait_ge(s_wTc, 1)
        for j in range(J):
            last = pe.matmul(bank[6][0:64, j * 128:(j + 1) * 128], BK[:, j, C * 128:CW], arzS[:, j].rearrange("p q x -> p (q x)"), start=True, stop=True)
        last.then_inc(s_gs, 1)
        pe.wait_ge(s_vtc, C)
        for j in range(J):
            pe.matmul(bank[7][0:32, j * 64:j * 64 + 64].rearrange("p (q t) -> p q t", q=2), BKs[:, j, 1, :], arzS[:, j, :, 0:32], start=True, stop=True)
        for h in range(H):
            last = pe.matmul(bank[7][0:32, 256 + h * 32:288 + h * 32], arzS[:, h // 2, h % 2, 0:32], BKs[:, h // 2, 1, :], start=True, stop=True)
        last.then_inc(s_ms_, 1)
        pe.wait_ge(s_msc, 1)
        pe.wait_ge(s_s0s, 4)
        for h in range(H):
            last = pe.matmul(bank[4][0:32, h * 32:h * 32 + 32], Ms[:, h * 32:h * 32 + 32], MTs[:, h * 32:h * 32 + 32], start=True, stop=True)
        last.then_inc(s_m2, 1)
        took(pe, N1)
        for b in range(NB):
            for j in range(J):
                pe.matmul(bank[0][0:64, j * 128:(j + 1) * 128], arB[:, j, b * 64:b * 64 + 64], S0S[:, b, j].rearrange("p q v -> p (q v)"),
                          start=(b == 0 and j == 0), stop=False, skip_group_check=True)
        pe.wait_ge(s_m2c, 1)
        for h in range(H):
            last = pe.matmul(bank[5][0:32, h * 32:h * 32 + 32], Ms[:, h * 32:h * 32 + 32], M2s[:, h * 32:h * 32 + 32], start=True, stop=True)
        last.then_inc(s_m3, 1)
        pe.wait_ge(s_gsc, 1)
        pe.wait_ge(s_vtsc, 1)
        for h in range(H):
            last = pe.matmul(bank[0][0:32, h * 64:h * 64 + 64], GsS[0:32, h, 0:32], SAVs[0:32, h * 64:h * 64 + 64], start=False, stop=True, skip_group_check=True)
        last.then_inc(s_rs, 1)
        pe.wait_ge(s_rsc, 1)
        pe.wait_ge(s_xs, 1)
        for h in range(H):
            last = pe.matmul(bank[1][32:64, h * 64:h * 64 + 64], Xs[:, h * 32:h * 32 + 32], RHSs[:, h * 64:h * 64 + 64], start=True, stop=True)
        last.then_inc(s_sas, 1)
        pe.wait_ge(s_sasc, 1)
        for h in range(H):
            last = pe.matmul(bank[0][32:64, h * 64:h * 64 + 64], GsS[:, h, 32:64], SAVs[:, h * 64:h * 64 + 64], start=False, stop=True, skip_group_check=True)
        last.then_inc(s_os, 1)
        pe.wait_ge(s_btsc, 1)
        group(N1 + 1)
        for h in range(H):
            j, q = h // 2, h % 2
            pe.wait_ge(s_sm, h + 1)
            if h == 0:
                pe.wait_ge(s_gsc, 1)
            if h >= 4:
                pe.wait_ge(s_sn, h - 3)
            pe.matmul(bank[6 + j % 2][64 * q:64 * q + 64, :], BKtS[:, h * 64:h * 64 + 64], SAVm[h % 2].rearrange("p b v -> p (b v)"), start=True, stop=True).then_inc(s_sts, 1)
        pe.wait_ge(s_osc, 1)
        for j in range(J):
            last = pe.transpose(bank[4][:, j * 32:j * 32 + 32], OsS[32:64, j * 128:(j + 1) * 128], ident[32:64, 32:64])
        last.then_inc(s_osT, 1)
        group(N1 + 2)
        pe.wait_ge(s_sn, 2 * J)
        pe.wait_ge(s_oc, C + 1)
        for b in range(NB):
            if b >= 2:
                pe.wait_ge(s_wTc, b)
            for j in range(J):
                last = pe.transpose(bank[4 + b % 2][0:64, j * 128:(j + 1) * 128], Sn[:, j, b, :], ident)
            last.then_inc(s_wT, 1)
        for n in range(N1 + 3, len(plan)):
            group(n)
        pe.wait_ge(s_gn, KD)
        pe.wait_ge(s_wo, 16)
        pe.wait_ge(s_wTc, WT_N)
        for g in range(2 * NTILE):
            n, q = g // 2, g % 2
            r = ROWS[n]
            if g >= 4:
                pe.wait_ge(s_new, g - 3)
            for k in range(KD):
                last = pe.matmul(bank[4 + g % 4][0:r, :], merged[:, k, n * P:n * P + r], WO[:, k, 512 * q:512 * q + 512], start=(k == 0), stop=(k == KD - 1))
            last.then_inc(s_xo2, 1)


E_ALL, G_ALL, EPG = 32, 4, 8
DE = 256
CAP = 64
NOV = 16
NBLK = E_ALL + NOV
U = 4
PLE = 256


def const_layout_moe():
    at, out = 0, {}
    for name, n in (("ident", 128), ("ones", 128), ("tri", 128), ("valid", 5), ("rev4", 4), ("rev8", 8), ("idx32", 32),
                    ("thr8", 8), ("thr4", 4), ("idx16", 16)):
        out[name] = (at, n)
        at += n
    return out, at

CONST2, NCONST2 = const_layout_moe()


def make_consts_moe():
    c = np.zeros((P, NCONST2), np.float32)
    p = np.arange(P)
    def put(name, a):
        at, n = CONST2[name]
        c[:, at:at + n] = a
    put("ident", np.eye(P))
    put("ones", 1.0)
    put("tri", (p[:, None] < p[None, :]).astype(np.float32))
    valid = np.ones((P, 5))
    valid[NSM:, 4] = 0
    put("valid", valid)
    put("rev4", np.arange(4, 0, -1))
    put("rev8", np.arange(8, 0, -1))
    put("idx32", np.arange(32))
    put("thr8", CAP * np.arange(1, 9))
    put("thr4", 4 * np.arange(4))
    put("idx16", np.arange(16))
    return c


def emb_views(BIG):
    w = NTILE * D
    pin = BIG[:, w:w + NTILE * PLE].rearrange("p (n d) -> p n d", n=NTILE)
    w += NTILE * PLE
    return pin, BIG[:, w:w + 2 * D].rearrange("p (k m) -> p k m", k=2)


def load_for_experts(sp, a, kept, done):
    cst, wr, gffn, gple, bias = kept
    sp.dma_start(cst[:, :], a["consts2"]).then_inc(done, 16)
    sp.dma_start(gffn[:, :], a["norm_ffn"][0].rearrange("(p k) -> p k", k=KD)).then_inc(done, 16)
    sp.dma_start(gple[:, :], a["norm_ple"][0].rearrange("(p k) -> p k", k=KD)).then_inc(done, 16)
    sp.dma_start(wr[:, :, 0:4], a["w_route_group"][0].rearrange("(p k) e -> p k e", k=KD)).then_inc(done, 16)
    sp.dma_start(wr[:, :, 4:36], a["w_route_expert"][0].rearrange("(p k) e -> p k e", k=KD)).then_inc(done, 16)
    sp.dma_start(bias[:, 0:4], a["b_route_group"][0].partition_broadcast(P)).then_inc(done, 16)
    sp.dma_start(bias[:, 4:36], a["b_route_expert"][0].partition_broadcast(P)).then_inc(done, 16)
    return 7 * 16


def load_embeddings(sp, a, BIG, done):
    pin, wproj = emb_views(BIG)
    for n in range(NTILE):
        src = a["p_prompt"][0, 0, n * P:(n + 1) * P, :] if n < 4 else a["p_sample"][0].rearrange("b t d -> (b t) d")
        sp.dma_start(pin[0:ROWS[n], n, :], src).then_inc(done, 16)
    sp.dma_start(wproj, a["w_ple_proj"][0].rearrange("(k p) m -> p k m", p=P)).then_inc(done, 16)
    return (NTILE + 1) * 16


def experts(nc, a, o, ctx, BIG, bank, kept):
    def sb(name, shape, dt=F32):
        return ctx.enter_context(nc.sbuf_tensor(name, shape, dt))

    def sem(name):
        return ctx.enter_context(nc.semaphore("m_" + name))

    EARLY = 4
    U32 = mybir.dt.uint32
    W8 = 4 * T
    X1 = BIG[:, 5 * W8:5 * W8 + NTILE * D].rearrange("p (n d) -> p n d", n=NTILE)
    HN = BIG[:, 0:NTILE * D].rearrange("p (n d) -> p n d", n=NTILE)
    PP = HN
    W0 = NTILE * D
    yb = [BIG[0:64, W0 + 2048 + 1024 * k:W0 + 3072 + 1024 * k] for k in range(2)]
    xgT = [BIG[:, W0 + 4096 + 512 * k:W0 + 4608 + 512 * k].rearrange("p (k t) -> p k t", k=KD) for k in range(2)]
    W1 = 5 * W8 + NTILE * D
    sg = [BIG[0:64, W1 + 256 * k:W1 + 256 * k + 256] for k in range(2)]
    hid = [BIG[0:64, W1 + 512 + 256 * k:W1 + 768 + 256 * k] for k in range(2)]
    hidT = [BIG[:, W1 + 1024 + 128 * k:W1 + 1152 + 128 * k].rearrange("p (k t) -> p k t", k=2) for k in range(2)]
    pin, wproj = emb_views(BIG)
    pT = BIG[:, W0 + 3328:W0 + 3328 + 2 * T].rearrange("p (k t) -> p k t", k=2)
    yg = [BIG[:, W0 + 1024 * k:W0 + 1024 * k + 1024] for k in range(4)]
    hT = sb("mhT", [P, KD, T])
    xg = [hT[:, :, :].rearrange("p k t -> p (k t)")[0:64, D * k:D * k + D] for k in range(U)]
    wexp = sb("wexp", [P, U, 3 * 2048])
    wf = wexp[:, :, :].rearrange("p u x -> p (u x)")
    WG = wf[:, 0:KD * D].rearrange("p (k m) -> p k m", k=KD)
    xn = [wf[:, KD * D + 4096 + 1024 * k:KD * D + 5120 + 1024 * k] for k in range(2)]
    sq = wf[:, KD * D + 6144:KD * D + 6144 + NTILE * 1024].rearrange("p (n d) -> p n d", n=NTILE)
    gf = wf[:, KD * D + 11264:KD * D + 12288]
    sgp = [wf[:, KD * D + 12288 + 512 * k:KD * D + 12800 + 512 * k] for k in range(2)]
    cst, wr, gffn, gple, bias = kept
    c_ = lambda name: cst[:, CONST2[name][0]:CONST2[name][0] + CONST2[name][1]]
    ident = c_("ident")
    LT = sb("LT", [36, T])
    rt = sb("rt", [P, 2450])
    at = [0]

    def small(n, dt=None, **dims):
        x = rt[:, at[0]:at[0] + n]
        at[0] += n
        return x
    Lg = small(180).rearrange("p (n x) -> p n x", n=5)
    E1, E2, EE, RR, TT, ET = [small(160).rearrange("p (n x) -> p n x", n=5) for _ in range(6)]
    g4a, g4b, ohg = [small(20).rearrange("p (n x) -> p n x", n=5) for _ in range(3)]
    els, t8, oh1, oh2, th = [small(40).rearrange("p (n x) -> p n x", n=5) for _ in range(5)]
    gmax, mx, pg, m1, m2, dd, p1, p2, ssq = [small(5) for _ in range(9)]
    rank, eid, ovb, rq, isov, blk, pos, row = [small(5) for _ in range(8)]
    acc, nov, incl, excl = [small(32) for _ in range(4)]
    ov8 = small(256).rearrange("p (e j) -> p e j", e=32)
    eo16 = small(512).rearrange("p (o e) -> p o e", o=16)
    q4, nbj, eo = small(4), small(1), small(16)
    ints = sb("ints", [P, 64], U32)
    ipos = [ints[:, 0:5], ints[:, 5:10]]
    irow = [ints[:, 10:15], ints[:, 15:20]]
    tok = ints[:, 20:25]
    inb, ieo = ints[:, 25:26], ints[:, 26:42]
    idxT = sb("idxT", [CAP, NBLK], U32)
    idxc = sb("idxc", [CAP, U], U32)

    hd = nc.dram_tensor("hd", (T, D), F32, kind="Internal").ap()
    tabd = nc.dram_tensor("tabd", (CAP * NBLK, 1), U32, kind="Internal").ap()
    yd = nc.dram_tensor("yd", (NBLK * CAP, D), F32, kind="Internal").ap()

    names = ("c x1 wr gv bias pin wproj sq ms rt xn xT hT hst pT0 pTt pTc lg lgc lt ltc ge gec d dc ee rk own ohx int tab0 tab1 tab2 idx "
             "pp ppc x ic xgt xtc gu sig mul ht htc dn ybc ygf add rms xs xr xx tt ttc gt sgt plus "
             "rms2 y out wg gf v p a fs fr pos zero fill idxok xgok hidok").split()
    S = {n: sem(n) for n in names}
    s_w = [sem(f"w{k}") for k in range(U)]
    s_xg = [sem(f"xg{k}") for k in range(U)]
    s_st = [sem(f"st{k}") for k in range(2)]
    s_yg = [sem(f"yg{k}") for k in range(4)]

    block = ctx.enter_context(nc.Block())

    def load_expert(sp, k, e):
        gu = wexp[:, k, 0:4096].rearrange("p (k q f) -> p k q f", k=KD, q=2)
        src = lambda name: a[name][0][bass.ds(e, 1)] if not isinstance(e, int) else a[name][0][e:e + 1]
        sp.dma_start(gu[:, :, 0, :], src("expert_gate").rearrange("o (p k) f -> p (o k) f", k=KD)).then_inc(s_w[k], 16)
        sp.dma_start(gu[:, :, 1, :], src("expert_up").rearrange("o (p k) f -> p (o k) f", k=KD)).then_inc(s_w[k], 16)
        sp.dma_start(wexp[:, k, 4096:6144].rearrange("p (k m) -> p k m", k=2),
                     src("expert_down").rearrange("o (p k) m -> p (o k) m", k=2)).then_inc(s_w[k], 16)

    @block.sync
    def _(sp):
        for n in range(NTILE):
            sp.dma_start(hd[n * P:n * P + ROWS[n], :], HN[0:ROWS[n], n, :]).then_inc(S["hst"], 16)
        for k in range(U):
            load_expert(sp, k, k)
        with sp.Fori(1, E_ALL // U) as i:
            for k in range(U):
                sp.wait_ge(S["dn"], U * i + k - U + 1)
                load_expert(sp, k, i * U + k)
        sp.wait_ge(S["int"], 1)
        more_turns = sp.value_load(inb[0:1, :], min_val=0, max_val=NOV // U)
        n_turns, last_turn = more_turns + E_ALL // U, more_turns + (E_ALL // U - 1)
        with sp.If(more_turns > 0):
            with sp.Fori(E_ALL // U, n_turns) as i:
                for k in range(U):
                    sp.wait_ge(S["dn"], U * i + k - U + 1)
                    e = sp.value_load(ieo[0:1, bass.ds(U * i + k - E_ALL, 1)], min_val=0, max_val=E_ALL - 1)
                    load_expert(sp, k, e)
        sp.wait_ge(S["dn"], U * last_turn + 2)
        sp.dma_start(WG, a["w_ple_gate"][0].rearrange("(p k) m -> p k m", k=KD)).then_inc(S["wg"], 16)
        sp.wait_ge(S["dn"], U * n_turns)
        sp.dma_start(gf, a["norm_final"].partition_broadcast(P)).then_inc(S["gf"], 16)
        for n in range(NTILE):
            sp.wait_ge(S["y"], n + 1)
            dst = o["y_prompt"][0, n * P:(n + 1) * P, :] if n < 4 else o["y_sample"].rearrange("b t d -> (b t) d")
            sp.dma_start(dst, X1[0:ROWS[n], n, :]).then_inc(S["out"], 16)
        sp.wait_ge(S["out"], 16 * NTILE)

    @block.gpsimd
    def _(pool):
        pool.dma_start(yd[E_ALL * CAP:, :], a["w_ple_gate"][0]).then_inc(S["fill"], 16)
        pool.iota(tok, pattern=[[P, NTILE]], base=0, channel_multiplier=1).then_inc(S["p"], 1)
        pool.memset(idxT[:, :], 0).then_inc(S["zero"], 1)
        pool.wait_ge(S["zero"], 1)
        pool.dma_start(tabd.rearrange("(r b) o -> r (b o)", r=CAP), idxT[:, :]).then_inc(S["tab0"], 16)
        pool.wait_ge(S["tab0"], 16)
        pool.wait_ge(S["p"], 1)
        for i in range(2):
            pool.wait_ge(S["pos"], i + 1)
            for n in range(NTILE):
                pool.indirect_dma_start(tabd, bass.IndirectOffsetOnAxis(ap=ipos[i][0:ROWS[n], n:n + 1], axis=0), tok[0:ROWS[n], n:n + 1], None).then_inc(S["tab1"], 16)
        pool.wait_ge(S["tab1"], 16 * 2 * NTILE)
        pool.dma_start(idxT[:, :], tabd.rearrange("(r b) o -> r (b o)", r=CAP)).then_inc(S["idx"], 16)
        pool.wait_ge(S["idx"], 16)
        pool.wait_ge(S["hst"], 16 * NTILE)
        pool.wait_ge(S["pp"], 2 * NTILE)
        pool.wait_ge(S["int"], 1)
        more_turns = pool.value_load(inb[0:1, :], min_val=0, max_val=NOV // U)
        n_turns, last_turn = more_turns + E_ALL // U, more_turns + (E_ALL // U - 1)
        with pool.Fori(0, n_turns) as i:
            for k in range(U):
                x = k
                pool.wait_ge(S["xgt"], U * i + k + 1)
                pool.tensor_copy(idxc[:, x:x + 1], idxT[:, bass.ds(U * i + k, 1)]).then_inc(S["ic"], 1)
                pool.wait_ge(S["ic"], U * i + k + 1)
                pool.nop().then_inc(S["idxok"], 1)
                pool.indirect_dma_start(xg[x], None, hd, bass.IndirectOffsetOnAxis(ap=idxc[:, x:x + 1], axis=0)).then_inc(s_xg[x], 16)
        pool.wait_ge(S["fill"], 16)
        pool.wait_ge(s_st[0], 16 * 2 * n_turns)
        pool.wait_ge(s_st[1], 16 * 2 * n_turns)
        pool.nop().then_inc(S["idxok"], 1)
        for n in range(NTILE):
            for i in range(2):
                g = 2 * n + i
                if g >= 4:
                    pool.wait_ge(S["ygf"], g - 3)
                pool.indirect_dma_start(yg[g % 4][0:ROWS[n]], None, yd, bass.IndirectOffsetOnAxis(ap=irow[i][0:ROWS[n], n:n + 1], axis=0)).then_inc(s_yg[g % 4], 16)

    @block.scalar
    def _(act):
        A_ = nc.scalar.activation

        def take_embedding(n):
            act.wait_ge(S["pTt"], n + 1)
            A_(pT[:, :, n * P:n * P + ROWS[n]], bank[4 + n % 2][:, 0:256].rearrange("p (k t) -> p k t", k=2)[:, :, 0:ROWS[n]], ACT.Copy).then_inc(S["pTc"], 1)

        def take_projection(g):
            n, q = g // 2, g % 2
            act.wait_ge(S["pp"], g + 1)
            A_(PP[0:ROWS[n], n, 512 * q:512 * q + 512], bank[4 + g % 4][0:ROWS[n], :], ACT.Copy).then_inc(S["ppc"], 1)

        take_embedding(0)
        act.wait_ge(S["lg"], 1)
        for h in range(2):
            ins = A_(LT[:, h * HT:(h + 1) * HT], bank[2 + h][0:36, 0:HT], ACT.Copy)
        ins.then_inc(S["lgc"], 1)
        for n in range(1, NTILE):
            take_embedding(n)
        act.wait_ge(S["hst"], 16 * NTILE)
        act.wait_ge(S["xT"], 2 * NTILE)
        for g in range(EARLY):
            take_projection(g)
        act.wait_ge(S["ge"], 1)
        A_(g4b, g4b, ACT.Exp).then_inc(S["gec"], 1)
        act.wait_ge(S["d"], 1)
        A_(dd, dd, ACT.Exp).then_inc(S["dc"], 1)
        for g in range(EARLY, 2 * NTILE):
            take_projection(g)
        act.wait_ge(S["int"], 1)
        more_turns = act.value_load(inb[0:1, :], min_val=0, max_val=NOV // U)
        n_turns, last_turn = more_turns + E_ALL // U, more_turns + (E_ALL // U - 1)

        def sigm(b, x):
            act.wait_ge(S["gu"], b + 3)
            if not isinstance(b, int) or b:
                act.wait_ge(S["mul"], b)
            A_(sg[x], bank[2 + x][0:64, 0:DE], ACT.Sigmoid).then_inc(S["sig"], 1)

        def take_hidT(b, x):
            act.wait_ge(S["ht"], b + 1)
            A_(hidT[x], bank[1][:, 0:128].rearrange("p (k t) -> p k t", k=2), ACT.Copy).then_inc(S["htc"], 1)

        def take_y(b, x, turn):
            act.wait_ge(S["dn"], b + 1)
            if not isinstance(turn, int) or turn:
                act.wait_ge(s_st[x], turn)
            A_(yb[x][:, 0:512], bank[4 + 2 * x][0:64, :], ACT.Copy)
            A_(yb[x][:, 512:1024], bank[5 + 2 * x][0:64, :], ACT.Copy).then_inc(S["ybc"], 1)

        def store_y(b, x):
            act.wait_ge(S["ybc"], b + 1)
            act.dma_start(yd[bass.ds(b * CAP, CAP), :] if not isinstance(b, int) else yd[b * CAP:(b + 1) * CAP, :], yb[x]).then_inc(s_st[x], 16)

        act.wait_ge(S["fill"], 16)
        sigm(0, 0)
        take_hidT(0, 0)

        def step(i, k):
            b = U * i + k
            sigm(b, k % 2)
            take_y(b - 1, (k + 1) % 2, 16 * (2 * i + (k - 1) // 2))
            take_hidT(b, k % 2)
            store_y(b - 1, (k + 1) % 2)

        for k in range(1, U + 1):
            step(0, k)
        with act.Fori(1, last_turn) as i:
            for k in range(1, U + 1):
                step(i, k)
        for k in range(1, U):
            step(last_turn, k)
        last_b = U * last_turn + (U - 1)
        take_y(last_b, 1, 16 * (2 * last_turn + 1))
        store_y(last_b, 1)
        act.wait_ge(S["dn"], U * n_turns)
        for n in range(NTILE):
            act.wait_ge(S["add"], n + 1)
            A_(sq[0:ROWS[n], n, :], X1[0:ROWS[n], n, :], ACT.Square, accum_out=ssq[0:ROWS[n], n:n + 1]).then_inc(S["rms"], 1)
            act.wait_ge(S["xs"], n + 1)
            A_(ssq[0:ROWS[n], n:n + 1], ssq[0:ROWS[n], n:n + 1], ACT.Sqrt).then_inc(S["xr"], 1)

        def gate_sigmoid(g):
            n, r = g // 2, ROWS[g // 2]
            act.wait_ge(S["gt"], g + 1)
            if g >= 2:
                act.wait_ge(S["plus"], g - 1)
            A_(sgp[g % 2][0:r], bank[4 + g % 4][0:r, :], ACT.Sigmoid).then_inc(S["sgt"], 1)

        def last_norm(n):
            r = ROWS[n]
            act.wait_ge(S["plus"], 2 * n + 2)
            A_(sq[0:r, n, :], X1[0:r, n, :], ACT.Square, accum_out=ssq[0:r, n:n + 1]).then_inc(S["rms2"], 1)
            act.wait_ge(S["fs"], n + 1)
            A_(ssq[0:r, n:n + 1], ssq[0:r, n:n + 1], ACT.Sqrt).then_inc(S["fr"], 1)

        for n in range(NTILE):
            gate_sigmoid(2 * n)
            gate_sigmoid(2 * n + 1)
            if n:
                last_norm(n - 1)
        last_norm(NTILE - 1)

    @block.vector
    def _(dve):
        v = nc.vector
        done = [0]

        def link(ins):
            done[0] += 1
            ins.then_inc(S["v"], 1)
            dve.wait_ge(S["v"], done[0])

        def bc(x, *shape):
            return x.to_broadcast(list(shape))

        v.memset(Lg, 0.0)

        def take_turned(g, gain, base):
            n, q = g // 2, g % 2
            r = ROWS[n]
            dve.wait_ge(S["xT" if base == 0 else "tt"], g + 1)
            v.tensor_tensor(hT[:, 4 * q:4 * q + 4, n * P:n * P + r], bank[g % 2].rearrange("p (k t) -> p k t", k=4)[:, :, 0:r],
                            bc(gain[:, 4 * q:4 * q + 4].unsqueeze(2), P, 4, r), ALU.mult).then_inc(S["hT" if base == 0 else "ttc"], 1)

        for g in range(2 * NTILE):
            take_turned(g, gffn, 0)
        dve.wait_ge(S["lt"], 1)
        pl = bank[0][:, 0:180].rearrange("p (n x) -> p n x", n=5)
        v.tensor_tensor(Lg[:, 0:4], pl[:, 0:4], bc(bias[:, :].unsqueeze(1), P, 4, 36), ALU.add)
        link(v.tensor_tensor(Lg[0:NSM, 4], pl[0:NSM, 4], bias[0:NSM, :], ALU.add))
        gl, el = Lg[:, :, 0:4], Lg[:, :, 4:36]

        def first_best(x, best, hot, rev, n, work):
            link(v.tensor_reduce(best, x, AX.X, ALU.max))
            link(v.tensor_tensor(work, x, bc(best.unsqueeze(2), P, 5, n), ALU.is_equal))
            link(v.tensor_tensor(work, work, bc(rev.unsqueeze(1), P, 5, n), ALU.mult))
            link(v.tensor_reduce(mx, work, AX.X, ALU.max))
            link(v.tensor_tensor(hot, work, bc(mx.unsqueeze(2), P, 5, n), ALU.is_equal))

        first_best(gl, gmax, ohg, c_("rev4"), 4, g4a)
        link(v.tensor_tensor(ohg, ohg, bc(c_("valid").unsqueeze(2), P, 5, 4), ALU.mult))
        v.tensor_tensor(g4b, gl, bc(gmax.unsqueeze(2), P, 5, 4), ALU.subtract).then_inc(S["ge"], 1)
        link(v.tensor_tensor(ET.rearrange("p n (g e) -> p n g e", g=4), el.rearrange("p n (g e) -> p n g e", g=4),
                             bc(ohg.unsqueeze(3), P, 5, 4, 8), ALU.mult))
        link(v.tensor_reduce(els, ET.rearrange("p n (g e) -> p n e g", g=4), AX.X, ALU.add))
        first_best(els, m1, oh1, c_("rev8"), 8, t8)
        link(v.scalar_tensor_tensor(els, oh1, -1e30, els, ALU.mult, ALU.add))
        first_best(els, m2, oh2, c_("rev8"), 8, t8)
        v.tensor_tensor(dd, m2, m1, ALU.subtract).then_inc(S["d"], 1)
        for hot, E in ((oh1, E1), (oh2, E2)):
            last = v.tensor_tensor(E.rearrange("p n (g e) -> p n g e", g=4), bc(ohg.unsqueeze(3), P, 5, 4, 8), bc(hot.unsqueeze(2), P, 5, 4, 8), ALU.mult)
        link(last)
        v.tensor_tensor(EE, E1, E2, ALU.add).then_inc(S["ee"], 1)
        dve.wait_ge(S["gec"], 1)
        link(v.tensor_reduce(pg, g4b, AX.X, ALU.add))
        link(v.reciprocal(pg, pg))
        dve.wait_ge(S["dc"], 1)
        link(v.tensor_scalar(p1, dd, 1.0, None, ALU.add))
        link(v.reciprocal(p1, p1))
        link(v.tensor_tensor(p1, p1, pg, ALU.mult))
        link(v.tensor_tensor(p2, p1, dd, ALU.mult))
        dve.wait_ge(S["rk"], 1)
        v.tensor_copy(TT, bank[1][:, 0:160].rearrange("p (n x) -> p n x", n=5))
        link(v.tensor_copy(RR, bank[0][:, 256:416].rearrange("p (n x) -> p n x", n=5)))
        link(v.tensor_copy(acc, TT[:, 0]))
        for n in range(1, 5):
            link(v.tensor_tensor(RR[:, n], RR[:, n], acc, ALU.add))
            link(v.tensor_tensor(acc, acc, TT[:, n], ALU.add))
        link(v.tensor_tensor(ov8, bc(acc.unsqueeze(2), P, 32, 8), bc(c_("thr8").unsqueeze(1), P, 32, 8), ALU.is_gt))
        link(v.tensor_reduce(nov, ov8, AX.X, ALU.add))
        link(v.tensor_tensor_scan(incl, c_("ones")[:, 0:32], nov, 0.0, ALU.mult, ALU.add))
        link(v.tensor_tensor(excl, incl, nov, ALU.subtract))
        link(v.tensor_tensor(q4, bc(incl[:, 31:32], P, 4), c_("thr4"), ALU.is_gt))
        link(v.tensor_reduce(nbj, q4, AX.X, ALU.add))
        link(v.tensor_tensor(eo16, bc(incl.unsqueeze(1), P, 16, 32), bc(c_("idx16").unsqueeze(2), P, 16, 32), ALU.is_le))
        link(v.tensor_reduce(eo, eo16, AX.X, ALU.add))
        link(v.tensor_scalar(eo, eo, float(E_ALL - 1), None, ALU.min))
        v.tensor_copy(inb, nbj)
        v.tensor_copy(ieo, eo)
        for i, E in ((0, E1), (1, E2)):
            for dst, x in ((rank, RR), (eid, bc(c_("idx32").unsqueeze(1), P, 5, 32)), (ovb, bc(excl.unsqueeze(1), P, 5, 32))):
                link(v.tensor_tensor(ET, E, x, ALU.mult))
                link(v.tensor_reduce(dst, ET, AX.X, ALU.add))
            link(v.tensor_tensor(th, bc(rank.unsqueeze(2), P, 5, 8), bc(c_("thr8").unsqueeze(1), P, 5, 8), ALU.is_ge))
            link(v.tensor_reduce(rq, th, AX.X, ALU.add))
            link(v.tensor_scalar(isov, rq, 1.0, None, ALU.min))
            link(v.tensor_tensor(blk, ovb, rq, ALU.add))
            link(v.scalar_tensor_tensor(blk, blk, float(E_ALL - 1), eid, ALU.add, ALU.subtract))
            link(v.tensor_tensor(blk, blk, isov, ALU.mult))
            link(v.tensor_tensor(blk, blk, eid, ALU.add))
            link(v.scalar_tensor_tensor(rank, rq, -float(CAP), rank, ALU.mult, ALU.add))
            link(v.scalar_tensor_tensor(pos, rank, float(NBLK), blk, ALU.mult, ALU.add))
            link(v.scalar_tensor_tensor(row, blk, float(CAP), rank, ALU.mult, ALU.add))
            v.tensor_copy(ipos[i], pos).then_inc(S["pos"], 1)
            link(v.tensor_copy(irow[i], row))
        v.tensor_copy(nbj, nbj).then_inc(S["int"], 1)
        dve.wait_ge(S["int"], 1)
        more_turns = dve.value_load(inb[0:1, :], min_val=0, max_val=NOV // U)
        n_turns, last_turn = more_turns + E_ALL // U, more_turns + (E_ALL // U - 1)

        def take_x(b, x):
            dve.wait_ge(S["xgt"], b + 1 + U)
            dve.wait_ge(S["gu"], b + 1)
            v.tensor_tensor(xgT[x], bank[0].rearrange("p (k t) -> p k t", k=KD), bc(gffn[:, :].unsqueeze(2), P, KD, CAP), ALU.mult).then_inc(S["xtc"], 1)

        def swiglu(b, x):
            dve.wait_ge(S["sig"], b + 1)
            v.tensor_tensor(sg[x], sg[x], bank[2 + x][0:64, 0:DE], ALU.mult).then_inc(S["xx"], 1)
            dve.wait_ge(S["xx"], b + 1)
            v.tensor_tensor(hid[x], sg[x], bank[2 + x][0:64, DE:2 * DE], ALU.mult).then_inc(S["mul"], 1)

        take_x(0, 0)
        swiglu(0, 0)
        take_x(1, 1)

        def step(i, k, more):
            b = U * i + k
            swiglu(b, k % 2)
            if more:
                take_x(b + 1, (k + 1) % 2)

        with dve.Fori(0, last_turn) as i:
            for k in range(1, U + 1):
                step(i, k, True)
        for k in range(1, U):
            step(last_turn, k, k < U - 1)
        dve.wait_ge(S["dn"], U * n_turns)
        for n in range(NTILE):
            r = ROWS[n]
            for i in range(2):
                g = 2 * n + i
                dve.wait_ge(s_yg[g % 4], 16 * (g // 4 + 1))
                ins = v.scalar_tensor_tensor(X1[0:r, n, :], yg[g % 4][0:r], (p1, p2)[i][0:r, n:n + 1], X1[0:r, n, :], ALU.mult, ALU.add)
                ins.then_inc(S["ygf"], 1)
                dve.wait_ge(S["ygf"], g + 1)
            v.tensor_copy(nbj, nbj).then_inc(S["add"], 1)
            dve.wait_ge(S["rms"], n + 1)
            v.tensor_scalar(ssq[0:r, n:n + 1], ssq[0:r, n:n + 1], 1.0 / D, RMS_EPS, ALU.mult, ALU.add).then_inc(S["xs"], 1)
            dve.wait_ge(S["xr"], n + 1)
            link(v.reciprocal(ssq[0:r, n:n + 1], ssq[0:r, n:n + 1]))
            if n >= 2:
                dve.wait_ge(S["tt"], 2 * n - 2)
            v.tensor_scalar(xn[n % 2][0:r], X1[0:r, n, :], ssq[0:r, n:n + 1], None, ALU.mult).then_inc(S["x"], 1)
            if n:
                take_turned(2 * n - 2, gple, 1)
                take_turned(2 * n - 1, gple, 1)
        take_turned(8, gple, 1)
        take_turned(9, gple, 1)
        dve.wait_ge(S["gf"], 16)

        def add_embedding(g):
            n, q = g // 2, g % 2
            r = ROWS[n]
            dve.wait_ge(S["sgt"], g + 1)
            link(v.tensor_tensor(sgp[g % 2][0:r], sgp[g % 2][0:r], PP[0:r, n, 512 * q:512 * q + 512], ALU.mult))
            x = X1[0:r, n, 512 * q:512 * q + 512]
            v.tensor_tensor(x, x, sgp[g % 2][0:r], ALU.add).then_inc(S["plus"], 1)

        def last_norm(n):
            r = ROWS[n]
            dve.wait_ge(S["rms2"], n + 1)
            v.tensor_scalar(ssq[0:r, n:n + 1], ssq[0:r, n:n + 1], 1.0 / D, RMS_EPS, ALU.mult, ALU.add).then_inc(S["fs"], 1)
            dve.wait_ge(S["fr"], n + 1)
            link(v.reciprocal(ssq[0:r, n:n + 1], ssq[0:r, n:n + 1]))
            v.scalar_tensor_tensor(X1[0:r, n, :], X1[0:r, n, :], ssq[0:r, n:n + 1], gf[0:r], ALU.mult, ALU.mult).then_inc(S["y"], 1)

        for n in range(NTILE):
            add_embedding(2 * n)
            add_embedding(2 * n + 1)
            if n:
                last_norm(n - 1)
        last_norm(NTILE - 1)

    @block.tensor
    def _(pe):
        for g in range(2 * NTILE):
            n, q = g // 2, g % 2
            r = ROWS[n]
            if g >= 2:
                pe.wait_ge(S["hT"], g - 1)
            for k in range(4):
                last = pe.transpose(bank[g % 2][:, k * P:k * P + r], HN[0:r, n, 4 * q + k:D:KD], ident[0:r, 0:r])
            last.then_inc(S["xT"], 1)

        def turn_embedding(n):
            r = ROWS[n]
            if n >= 2:
                pe.wait_ge(S["pTc"], n - 1)
            for k in range(2):
                last = pe.transpose(bank[4 + n % 2][:, k * P:k * P + r], pin[0:r, n, k * P:(k + 1) * P], ident[0:r, 0:r])
            last.then_inc(S["pTt"], 1)

        def project_embedding(g):
            n, q = g // 2, g % 2
            r = ROWS[n]
            if g >= 4:
                pe.wait_ge(S["ppc"], g - 3)
            for k in range(2):
                last = pe.matmul(bank[4 + g % 4][0:r, :], pT[:, k, n * P:n * P + r], wproj[:, k, 512 * q:512 * q + 512], start=(k == 0), stop=(k == 1))
            last.then_inc(S["pp"], 1)

        turn_embedding(0)
        pe.wait_ge(S["hT"], 2 * NTILE)
        for h in range(2):
            for k in range(KD):
                last = pe.matmul(bank[2 + h][0:36, 0:HT], wr[:, k, :], hT[:, k, h * HT:(h + 1) * HT], start=(k == 0), stop=(k == KD - 1))
        last.then_inc(S["lg"], 1)
        turn_embedding(1)
        pe.wait_ge(S["lgc"], 1)
        for m in range(NTILE):
            last = pe.transpose(bank[0][0:ROWS[m], m * 36:(m + 1) * 36], LT[:, m * P:m * P + ROWS[m]], ident[0:36, 0:36])
        last.then_inc(S["lt"], 1)
        for n in range(2, NTILE):
            turn_embedding(n)
        pe.wait_ge(S["pTc"], NTILE)
        for g in range(EARLY):
            project_embedding(g)
        pe.wait_ge(S["ee"], 1)
        ee = EE.rearrange("p n x -> p (n x)")
        pe.matmul(bank[0][:, 256:416], c_("tri"), ee, start=True, stop=True)
        pe.matmul(bank[1][:, 0:160], c_("ones"), ee, start=True, stop=True).then_inc(S["rk"], 1)
        for g in range(EARLY, 2 * NTILE):
            project_embedding(g)
        for _ in range(U):
            pe.nop().then_inc(S["xgt"], 1)
        for _ in range(2):
            pe.nop().then_inc(S["gu"], 1)
        pe.wait_ge(S["ppc"], 2 * NTILE)
        pe.wait_ge(S["int"], 1)
        more_turns = pe.value_load(inb[0:1, :], min_val=0, max_val=NOV // U)
        n_turns, last_turn = more_turns + E_ALL // U, more_turns + (E_ALL // U - 1)

        def turn(b, x, w, turn_no):
            pe.wait_ge(s_xg[w], turn_no)
            if not isinstance(b, int) or b:
                pe.wait_ge(S["xtc"], b)
            pe.nop().then_inc(S["xgok"], 1)
            for k in range(KD):
                last = pe.transpose(bank[0][:, k * CAP:(k + 1) * CAP], xg[w][:, k:D:KD], ident[0:CAP, 0:CAP])
            last.then_inc(S["xgt"], 1)

        def gate_up(b, x, w, turn_no):
            pe.wait_ge(S["xtc"], b + 1)
            pe.wait_ge(s_w[w], turn_no)
            gu = wexp[:, w, 0:4096].rearrange("p (k f) -> p k f", k=KD)
            for k in range(KD):
                last = pe.matmul(bank[2 + x][0:CAP, :], xgT[x][:, k, :], gu[:, k, :], start=(k == 0), stop=(k == KD - 1))
            last.then_inc(S["gu"], 1)
            
        def turn_hidden(b, x):
            pe.wait_ge(S["mul"], b + 1)
            if not isinstance(b, int) or b:
                pe.wait_ge(S["htc"], b)
            pe.nop().then_inc(S["hidok"], 1)
            for k in range(2):
                last = pe.transpose(bank[1][:, k * CAP:(k + 1) * CAP], hid[x][:, k:DE:2], ident[0:CAP, 0:CAP])
            last.then_inc(S["ht"], 1)

        def down(b, x, w, first):
            pe.wait_ge(S["htc"], b + 1)
            if not first:
                pe.wait_ge(S["ybc"], b - 1)
            dn = wexp[:, w, 4096:6144].rearrange("p (k m) -> p k m", k=2)
            for q in range(2):
                for k in range(2):
                    last = pe.matmul(bank[4 + 2 * x + q][0:CAP, :], hidT[x][:, k, :], dn[:, k, 512 * q:512 * q + 512], start=(k == 0), stop=(k == 1))
            last.then_inc(S["dn"], 1)

        turn(0, 0, 0, 16)
        gate_up(0, 0, 0, 48)
        turn(1, 1, 1, 16)
        turn_hidden(0, 0)

        def step(i, k, more, first=False):
            b = U * i + k
            gate_up(b, k % 2, k % U, 48 * (i + k // U + 1))
            if more:
                turn(b + 1, (k + 1) % 2, (k + 1) % U, 16 * (i + (k + 1) // U + 1))
            down(b - 1, (k + 1) % 2, k - 1, first)
            turn_hidden(b, k % 2)

        for k in range(1, U + 1):
            step(0, k, True, first=(k <= 2))
        with pe.Fori(1, last_turn) as i:
            for k in range(1, U + 1):
                step(i, k, True)
        for k in range(1, U):
            step(last_turn, k, k < U - 1)
        down(U * last_turn + (U - 1), 1, U - 1, False)
        def turn_normed(n):
            r = ROWS[n]
            pe.wait_ge(S["x"], n + 1)
            for g in (2 * n, 2 * n + 1):
                if g >= 2:
                    pe.wait_ge(S["ttc"], g - 1)
                for k in range(4):
                    last = pe.transpose(bank[g % 2][:, k * P:k * P + r], xn[n % 2][0:r, 4 * (g % 2) + k:D:KD], ident[0:r, 0:r])
                last.then_inc(S["tt"], 1)

        def gate(n):
            r = ROWS[n]
            pe.wait_ge(S["ttc"], 2 * n + 2)
            for g in (2 * n, 2 * n + 1):
                if g >= 4:
                    pe.wait_ge(S["sgt"], g - 3)
                for k in range(KD):
                    last = pe.matmul(bank[4 + g % 4][0:r, :], hT[:, k, n * P:n * P + r], WG[:, k, 512 * (g % 2):512 * (g % 2) + 512], start=(k == 0), stop=(k == KD - 1))
                last.then_inc(S["gt"], 1)

        turn_normed(0)
        turn_normed(1)
        pe.wait_ge(S["wg"], 16)
        pe.wait_ge(S["ybc"], U * n_turns)
        gate(0)
        turn_normed(2)
        turn_normed(3)
        gate(1)
        turn_normed(4)
        gate(2)
        gate(3)
        gate(4)


def program(nc, a, o):
    with ExitStack() as ctx:
        BIG = ctx.enter_context(nc.sbuf_tensor("BIG", [P, 8 * 4 * T], F32))
        kept = [ctx.enter_context(nc.sbuf_tensor(n, s, F32)) for n, s in
                (("cst2", [P, NCONST2]), ("wr", [P, KD, 36]), ("gffn", [P, KD]), ("gple", [P, KD]), ("bias", [P, 36]))]
        PB = [ctx.enter_context(nc.psum_tensor(f"PB{i}", [P, 2, 512], F32)) for i in range(2)]
        PQ = [ctx.enter_context(nc.psum_tensor(f"PQ{i}", [P, 512], F32)) for i in range(4)]
        bank = [PB[0][:, 0, :], PB[0][:, 1, :], PB[1][:, 0, :], PB[1][:, 1, :]] + [q[:, :] for q in PQ]
        with nc.cleanup_on_exit():
            with ExitStack() as half:
                mixer(nc, a, o, half, BIG[:, :], PB, PQ, bank, kept)
        with ExitStack() as half:
            experts(nc, a, o, half, BIG[:, :], bank, kept)


def kernel(**inputs):
    import concourse.bacc as _bacc
    from concourse.bass_utils import run_bass_kernel_spmd as _run
    nc = _bacc.Bacc("TRN2", target_bir_lowering=False, num_devices=1)
    arrays, a = {}, {}
    for n, x in dict(inputs, consts=make_consts(), consts2=make_consts_moe()).items():
        x = np.ascontiguousarray(x)
        arrays["in_" + n] = x
        a[n] = nc.dram_tensor("in_" + n, x.shape, mybir.dt.from_np(x.dtype), kind="ExternalInput").ap()
    o = {}
    for n, s in (("y_prompt", (1, NPR, D)), ("y_sample", (NB, TS, D)), ("pool_prompt", (1, 1, 15, 512)), ("shift_prompt", (1, 1, 1792)),
                 ("wkv_prompt", (1, 1, 8, 64, 64)), ("pool_sample", (1, 8, 15, 512)), ("shift_sample", (1, 8, 1792)), ("wkv_sample", (1, 8, 8, 64, 64))):
        o[n] = nc.dram_tensor("out_" + n, s, F32, kind="ExternalOutput").ap()
    program(nc, a, o)
    r = _run(nc, [arrays], core_ids=[0]).results[0]
    return tuple(r["out_" + n] for n in o)
```

```python
import concourse.bass as bass
from concourse import mybir
from contextlib import ExitStack
import numpy as np
import math

F32 = mybir.dt.float32
ALU = mybir.AluOpType
ACT = mybir.ActivationFunctionType
AX = mybir.AxisListType

P = 128
D = 1024
KD = D // P
NPR, NB, TS = 512, 8, 4
NSM = NB * TS
T = NPR + NSM
HT = T // 2
H, HD = 8, 64
J = H // 2
C = NPR // HD
L = 64
NTILE = 5
ROWS = [P, P, P, P, NSM]
ZB = 14
DECAY = math.exp(-0.5)
GN_EPS = 64e-5
RMS_EPS = 1e-6

def const_layout():
    at, out = 0, {}
    for name, n in (("ident", 128), ("pair", 128), ("pairmean", 128), ("gmask", 128), ("gmask_s", 64),
                    ("bmask", 8), ("mt_s", 32), ("m_s", 32), ("up32", 32), ("inv", 64), ("eps", 1), ("seg", T)):
        out[name] = (at, n)
        at += n
    return out, at

CONST, NCONST = const_layout()


def make_consts():
    c = np.zeros((P, NCONST), np.float32)
    def put(name, a):
        at, n = CONST[name]
        c[:a.shape[0], at:at + n] = a
    p = np.arange(P)
    put("ident", np.eye(P))
    pair = (p[:, None] // 64 == p[None, :] // 64).astype(np.float32)
    put("pair", pair)
    put("pairmean", pair / 64)
    s = np.arange(64)
    strict = (s[:, None] < s[None, :]).astype(np.float32)
    incl = (s[:, None] <= s[None, :]).astype(np.float32)
    put("gmask", np.tile(np.concatenate([strict, incl], 1), (2, 1)))
    q = np.arange(32)
    same = q[:, None] // 4 == q[None, :] // 4
    ss, si = same & (q[:, None] < q[None, :]), same & (q[:, None] <= q[None, :])
    put("gmask_s", np.tile(np.concatenate([ss, si], 1).astype(np.float32), (2, 1)))
    put("bmask", np.tile((q[:, None] // 4 == np.arange(8)[None, :]).astype(np.float32), (2, 1)))
    put("mt_s", ss.astype(np.float32))
    put("m_s", ss.T.astype(np.float32))
    up = (q[:, None] < q[None, :]).astype(np.float32)
    put("up32", np.tile(up, (2, 1)))
    inv = np.stack([1.0 / np.minimum(np.arange(16) + 1, 2 << g) for g in range(4)])
    put("inv", np.tile(inv.reshape(1, 64), (P, 1)))
    put("eps", np.full((P, 1), GN_EPS))
    seg = np.ones(T)
    seg[0:NPR:L] = 0
    seg[NPR::TS] = 0
    put("seg", np.tile(seg[None], (P, 1)))
    return c


def mixer(nc, a, o, ctx, BIG, PB, PQ, bank, kept):
    def sb(name, shape, dt=F32):
        return ctx.enter_context(nc.sbuf_tensor(name, shape, dt))

    def sem(name):
        return nc.alloc_semaphore(name=name)

    W8 = 4 * T
    slot = lambda i, n=W8: BIG[:, i * W8:i * W8 + n]
    R, K, V, SG, A, CS, KQ, NR = [slot(i).rearrange("p (j t) -> p j t", j=J) for i in range(8)]
    xt = BIG[:, 5 * W8:5 * W8 + NTILE * D].rearrange("p (n d) -> p n d", n=NTILE)
    CW = C * 128 + 64
    ARBK = sb("ARBK", [P, 2 * J * CW])
    AR = ARBK[:, 0:J * CW].rearrange("p (j x) -> p j x", j=J)
    BK = ARBK[:, J * CW:2 * J * CW].rearrange("p (j x) -> p j x", j=J)
    hT = sb("hT", [P, KD, T])
    NU = 5
    ring = sb("ring", [P, NU, KD * P])
    merged = sb("merged", [P, KD, T])
    zx = sb("zx", [P, 2, T + 1])
    dz = sb("dz", [P, T])
    twa = sb("twa", [P, T])
    sgd = sb("sgd", [P, T])
    sga = sb("sga", [P, 2, T])
    ux = sb("ux", [P, 15 + T])
    uxs = sb("uxs", [P, NB, 19])
    pt = sb("pt", [P, 2, 15 + NPR + NB * 19])
    pooled = sb("pooled", [P, J, T])
    mixw = merged[:, 7, 0:512].rearrange("p (g d) -> p g d", g=J)
    cst = sb("cst", [P, NCONST])
    w2z = merged[:, 5, 0:512]
    a2z = merged[:, 6, 0:512]
    g2w = sb("g2w", [P, 512])
    rows = sb("rows", [46, P])
    vec = sb("vec", [P, 46])
    omka = sb("omka", [P, J])
    gmix = sb("gmix", [P, KD])
    ss = sb("ss", [P, NTILE])
    sh_in = merged[0:NB, 0:4, :].rearrange("p a b -> p (a b)")[:, 0:ZB * P]
    stT = sb("stT", [P, ZB, NB])
    sh = sb("sh", [P, 9, ZB])
    shT = sb("shT", [9 * ZB, P])
    pl_in = merged[0:120, 4, 0:512]
    plT = sb("plT", [P, J, 120])
    ul = sb("ul", [P, J, 47])
    ulT = sb("ulT", [47, 512])
    GL = sb("GL", [P, J, C + NB])

    c_ = lambda name: cst[:, CONST[name][0]:CONST[name][0] + CONST[name][1]]
    ident, pair, pairmean = c_("ident"), c_("pair"), c_("pairmean")
    MU, W0, A0, KKW, KAW, RKW, LNW, LNB, PSC = 0, 14, 18, 22, 26, 30, 34, 38, 42

    def view(i, off, n, parts=P):
        return BIG[0:parts, i * W8 + off:i * W8 + off + n]
    az = [view(0, 512 * k, 512).rearrange("p (j q t) -> p j q t", j=J, q=2) for k in range(2)]
    MDs = view(1, 0, C * H * 32, 64).rearrange("p (n t) -> p n t", t=32)
    MOs = view(3, 0, C * H * 32, 32).rearrange("p (n t) -> p n t", t=32)
    MT = view(5, 0, 1024).rearrange("p (s t) -> p s t", s=32)
    XTi = view(5, 1024, 1024).rearrange("p (s t) -> p s t", s=32)
    tmpi = view(6, 0, 1024)
    XNi = view(6, 1024, 1024).rearrange("p (s t) -> p s t", s=32)
    XA = view(7, 0, C * H * 32, 32).rearrange("p (n t) -> p n t", t=32)
    XT = BIG[0:64, 5 * W8:5 * W8 + C * H * 64].rearrange("p (n t) -> p n t", t=64)
    P2T = view(1, 0, C * H * 32, 64).rearrange("p (n t) -> p n t", t=32)
    ARZ = [view(0, 1024 * k, 1024).rearrange("p (j q x t) -> p j q x t", j=J, q=2, x=2) for k in range(2)]
    Gs = [view(1, 1024 * k, 1024).rearrange("p (h x) -> p h x", h=H) for k in range(2)]
    BKt = [view(3, 512 * k, 512) for k in range(2)]
    SAV = [view(3, 1024 + 512 * k, 512) for k in range(2)]
    RHS = view(7, 0, 512, 64)
    S0z = view(7, 512, 512).rearrange("p (j q v) -> p j q v", j=J, q=2)
    Stmp = view(7, 1024, 256).rearrange("p (j v) -> p j v", j=J)
    SoT = twa[0:64, 0:512]
    OT = pooled

    LATE = KD - 5
    plan = []
    plan += [("z", 12, "a"), ("z", 13, "a")]
    plan += [("z", 4 + j, "a") for j in range(J)]
    plan += [("lw", j, "a") for j in range(J)] + [("la", j, "a") for j in range(J)]
    plan += [("z", j, "a") for j in range(J)]
    plan += [("nrm", j, "a") for j in range(J)]
    plan += [("z", 8 + j, "a") for j in range(J)]
    plan += [("u", g, "a") for g in range(J)]
    plan += [("ga", 0, "a"), ("ga", 1, "a")]
    plan += [("mix", g, "v") for g in range(J)]
    plan += [("ba", 0, "v"), ("ba", 1, "v")]
    for m in range(2, LATE):
        plan += [("ga", m, "a"), ("ba", m, "v")]
    plan += [("bon", j, "v") for j in range(J)]
    N0 = len(plan)
    for m in range(LATE, KD):
        plan += [("ga", m, "a"), ("ba", m, "v")]
    N1 = len(plan)
    plan += [("gb", m, "a") for m in range(3)]
    plan += [("mean", j, "v") for j in range(J)] + [("gb", 3, "a")] + [("var", j, "a") for j in range(J)]
    plan += [("gb", m, "a") for m in range(4, KD)]
    plan += [("g2", j, "v") for j in range(J)]
    plan += [("bb", m, "v") for m in range(KD)]
    index = {(k, i): n for n, (k, i, _) in enumerate(plan)}
    taken = lambda n: sum(1 for q in plan[:n + 1] if q[2] == plan[n][2])

    units = []
    for kind, i, _ in plan:
        if kind == "z":
            units.append(("in", 4 + i))
        if kind == "u":
            units.append(("in", i))
        if kind == "ga":
            units.append(("in", 18 + i))
        if kind == "gb":
            units.append(("in", 26 + i))
        if kind == "ba" and i % 2 == 0:
            units.append(("ba", i))
        if kind == "bb" and i % 2 == 0:
            units.append(("bb", i))
    unit_no = {u: n for n, u in enumerate(units)}

    def unit_of(kind, i):
        if kind in ("z", "u", "ga", "gb"):
            return unit_no[("in", {"z": 4, "u": 0, "ga": 18, "gb": 26}[kind] + i)]
        if kind in ("ba", "bb"):
            return unit_no[(kind, i - i % 2)]
        return None
    last_use = {}
    for n, (kind, i, _) in enumerate(plan):
        if unit_of(kind, i) is not None:
            last_use[unit_of(kind, i)] = n

    consts_loaded = sem("consts_loaded"); vectors_loaded = sem("vectors_loaded"); x_loaded = [sem(f"x_loaded{n}") for n in range(NTILE)]
    gain_loaded = sem("gain_loaded"); shift_state_loaded = sem("shift_state_loaded"); pool_state_loaded = sem("pool_state_loaded"); low_rank_loaded = sem("low_rank_loaded"); pool_mix_loaded = sem("pool_mix_loaded")
    weights_loaded = [sem(f"weights_loaded{n}") for n in range(NU)]
    zeros_written = sem("zeros_written")
    squares_summed = sem("squares_summed"); mean_square_ready = sem("mean_square_ready"); root_ready = sem("root_ready"); x_normed = sem("x_normed"); x_turned = sem("x_turned"); x_turned_taken = sem("x_turned_taken")
    vectors_turned = sem("vectors_turned"); vectors_taken = sem("vectors_taken"); shift_state_turned = sem("shift_state_turned"); shift_state_taken = sem("shift_state_taken")
    pool_state_turned = sem("pool_state_turned"); pool_state_taken = sem("pool_state_taken")
    product_ready = sem("product_ready"); act_took_product = sem("act_took_product"); dve_took_product = sem("dve_took_product")
    shift_mixed = sem("shift_mixed"); tanh_ready = sem("tanh_ready"); gate_sigmoid_ready = sem("gate_sigmoid_ready")
    shift_rows_ready = sem("shift_rows_ready"); shift_rows_turned = sem("shift_rows_turned"); shift_rows_taken = sem("shift_rows_taken")
    pool_rows_ready = sem("pool_rows_ready"); pool_rows_turned = sem("pool_rows_turned"); pool_rows_taken = sem("pool_rows_taken"); pooled_ready = sem("pooled_ready")
    key_squares_ready = sem("key_squares_ready"); decay_sums_ready = sem("decay_sums_ready"); decays_ready = sem("decays_ready"); bonus_terms_ready = sem("bonus_terms_ready")
    outputs_stored = sem("outputs_stored")
    dve_wrote = sem("dve_wrote"); pool_wrote = sem("pool_wrote")
    inverse_buffer_set = sem("inverse_buffer_set"); a_split = sem("a_split"); pass1_products = sem("pass1_products"); pass1_masked = sem("pass1_masked"); triangles_stored = sem("triangles_stored"); triangles_loaded = sem("triangles_loaded")
    triangles_inverted = sem("triangles_inverted"); inverses_stored = sem("inverses_stored"); inverses_loaded = sem("inverses_loaded"); offdiag_first_product = sem("offdiag_first_product"); offdiag_first_taken = sem("offdiag_first_taken"); offdiag_ready = sem("offdiag_ready"); offdiag_taken = sem("offdiag_taken")
    ar_split = sem("ar_split"); gram_ready = sem("gram_ready"); gram_masked = sem("gram_masked"); bk_turned = sem("bk_turned"); bk_taken = sem("bk_taken"); values_turned = sem("values_turned"); values_taken = sem("values_taken")
    rhs_ready = sem("rhs_ready"); rhs_taken = sem("rhs_taken"); solution_ready = sem("solution_ready"); solution_taken = sem("solution_taken"); state_product_ready = sem("state_product_ready"); state_ready = sem("state_ready"); chunk_output_ready = sem("chunk_output_ready"); chunk_output_taken = sem("chunk_output_taken")
    states_turned = sem("states_turned"); states_turned_taken = sem("states_turned_taken")

    mmd = nc.dram_tensor("mmd", (128, 32, 32), F32, kind="Internal").ap()
    xtd = nc.dram_tensor("xtd", (128, 32, 32), F32, kind="Internal").ap()
    xnd = nc.dram_tensor("xnd", (128, 32, 32), F32, kind="Internal").ap()


    half = lambda x: x.rearrange("p (q t) -> p q t", q=2)
    big = lambda n: PB[n % 2][:, :, 0:HT]
    prompt = lambda x: x[:, :, 0:NPR].rearrange("p j (c t) -> p j c t", t=L)
    ARp = AR[:, :, 0:C * 128].rearrange("p j (c x t) -> p j c x t", x=2, t=L)
    BKp = BK[:, :, 0:C * 128].rearrange("p j (c x t) -> p j c x t", x=2, t=L)
    ARs = AR[:, :, C * 128:CW].rearrange("p j (x t) -> p j x t", x=2)
    BKs = BK[:, :, C * 128:CW].rearrange("p j (x t) -> p j x t", x=2)
    zorder = [i for k, i, _ in plan if k == "z"]
    zpos = {i: n for n, i in enumerate(zorder)}
    counts = {}

    def took(eng, n):
        eng.wait_ge(act_took_product if plan[n][2] == "a" else dve_took_product, taken(n))


    S0S = BIG[:, 0:NB * J * 128].rearrange("p (b j q v) -> p b j q v", b=NB, j=J, q=2)
    arB = view(3, 0, W8).rearrange("p (j y) -> p j y", j=J)
    SL = BIG[0:64, 5 * W8:5 * W8 + NB * 512]
    arzS = view(7, 0, 512).rearrange("p (j q x) -> p j q x", j=J, q=2)
    GsS = view(7, 512, 512, 64).rearrange("p (h x) -> p h x", h=H)
    MTs = view(7, 1024, 256, 32)
    Ms = view(7, 1280, 256, 32)
    M2s = view(7, 1536, 256, 32)
    Xs = view(7, 1792, 256, 32)
    RHSs = dz[0:32, 0:512]
    zxf = zx[:, :, :].rearrange("p a b -> p (a b)")
    sgaf = sga[:, :, :].rearrange("p a b -> p (a b)")
    SAVs = zxf[0:64, 0:512]
    BKtS = sgaf[0:64, 0:512]
    OsS = sgaf[0:64, 512:1024]
    SAVm = [pt[:, k, 0:512].rearrange("p (b v) -> p b v", b=NB)[0:64] for k in range(2)]
    Sn = BIG[:, 5 * W8:5 * W8 + J * NB * 64].rearrange("p (j b v) -> p j b v", j=J, b=NB)
    WOUT = BIG[0:64, 0:NB * 512].rearrange("p (b x) -> p b x", b=NB)
    SF = view(7, 1792, 256).rearrange("p (j v) -> p j v", j=J)
    SB = BIG[:, 2 * W8:4 * W8].rearrange("p (m t) -> p m t", m=KD)
    SQ = [zx[:, 0, 0:T], zx[:, 1, 0:T], sga[:, 0, :], sga[:, 1, :]]
    WO = ARBK[:, 0:KD * D].rearrange("p (k m) -> p k m", k=KD)
    x0 = BIG[:, 5 * W8:5 * W8 + NTILE * D].rearrange("p (n d) -> p n d", n=NTILE)
    (w_out_loaded, residual_loaded, x1_ready, states_stored, output_squares_ready, sample_states_loaded, sample_states_zeroed, sample_ar_spread, sample_states_turned, sample_states_split, sample_gram_ready, sample_gram_masked, sample_triangles_ready, sample_triangles_masked, sample_square_ready, sample_square_taken, sample_cube_ready, sample_inverse_ready,
     sample_values_turned, sample_values_taken, sample_bk_turned, sample_bk_taken, sample_rhs_ready, sample_rhs_taken, sample_solution_ready, sample_solution_taken, sample_output_ready, sample_output_taken, sample_output_turned, sample_values_spread, sample_state_product, sample_state_summed, merged_ready) = [
        sem(n) for n in ("w_out_loaded residual_loaded x1_ready states_stored output_squares_ready sample_states_loaded sample_states_zeroed sample_ar_spread sample_states_turned sample_states_split sample_gram_ready sample_gram_masked sample_triangles_ready sample_triangles_masked sample_square_ready sample_square_taken sample_cube_ready sample_inverse_ready "
                         "sample_values_turned sample_values_taken sample_bk_turned sample_bk_taken sample_rhs_ready sample_rhs_taken sample_solution_ready sample_solution_taken sample_output_ready sample_output_taken sample_output_turned sample_values_spread sample_state_product sample_state_summed merged_ready").split()]
    HN = BIG[:, 0:NTILE * D].rearrange("p (n d) -> p n d", n=NTILE)
    WT_N = 1 + NB

    w_out_product = sem("w_out_product")
    rate_used, key_factor_ready = sem("rate_used"), sem("key_factor_ready")
    router_inputs_loaded, embeddings_loaded = sem("router_inputs_loaded"), sem("embeddings_loaded")
    x1_squares_summed, x1_mean_square_ready, x1_root_ready = sem("x1_squares_summed"), sem("x1_mean_square_ready"), sem("x1_root_ready")
    block = ctx.enter_context(nc.Block())

    @block.sync
    def _(sp):
        sp.dma_start(cst[:, :], a["consts"]).then_inc(consts_loaded, 16)
        for n in range(NTILE):
            src = a["x_prompt"][0, n * P:(n + 1) * P, :] if n < 4 else a["x_sample"].rearrange("b t d -> (b t) d")
            sp.dma_start(xt[0:ROWS[n], n, :], src).then_inc(x_loaded[n], 16)
        sp.dma_start(gmix[:, :], a["norm_mix"][0].rearrange("(p k) -> p k", k=KD)).then_inc(gain_loaded, 16)
        for at, name, n in ((0, "shift_mu", ZB), (14, "decay_w0", 4), (18, "iclr_a0", 4), (22, "k_k", 4), (26, "k_a", 4),
                            (34, "ln_x_w", 4), (38, "ln_x_b", 4), (42, "pool_scale", 4)):
            sp.dma_start(rows[at:at + n, :], a[name][0].rearrange("(r c) -> r c", c=P)).then_inc(vectors_loaded, 16)
        sp.dma_start(rows[30:34, :], a["r_k"][0].rearrange("(j q) d -> j (q d)", q=2)).then_inc(vectors_loaded, 16)
        sp.dma_start(sh_in, a["state_shift"][0]).then_inc(shift_state_loaded, 16)
        for n, (kind, i) in enumerate(units):
            if n >= NU:
                sp.wait_ge(product_ready, last_use[n - NU] + 1)
            if kind == "in":
                dst = ring[:, n % NU, :].rearrange("p (k m) -> p k m", k=KD)
                src = a["w_in"][0][:, i * P:(i + 1) * P].rearrange("(p k) m -> p k m", k=KD)
            else:
                dst = ring[:, n % NU, :].rearrange("p (k m) -> p k m", k=4)
                w = a["w_branch_a" if kind == "ba" else "w_branch_b"][0]
                src = w[:, i * P:(i + 2) * P].rearrange("(k p) m -> p k m", p=P)
            sp.dma_start(dst, src).then_inc(weights_loaded[n % NU], 16)
            if n == 1:
                sp.dma_start(w2z[0:64, :], a["decay_w2"][0]).then_inc(low_rank_loaded, 16)
                sp.dma_start(a2z[64:128, :], a["iclr_a2"][0]).then_inc(low_rank_loaded, 16)
                sp.dma_start(g2w[:, :], a["gate_g2"][0]).then_inc(low_rank_loaded, 16)
            if n == 3:
                sp.dma_start(pl_in, a["state_pool"][0].rearrange("b s c -> (b s) c")).then_inc(pool_state_loaded, 16)
                sp.dma_start(mixw, a["pool_mix"][0].rearrange("g c d -> c g d")).then_inc(pool_mix_loaded, 16)
                sp.dma_start(o["pool_sample"][0][:, 0:11, :], a["state_pool"][0][:, 4:15, :]).then_inc(outputs_stored, 16)
            if units[n] == ("in", 18 + 3):
                sp.wait_ge(shift_rows_taken, 1)
                sp.dma_start(o["shift_prompt"][0].rearrange("b (r c) -> (b r) c", c=P), shT[0:ZB, :]).then_inc(outputs_stored, 16)
                sp.dma_start(o["shift_sample"][0].rearrange("b (r c) -> (b r) c", c=P), shT[ZB:9 * ZB, :]).then_inc(outputs_stored, 16)
                sp.wait_ge(pool_rows_taken, 1)
                sp.dma_start(o["pool_prompt"][0, 0], ulT[0:15, :]).then_inc(outputs_stored, 16)
                for b in range(NB):
                    sp.dma_start(o["pool_sample"][0, b, 11:15, :], ulT[15 + 4 * b:19 + 4 * b, :]).then_inc(outputs_stored, 16)
        counts["out"] = 16 * (1 + 2 + 1 + NB)
        sp.wait_ge(states_turned_taken, WT_N)
        sp.dma_start(WO, a["w_out"][0].rearrange("(k p) m -> p k m", p=P)).then_inc(w_out_loaded, 16)
        for n in range(NTILE):
            src = a["x_prompt"][0, n * P:(n + 1) * P, :] if n < 4 else a["x_sample"].rearrange("b t d -> (b t) d")
            sp.dma_start(x0[0:ROWS[n], n, :], src).then_inc(residual_loaded, 16)
        small = load_for_experts(sp, a, kept, router_inputs_loaded)
        sp.wait_ge(merged_ready, KD)
        emb = load_embeddings(sp, a, BIG, embeddings_loaded)
        sp.wait_ge(router_inputs_loaded, small)
        sp.wait_ge(embeddings_loaded, emb)
        sp.wait_ge(outputs_stored, counts["out"])
        sp.wait_ge(states_stored, 32)

    @block.gpsimd
    def _(pool):
        done = [0]

        def link(ins):
            done[0] += 1
            ins.then_inc(pool_wrote, 1)
            pool.wait_ge(pool_wrote, done[0])

        pool.memset(zx[:, :, 0:1], 0.0).then_inc(zeros_written, 1)
        pool.memset(ux[:, 0:15], 0.0).then_inc(zeros_written, 1)
        pool.wait_ge(zeros_written, 2)
        pool.memset(w2z[64:128, :], 0.0).then_inc(zeros_written, 1)
        pool.wait_ge(zeros_written, 3)
        pool.memset(a2z[0:64, :], 0.0).then_inc(zeros_written, 1)
        pool.wait_ge(zeros_written, 4)
        pool.wait_ge(consts_loaded, 16)
        pool.wait_ge(pool_state_taken, 1)
        inv = c_("inv").rearrange("p (g t) -> p g t", g=J)
        for g in range(J):
            w = 2 << g
            pool.wait_ge(act_took_product, taken(index["u", g]))
            link(pool.tensor_copy(uxs[:, :, 0:15], plT[:, g, :].rearrange("p (b s) -> p b s", b=NB)))
            us = ux[:, 15 + NPR:15 + T]
            link(pool.tensor_copy(uxs[:, :, 15:19], us.rearrange("p (b t) -> p b t", b=NB)))
            pool.tensor_copy(ul[:, g, 0:15], ux[:, NPR:NPR + 15])
            pool.tensor_copy(ul[:, g, 15:47], us).then_inc(pool_rows_ready, 1)
            curp, curs = ux[:, 0:15 + NPR], uxs[:, :, :]
            step, k = 1, 0
            while step < w:
                nxt = pt[:, k, 0:15 + NPR]
                nxs = pt[:, k, 15 + NPR:].rearrange("p (b x) -> p b x", b=NB)
                lo = 2 * step - 1
                pool.tensor_tensor(nxt[:, lo:], curp[:, lo:], curp[:, lo - step:15 + NPR - step], ALU.add)
                link(pool.tensor_tensor(nxs[:, :, lo:], curs[:, :, lo:], curs[:, :, lo - step:19 - step], ALU.add))
                curp, curs = nxt, nxs
                step, k = 2 * step, 1 - k
            pool.tensor_scalar(pooled[:, g, 16:NPR], curp[:, 31:15 + NPR], 1.0 / w, None, ALU.mult)
            pool.tensor_tensor(pooled[:, g, 0:16], curp[:, 15:31], inv[:, g, :], ALU.mult)
            link(pool.tensor_scalar(pooled[:, g, NPR:T].rearrange("p (b t) -> p b t", b=NB), curs[:, :, 15:19],
                                    1.0 / w, None, ALU.mult))
            pool.tensor_tensor(pooled[:, g, :], pooled[:, g, :], ux[:, 15:15 + T], ALU.subtract).then_inc(pooled_ready, 1)
            pool.wait_ge(pooled_ready, g + 1)

        def split_heads(c):
            for q in range(2):
                part = slice(64 * q, 64 * q + 64)
                ins = pool.tensor_copy(ARZ[c % 2][part, :, q, :, :].rearrange("p j x t -> p j (x t)"), AR[part, :, c * 128:(c + 1) * 128])
                if q == 0:
                    link(ins)
            ins.then_inc(ar_split, 1)
            pool.wait_ge(ar_split, c + 1)

        pool.wait_ge(bonus_terms_ready, J)
        pool.memset(az[0], 0.0)
        pool.memset(XTi, 0.0)
        link(pool.memset(az[1], 0.0))
        for c in range(C):
            if c >= 2:
                pool.wait_ge(pass1_products, c - 1)
            link(pool.tensor_copy(az[c % 2][0:64, :, 0, :], ARp[0:64, :, c, 0, :]))
            pool.tensor_copy(az[c % 2][64:128, :, 1, :], ARp[64:128, :, c, 0, :]).then_inc(a_split, 1)
            pool.wait_ge(a_split, c + 1)
        pool.memset(XTi.rearrange("p s t -> p (s t)")[:, 0:1024:33], 1.0).then_inc(inverse_buffer_set, 1)
        pool.wait_ge(pass1_masked, C)
        pool.dma_start(mmd[0:64].rearrange("q s t -> s q t"), MDs[0:32]).then_inc(triangles_stored, 16)
        pool.dma_start(mmd[64:128].rearrange("q s t -> s q t"), MDs[32:64]).then_inc(triangles_stored, 16)
        pool.wait_ge(triangles_stored, 32)
        pool.dma_start(MT, mmd).then_inc(triangles_loaded, 16)
        pool.wait_ge(pass1_products, C)
        pool.memset(ARZ[0], 0.0)
        link(pool.memset(ARZ[1], 0.0))
        pool.wait_ge(triangles_inverted, 1)
        pool.dma_start(xtd, XTi).then_inc(inverses_stored, 16)
        pool.dma_start(xnd[0:64], XNi[0:64]).then_inc(inverses_stored, 16)
        for c in range(2):
            split_heads(c)
        pool.wait_ge(inverses_stored, 32)
        pool.dma_start(XT[0:32, :, 0:32], xtd[0:64].rearrange("q j t -> j q t")).then_inc(inverses_loaded, 16)
        pool.dma_start(XT[32:64, :, 32:64], xtd[64:128].rearrange("q j t -> j q t")).then_inc(inverses_loaded, 16)
        pool.dma_start(XA, xnd[0:64].rearrange("q s j -> s q j")).then_inc(inverses_loaded, 16)
        pool.memset(XT[32:64, :, 0:32], 0.0).then_inc(inverse_buffer_set, 1)
        pool.wait_ge(inverse_buffer_set, 2)
        pool.wait_ge(offdiag_first_product, 4)
        pool.memset(S0z, 0.0).then_inc(state_ready, 1)
        for c in range(2, C):
            pool.wait_ge(gram_ready, 2 * (c - 1))
            split_heads(c)
        pool.wait_ge(solution_ready, C)
        pool.dma_start(SL.rearrange("v (b h k) -> v b h k", b=NB, h=H), a["state_wkv"][0].rearrange("b h v k -> v b h k")).then_inc(sample_states_loaded, 16)
        pool.wait_ge(chunk_output_ready, C)
        pool.memset(BIG[:, 0:NB * J * 128], 0.0).then_inc(sample_states_zeroed, 1)
        link(pool.memset(arB, 0.0))
        for x in range(2):
            for j in range(J):
                last = pool.tensor_copy(arB[:, j, :].rearrange("p (b y) -> p b y", b=NB)[:, :, x * 32:x * 32 + 4],
                                        ARs[:, j, x, :].rearrange("p (b t) -> p b t", b=NB))
        last.then_inc(sample_ar_spread, 1)
        pool.wait_ge(state_ready, C + 1)
        link(pool.memset(arzS, 0.0))
        link(pool.tensor_copy(arzS[0:64, :, 0, :], AR[0:64, :, C * 128:CW]))
        pool.tensor_copy(arzS[64:128, :, 1, :], AR[64:128, :, C * 128:CW]).then_inc(sample_ar_spread, 1)
        pool.wait_ge(sample_ar_spread, 2)
        pool.wait_ge(sample_values_taken, 1)
        pool.wait_ge(sample_solution_taken, 1)
        for h in range(H):
            if h >= 2:
                pool.wait_ge(sample_state_product, h - 1)
            pool.tensor_tensor(SAVm[h % 2], SAVs[:, h * 64:h * 64 + 64].unsqueeze(1).to_broadcast([64, NB, 64]),
                               c_("bmask")[0:64].unsqueeze(2).to_broadcast([64, NB, 64]), ALU.mult).then_inc(sample_values_spread, 1)
        pool.wait_ge(states_turned_taken, 1)
        pool.dma_start(o["wkv_prompt"][0, 0].rearrange("h v k -> v h k"), SoT.rearrange("v (h k) -> v h k", h=H)).then_inc(states_stored, 16)
        pool.wait_ge(states_turned_taken, WT_N)
        pool.dma_start(o["wkv_sample"][0].rearrange("b h v k -> v b h k"), WOUT.rearrange("v b (h k) -> v b h k", h=H)).then_inc(states_stored, 16)

    @block.scalar
    def _(act):
        act.wait_ge(dve_wrote, 1)
        for n in range(NTILE):
            act.wait_ge(x_loaded[n], 16)
            nc.scalar.activation(ARBK[0:ROWS[n], n * D:(n + 1) * D], xt[0:ROWS[n], n, :], ACT.Square,
                                 accum_out=ss[0:ROWS[n], n:n + 1]).then_inc(squares_summed, 1)
        act.wait_ge(mean_square_ready, 1)
        nc.scalar.activation(ss[:, :], ss[:, :], ACT.Sqrt).then_inc(root_ready, 1)
        act.wait_ge(zeros_written, 4)
        act.wait_ge(vectors_taken, 1)

        def square_k(j):
            act.wait_ge(shift_mixed, zpos[4 + j] + 1)
            nc.scalar.activation(NR[:, j, :], K[:, j, :], ACT.Square, scale=vec[:, KKW + j:KKW + j + 1]).then_inc(key_squares_ready, 1)

        for n, (kind, i, eng) in enumerate(plan):
            if eng != "a":
                continue
            if n == N1:
                break
            if kind == "z":
                if zpos[i] >= 2:
                    act.wait_ge(shift_mixed, zpos[i] - 1)
                act.wait_ge(product_ready, n + 1)
                nc.scalar.activation(half(zx[:, zpos[i] % 2, 1:1 + T]), big(n), ACT.Copy).then_inc(act_took_product, 1)
                if zpos[i] == 1:
                    act.wait_ge(shift_mixed, 1)
                    nc.scalar.activation(twa[0:64, :], twa[0:64, :], ACT.Tanh).then_inc(tanh_ready, 1)
                    act.wait_ge(shift_mixed, 2)
                    nc.scalar.activation(sgd[:, :], sgd[:, :], ACT.Sigmoid).then_inc(gate_sigmoid_ready, 1)
            if kind in ("lw", "la"):
                if (kind, i) == ("lw", 0):
                    for j in range(J):
                        square_k(j)
                act.wait_ge(product_ready, n + 1)
                dst, b = (SG, W0) if kind == "lw" else (A, A0)
                nc.scalar.activation(half(dst[:, i, :]), big(n), ACT.Sigmoid, bias=vec[:, b + i:b + i + 1]).then_inc(act_took_product, 1)
            if kind == "nrm":
                act.wait_ge(product_ready, n + 1)
                nc.scalar.activation(half(NR[:, i, :]), big(n), ACT.Sqrt).then_inc(act_took_product, 1)
            if kind == "u":
                if i:
                    act.wait_ge(pooled_ready, i)
                act.wait_ge(product_ready, n + 1)
                nc.scalar.activation(half(ux[:, 15:15 + T]), big(n), ACT.Copy).then_inc(act_took_product, 1)
            if kind == "ga":
                if i >= 2:
                    act.wait_ge(dve_took_product, taken(index["ba", i - 2]))
                act.wait_ge(product_ready, n + 1)
                nc.scalar.activation(half(sga[:, i % 2, :]), big(n), ACT.Sigmoid).then_inc(act_took_product, 1)
                if i == 1:
                    act.wait_ge(decay_sums_ready, 1)
                    flat = lambda x: x.rearrange("p j t -> p (j t)")
                    nc.scalar.activation(flat(SG), flat(SG), ACT.Exp, scale=-DECAY).then_inc(decays_ready, 1)
                    nc.scalar.activation(flat(NR), flat(CS), ACT.Exp, scale=DECAY).then_inc(decays_ready, 1)
                    act.wait_ge(decays_ready, 2)
                    nc.scalar.activation(flat(CS), flat(CS), ACT.Exp, scale=-DECAY).then_inc(decays_ready, 1)
                    act.wait_ge(rate_used, 1)
                    for j in range(J):
                        nc.scalar.activation(A[:, j, :], A[:, j, :], ACT.Identity, scale=vec[:, KAW + j:KAW + j + 1], bias=omka[:, j:j + 1]).then_inc(key_factor_ready, 1)

        for r in range(4):
            act.wait_ge(offdiag_first_product, r + 1)
            if r == 0:
                act.wait_ge(triangles_stored, 32)
            nc.scalar.activation(P2T[32:64, 16 * r:16 * r + 16, :].rearrange("p n t -> p (n t)"), bank[4 + r % 2][32:64, :], ACT.Copy).then_inc(offdiag_first_taken, 1)
        for r in range(4):
            act.wait_ge(offdiag_ready, r + 1)
            nc.scalar.activation(XT[0:32, 16 * r:16 * r + 16, 32:64], bank[6 + r % 2][0:32, :].rearrange("p (n t) -> p n t", n=16), ACT.Copy).then_inc(offdiag_taken, 1)
        act.wait_ge(offdiag_first_product, 4)

        def take_turned(c):
            act.wait_ge(bk_turned, c + 1)
            if c >= 2:
                act.wait_ge(state_product_ready, c - 1)
            nc.scalar.activation(BKt[c % 2], bank[6], ACT.Copy).then_inc(bk_taken, 1)
            act.wait_ge(values_turned, c + 1)
            if c >= 2:
                act.wait_ge(chunk_output_ready, c - 1)
            nc.scalar.activation(SAV[c % 2][0:64], bank[7][0:64, :], ACT.Copy).then_inc(values_taken, 1)

        take_turned(0)
        for c in range(C):
            if c + 1 < C:
                take_turned(c + 1)
            act.wait_ge(solution_ready, c + 1)
            nc.scalar.activation(SAV[c % 2][64:128], bank[1][64:128, :], ACT.Copy).then_inc(solution_taken, 1)
            act.wait_ge(chunk_output_ready, c + 1)
            nc.scalar.activation(OT[:, :, c * L:(c + 1) * L], bank[3][:, 0:256].rearrange("p (j t) -> p j t", j=J), ACT.Copy).then_inc(chunk_output_taken, 1)
        act.wait_ge(states_turned, 1)
        nc.scalar.activation(SoT, bank[6][0:64, :], ACT.Copy).then_inc(states_turned_taken, 1)
        act.wait_ge(sample_values_turned, 1)
        nc.scalar.activation(SAVs[0:32], bank[3][0:32, :], ACT.Copy).then_inc(sample_values_taken, 1)
        act.wait_ge(sample_bk_turned, 1)
        nc.scalar.activation(BKtS, bank[2][0:64, :], ACT.Copy).then_inc(sample_bk_taken, 1)

        def take_gate(n):
            act.wait_ge(product_ready, n + 1)
            nc.scalar.activation(half(SB[:, plan[n][1], :]), big(n), ACT.Sigmoid).then_inc(act_took_product, 1)

        take_gate(N1)
        act.wait_ge(sample_rhs_ready, 1)
        nc.scalar.activation(RHSs, bank[0][0:32, :], ACT.Copy).then_inc(sample_rhs_taken, 1)
        act.wait_ge(sample_solution_ready, 1)
        nc.scalar.activation(SAVs[32:64], bank[1][32:64, :], ACT.Copy).then_inc(sample_solution_taken, 1)
        act.wait_ge(sample_output_ready, 1)
        nc.scalar.activation(OsS[32:64], bank[0][32:64, :], ACT.Copy).then_inc(sample_output_taken, 1)
        take_gate(N1 + 1)
        act.wait_ge(sample_output_turned, 1)
        nc.scalar.activation(OT[:, :, NPR:T], bank[4][:, 0:128].rearrange("p (j t) -> p j t", j=J), ACT.Copy).then_inc(chunk_output_taken, 1)
        take_gate(N1 + 2)
        act.wait_ge(sample_state_summed, 2 * J)
        for b in range(NB):
            act.wait_ge(states_turned, 2 + b)
            nc.scalar.activation(WOUT[:, b, :], bank[4 + b % 2][0:64, :], ACT.Copy).then_inc(states_turned_taken, 1)
        for n in range(N1 + 3, len(plan)):
            kind, i, eng = plan[n]
            if eng != "a":
                continue
            if kind == "gb":
                take_gate(n)
            if kind == "var":
                if i == 0:
                    for j in range(J):
                        act.wait_ge(dve_took_product, taken(index["mean", j]))
                        nc.scalar.activation(SQ[j], OT[:, j, :], ACT.Square).then_inc(output_squares_ready, 1)
                act.wait_ge(product_ready, n + 1)
                nc.scalar.activation(half(SQ[i]), big(n), ACT.Sqrt, bias=c_("eps")).then_inc(act_took_product, 1)

        act.wait_ge(states_stored, 32)
        for n in range(NTILE):
            r = ROWS[n]
            act.wait_ge(x1_ready, 2 * n + 2)
            nc.scalar.activation(HN[0:r, n, :], x0[0:r, n, :], ACT.Square, accum_out=ss[0:r, n:n + 1]).then_inc(x1_squares_summed, 1)
            act.wait_ge(x1_mean_square_ready, n + 1)
            nc.scalar.activation(ss[0:r, n:n + 1], ss[0:r, n:n + 1], ACT.Sqrt).then_inc(x1_root_ready, 1)

    @block.vector
    def _(dve):
        v = nc.vector
        done = [0]

        def link(ins):
            done[0] += 1
            ins.then_inc(dve_wrote, 1)
            dve.wait_ge(dve_wrote, done[0])

        link(v.memset(ss[:, :], 1.0))
        dve.wait_ge(squares_summed, NTILE)
        v.tensor_scalar(ss[:, :], ss[:, :], 1.0 / D, RMS_EPS, ALU.mult, ALU.add).then_inc(mean_square_ready, 1)
        dve.wait_ge(root_ready, 1)
        link(v.reciprocal(ss[:, :], ss[:, :]))
        for n in range(NTILE):
            v.tensor_scalar(xt[0:ROWS[n], n, :], xt[0:ROWS[n], n, :], ss[0:ROWS[n], n:n + 1], None, ALU.mult).then_inc(x_normed, 1)
        dve.wait_ge(vectors_turned, 1)
        v.tensor_copy(vec[:, :], bank[4][:, 0:46]).then_inc(vectors_taken, 1)
        dve.wait_ge(vectors_taken, 1)
        link(v.tensor_scalar(omka[:, :], vec[:, KAW:KAW + J], -1.0, 1.0, ALU.mult, ALU.add))
        dve.wait_ge(gain_loaded, 16)
        for g in range(2 * NTILE):
            n, q = g // 2, g % 2
            dve.wait_ge(x_turned, g + 1)
            r = ROWS[n]
            v.tensor_tensor(hT[:, 4 * q:4 * q + 4, n * P:n * P + r],
                            bank[5 + g % 2].rearrange("p (k t) -> p k t", k=4)[:, :, 0:r],
                            gmix[:, 4 * q:4 * q + 4].unsqueeze(2).to_broadcast([P, 4, r]), ALU.mult).then_inc(x_turned_taken, 1)
        dve.wait_ge(shift_state_turned, 1)
        v.tensor_copy(stT[:, :, :].rearrange("p z b -> p (z b)"), bank[7][:, 0:ZB * NB]).then_inc(shift_state_taken, 1)
        dve.wait_ge(shift_state_taken, 1)
        dve.wait_ge(consts_loaded, 16)
        dve.wait_ge(zeros_written, 4)

        def lerp(i):
            k = zpos[i]
            n = index["z", i]
            z = zx[:, k % 2, :]
            dst = {0: R, 1: K, 2: V}[i // 4][:, i % 4, :] if i < 12 else (twa[:, :] if i == 12 else sgd[:, :])
            dve.wait_ge(act_took_product, taken(n))
            v.tensor_copy(sh[:, :, i:i + 1], z[:, NPR:NPR + 33:4].unsqueeze(2)).then_inc(shift_rows_ready, 1)
            link(v.tensor_tensor(dz[:, :], z[:, 0:T], z[:, 1:1 + T], ALU.subtract))
            link(v.tensor_tensor(dz[:, NPR:T:TS], stT[:, i, :], z[:, NPR + 1:1 + T:TS], ALU.subtract))
            v.scalar_tensor_tensor(dst, dz[:, :], vec[:, MU + i:MU + i + 1], z[:, 1:1 + T], ALU.mult, ALU.add).then_inc(shift_mixed, 1)
            dve.wait_ge(shift_mixed, k + 1)

        flat = lambda x: x.rearrange("p j t -> p (j t)")
        for i in (12, 13, 4, 5, 6, 7):
            lerp(i)
        dve.wait_ge(pool_state_turned, 1)
        v.tensor_copy(plT[:, :, :].rearrange("p g r -> p (g r)"), bank[4][:, 0:480]).then_inc(pool_state_taken, 1)
        for i in (0, 1, 2, 3):
            lerp(i)
        dve.wait_ge(act_took_product, taken(index["la", 3]))
        for j in range(J):
            last = v.tensor_tensor_scan(CS[:, j, :], c_("seg"), SG[:, j, :], 0.0, ALU.mult, ALU.add)
        link(last)
        v.tensor_tensor(flat(SG), flat(CS), flat(SG), ALU.subtract)
        for j in range(J):
            last = v.tensor_scalar(KQ[:, j, :], K[:, j, :], vec[:, KKW + j:KKW + j + 1], None, ALU.mult)
        dve.wait_ge(act_took_product, taken(index["nrm", 3]))
        link(v.tensor_scalar(flat(NR), flat(NR), 1e-12, None, ALU.max))
        link(v.reciprocal(flat(NR), flat(NR)))
        v.scalar_tensor_tensor(flat(KQ), flat(KQ), -1.0, flat(NR), ALU.mult, ALU.mult).then_inc(decay_sums_ready, 1)
        dve.wait_ge(decay_sums_ready, 1)
        for i in (8, 9, 10, 11):
            lerp(i)

        def take_mix(g):
            n = index["mix", g]
            dve.wait_ge(product_ready, n + 1)
            v.tensor_scalar(half(pooled[:, g, :]), big(n), vec[:, PSC + g:PSC + g + 1], None, ALU.mult).then_inc(dve_took_product, 1)

        def take_ba(m):
            n = index["ba", m]
            dve.wait_ge(act_took_product, taken(index["ga", m]))
            dve.wait_ge(product_ready, n + 1)
            v.tensor_tensor(half(merged[:, m, :]), big(n), half(sga[:, m % 2, :]), ALU.mult).then_inc(dve_took_product, 1)

        for g in range(J):
            take_mix(g)
        dve.wait_ge(pool_rows_ready, 4)
        dve.wait_ge(shift_rows_turned, 1)
        v.tensor_copy(shT[:, :], bank[7][0:9 * ZB, 0:P]).then_inc(shift_rows_taken, 1)
        dve.wait_ge(pool_rows_turned, 1)
        v.tensor_copy(ulT[:, :], bank[4][0:47, :]).then_inc(pool_rows_taken, 1)
        take_ba(0)
        take_ba(1)
        dve.wait_ge(decays_ready, 1)
        v.tensor_tensor(ARp[:, :, :, 0, :], prompt(KQ), prompt(SG), ALU.mult)
        link(v.tensor_tensor(ARs[:, :, 0, :], KQ[:, :, NPR:T], SG[:, :, NPR:T], ALU.mult))
        v.scalar_tensor_tensor(flat(KQ), flat(KQ), -1.0, flat(A), ALU.mult, ALU.mult).then_inc(rate_used, 1)
        dve.wait_ge(rate_used, 1)
        take_ba(2)
        dve.wait_ge(decays_ready, 2)
        v.tensor_tensor(BKp[:, :, :, 1, :], prompt(KQ), prompt(NR), ALU.mult)
        v.tensor_tensor(BKs[:, :, 1, :], KQ[:, :, NPR:T], NR[:, :, NPR:T], ALU.mult)
        dve.wait_ge(key_factor_ready, J)
        link(v.tensor_tensor(flat(K), flat(K), flat(A), ALU.mult))
        v.tensor_tensor(BKp[:, :, :, 0, :], prompt(K), prompt(NR), ALU.mult)
        v.tensor_tensor(BKs[:, :, 0, :], K[:, :, NPR:T], NR[:, :, NPR:T], ALU.mult)
        dve.wait_ge(decays_ready, 3)
        v.tensor_copy(GL[:, :, 0:C], CS[:, :, L - 1:NPR:L])
        v.tensor_copy(GL[:, :, C:C + NB], CS[:, :, NPR + 3:T:TS])
        v.tensor_tensor(ARp[:, :, :, 1, :], prompt(R), prompt(CS), ALU.mult)
        v.tensor_tensor(ARs[:, :, 1, :], R[:, :, NPR:T], CS[:, :, NPR:T], ALU.mult)
        for j in range(J):
            v.scalar_tensor_tensor(KQ[:, j, :], R[:, j, :], vec[:, RKW + j:RKW + j + 1], K[:, j, :], ALU.mult, ALU.mult).then_inc(bonus_terms_ready, 1)
        for j in range(J):
            n = index["bon", j]
            dve.wait_ge(product_ready, n + 1)
            v.tensor_tensor(half(A[:, j, :]), big(n), half(V[:, j, :]), ALU.mult).then_inc(dve_took_product, 1)

        up = c_("up32")
        for c in range(C):
            dve.wait_ge(pass1_products, c + 1)
            g = bank[4 + c % 2].rearrange("p (h t) -> p h t", h=H)
            v.tensor_tensor(MDs[0:32, c * H:(c + 1) * H, :], g[0:32, :, 0:32], up[0:32].unsqueeze(1).to_broadcast([32, H, 32]), ALU.mult)
            v.tensor_tensor(MDs[32:64, c * H:(c + 1) * H, :], g[32:64, :, 32:64], up[32:64].unsqueeze(1).to_broadcast([32, H, 32]), ALU.mult)
            v.tensor_copy(MOs[0:32, c * H:(c + 1) * H, :], g[0:32, :, 32:64]).then_inc(pass1_masked, 1)
        dve.wait_ge(inverse_buffer_set, 1)
        dve.wait_ge(triangles_loaded, 16)
        BETWEEN = (8, 18, 25, 29)
        for t in range(1, 32):
            tm = tmpi[:, 0:t * t].rearrange("p (j s) -> p j s", j=t)
            link(v.tensor_tensor(tm, XTi[:, 0:t, 0:t], MT[:, 0:t, t].unsqueeze(1).to_broadcast([P, t, t]), ALU.mult))
            link(v.tensor_reduce(XTi[:, 0:t, t:t + 1], tm, AX.X, ALU.add))
            if t in BETWEEN:
                take_ba(LATE + BETWEEN.index(t))
        v.tensor_copy(XNi[0:64], XTi[0:64].rearrange("p j t -> p t j")).then_inc(triangles_inverted, 1)
        take_ba(KD - 1)

        gm = c_("gmask").unsqueeze(1).to_broadcast([P, 4, 128])

        def take_gram(c):
            for r in range(2):
                dve.wait_ge(gram_ready, 2 * c + r + 1)
                if c == 0 and r == 0:
                    dve.wait_ge(offdiag_ready, 4)
                if c >= 2:
                    dve.wait_ge(chunk_output_ready, c - 1)
                v.tensor_tensor(Gs[c % 2][:, 4 * r:4 * r + 4, :], bank[4 + r].rearrange("p (h x) -> p h x", h=4), gm, ALU.mult).then_inc(gram_masked, 1)

        take_gram(0)
        for c in range(C):
            dve.wait_ge(rhs_ready, c + 1)
            v.tensor_copy(RHS, bank[0][0:64, :]).then_inc(rhs_taken, 1)
            if c + 1 < C:
                take_gram(c + 1)
            dve.wait_ge(state_product_ready, c + 1)
            st = bank[2][:, 0:256].rearrange("p (j v) -> p j v", j=J)
            v.tensor_tensor(Stmp[0:64], st[0:64], S0z[0:64, :, 0, :], ALU.add)
            link(v.tensor_tensor(Stmp[64:128], st[64:128], S0z[64:128, :, 1, :], ALU.add))
            gl = GL[:, :, c].unsqueeze(2).to_broadcast([P, J, 64])
            if c + 1 < C:
                v.tensor_tensor(S0z[0:64, :, 0, :], Stmp[0:64], gl[0:64], ALU.mult)
                v.tensor_tensor(S0z[64:128, :, 1, :], Stmp[64:128], gl[64:128], ALU.mult).then_inc(state_ready, 1)
            else:
                v.tensor_tensor(SF, Stmp, gl, ALU.mult).then_inc(state_ready, 1)
        dve.wait_ge(sample_states_zeroed, 1)
        for r in range(4):
            dve.wait_ge(sample_states_turned, r + 1)
            s = bank[4 + r % 2].rearrange("p (b j v) -> p b j v", b=2, j=J)
            for q in range(2):
                for b in range(2):
                    last = v.tensor_copy(S0S[64 * q:64 * q + 64, 2 * r + b, :, q, :], s[64 * q:64 * q + 64, b])
            last.then_inc(sample_states_split, 1)
        dve.wait_ge(sample_gram_ready, 1)
        v.tensor_tensor(GsS, bank[6][0:64, :].rearrange("p (h x) -> p h x", h=H), c_("gmask_s")[0:64].unsqueeze(1).to_broadcast([64, H, 64]), ALU.mult).then_inc(sample_gram_masked, 1)
        dve.wait_ge(sample_triangles_ready, 1)
        wide = lambda x: x.rearrange("p (h t) -> p h t", h=H)
        v.tensor_tensor(wide(MTs), wide(bank[7][0:32, 0:256]), c_("mt_s")[0:32].unsqueeze(1).to_broadcast([32, H, 32]), ALU.mult)
        link(v.tensor_tensor(wide(Ms), wide(bank[7][0:32, 256:512]), c_("m_s")[0:32].unsqueeze(1).to_broadcast([32, H, 32]), ALU.mult))
        dve.wait_ge(states_turned_taken, 1)
        v.tensor_tensor(wide(Xs), wide(MTs), ident[0:32, 0:32].unsqueeze(1).to_broadcast([32, H, 32]), ALU.add).then_inc(sample_triangles_masked, 1)
        dve.wait_ge(sample_square_ready, 1)
        link(v.tensor_copy(M2s, bank[4][0:32, 0:256]))
        v.tensor_tensor(Xs, Xs, M2s, ALU.add).then_inc(sample_square_taken, 1)
        dve.wait_ge(sample_square_taken, 1)
        dve.wait_ge(sample_cube_ready, 1)
        v.tensor_tensor(Xs, Xs, bank[5][0:32, 0:256], ALU.add).then_inc(sample_inverse_ready, 1)
        for h in range(H):
            j, q = h // 2, h % 2
            dve.wait_ge(sample_state_product, h + 1)
            sn = Sn[64 * q:64 * q + 64, j]
            link(v.tensor_tensor(sn, bank[6 + j % 2][64 * q:64 * q + 64, :].rearrange("p (b v) -> p b v", b=NB), S0S[64 * q:64 * q + 64, :, j, q, :], ALU.add))
            v.tensor_tensor(sn, sn, GL[64 * q:64 * q + 64, j, C:C + NB].unsqueeze(2).to_broadcast([64, NB, 64]), ALU.mult).then_inc(sample_state_summed, 1)
        for j in range(J):
            last = v.tensor_scalar(A[:, j, :], A[:, j, :], vec[:, LNB + j:LNB + j + 1], None, ALU.add)
        link(last)
        for j in range(J):
            n = index["mean", j]
            dve.wait_ge(product_ready, n + 1)
            v.tensor_tensor(half(OT[:, j, :]), half(OT[:, j, :]), big(n), ALU.subtract).then_inc(dve_took_product, 1)
        for j in range(J):
            dve.wait_ge(act_took_product, taken(index["var", j]))
            link(v.reciprocal(SQ[j], SQ[j]))
            link(v.tensor_tensor(OT[:, j, :], OT[:, j, :], SQ[j], ALU.mult))
            link(v.scalar_tensor_tensor(OT[:, j, :], OT[:, j, :], vec[:, LNW + j:LNW + j + 1], A[:, j, :], ALU.mult, ALU.add))
            n = index["g2", j]
            dve.wait_ge(product_ready, n + 1)
            v.tensor_tensor(half(OT[:, j, :]), half(OT[:, j, :]), big(n), ALU.mult).then_inc(dve_took_product, 1)
        for m in range(KD):
            n = index["bb", m]
            dve.wait_ge(act_took_product, taken(index["gb", m]))
            dve.wait_ge(product_ready, n + 1)
            v.tensor_tensor(half(SB[:, m, :]), half(SB[:, m, :]), big(n), ALU.mult).then_inc(dve_took_product, 1)
            dve.wait_ge(dve_took_product, taken(n))
            v.tensor_tensor(merged[:, m, :], merged[:, m, :], SB[:, m, :], ALU.add).then_inc(merged_ready, 1)

        def norm_tile(n):
            r = ROWS[n]
            dve.wait_ge(x1_squares_summed, n + 1)
            v.tensor_scalar(ss[0:r, n:n + 1], ss[0:r, n:n + 1], 1.0 / D, RMS_EPS, ALU.mult, ALU.add).then_inc(x1_mean_square_ready, 1)
            dve.wait_ge(x1_root_ready, n + 1)
            link(v.reciprocal(ss[0:r, n:n + 1], ss[0:r, n:n + 1]))
            v.tensor_scalar(HN[0:r, n, :], x0[0:r, n, :], ss[0:r, n:n + 1], None, ALU.mult)

        dve.wait_ge(residual_loaded, 16 * NTILE)
        for g in range(2 * NTILE):
            n, q = g // 2, g % 2
            dve.wait_ge(w_out_product, g + 1)
            x = x0[0:ROWS[n], n, 512 * q:512 * q + 512]
            v.tensor_tensor(x, x, bank[4 + g % 4][0:ROWS[n], :], ALU.add).then_inc(x1_ready, 1)
            if q and n:
                norm_tile(n - 1)
        norm_tile(NTILE - 1)

    @block.tensor
    def _(pe):
        pe.wait_ge(consts_loaded, 16)
        pe.wait_ge(vectors_loaded, 16 * 9)
        pe.transpose(bank[4][:, 0:46], rows[:, :], ident[0:46, 0:46]).then_inc(vectors_turned, 1)
        for g in range(2 * NTILE):
            n, q = g // 2, g % 2
            r = ROWS[n]
            pe.wait_ge(x_normed, n + 1)
            if g >= 2:
                pe.wait_ge(x_turned_taken, g - 1)
            for k in range(4):
                last = pe.transpose(bank[5 + g % 2][:, k * P:k * P + r], xt[0:r, n, 4 * q + k:D:KD], ident[0:r, 0:r])
            last.then_inc(x_turned, 1)
        pe.wait_ge(shift_state_loaded, 16)
        for z in range(ZB):
            last = pe.transpose(bank[7][:, z * NB:(z + 1) * NB], sh_in[:, z * P:(z + 1) * P], ident[0:NB, 0:NB])
        last.then_inc(shift_state_turned, 1)
        pe.wait_ge(x_turned_taken, 2 * NTILE)

        def group(n):
            kind, i, _ = plan[n]
            if n >= 2:
                took(pe, n - 2)
            u = unit_of(kind, i)
            if u is not None:
                pe.wait_ge(weights_loaded[u % NU], 16 * (u // NU + 1))
            if kind in ("z", "u", "ga", "gb"):
                wt = ring[:, u % NU, :].rearrange("p (k m) -> p k m", k=KD)
                ops = [(wt[:, k, :], hT[:, k, :]) for k in range(KD)]
            if kind in ("ba", "bb"):
                wt = ring[:, u % NU, :].rearrange("p (k m) -> p k m", k=4)
                rhs = pooled if kind == "ba" else OT
                if (kind, i) == ("ba", 0):
                    pe.wait_ge(dve_took_product, taken(index["mix", 3]))
                if (kind, i) == ("bb", 0):
                    took(pe, index["g2", J - 1])
                ops = [(wt[:, k, (i % 2) * P:(i % 2) * P + P], rhs[:, k, :]) for k in range(J)]
            if kind in ("lw", "la"):
                pe.wait_ge(tanh_ready, 1)
                pe.wait_ge(zeros_written, 4)
                pe.wait_ge(low_rank_loaded, 48)
                ops = [((w2z if kind == "lw" else a2z)[:, i * P:(i + 1) * P], twa[:, :])]
            if kind == "nrm":
                pe.wait_ge(key_squares_ready, i + 1)
                ops = [(pair, NR[:, i, :])]
            if kind == "mix":
                pe.wait_ge(pool_mix_loaded, 16)
                pe.wait_ge(pooled_ready, i + 1)
                ops = [(mixw[:, i, :], pooled[:, i, :])]
            if kind == "bon":
                pe.wait_ge(bonus_terms_ready, i + 1)
                ops = [(pair, KQ[:, i, :])]
            if kind == "mean":
                pe.wait_ge(chunk_output_taken, C + 1)
                ops = [(pairmean, OT[:, i, :])]
            if kind == "var":
                pe.wait_ge(output_squares_ready, i + 1)
                ops = [(pairmean, SQ[i])]
            if kind == "g2":
                ops = [(g2w[:, i * P:(i + 1) * P], sgd[:, :])]
            for h in range(2):
                for k, (w, x) in enumerate(ops):
                    last = pe.matmul(PB[n % 2][:, h, 0:HT], w, x[:, h * HT:(h + 1) * HT], start=(k == 0), stop=(k == len(ops) - 1))
            last.then_inc(product_ready, 1)

        for n in range(N0):
            if plan[n][:2] == ("lw", 0):
                pe.wait_ge(pool_state_loaded, 16)
                pe.wait_ge(vectors_taken, 1)
                for g in range(J):
                    last = pe.transpose(bank[4][:, g * 120:(g + 1) * 120], pl_in[:, g * P:(g + 1) * P], ident[0:120, 0:120])
                last.then_inc(pool_state_turned, 1)
            group(n)
            if plan[n][:2] == ("mix", 3):
                pe.wait_ge(shift_rows_ready, ZB)
                pe.wait_ge(shift_state_taken, 1)
                pe.transpose(bank[7][0:9 * ZB, 0:P], sh[:, :, :].rearrange("p i z -> p (i z)"), ident).then_inc(shift_rows_turned, 1)
                pe.wait_ge(pool_rows_ready, J)
                pe.wait_ge(pool_state_taken, 1)
                for g in range(J):
                    last = pe.transpose(bank[4][0:47, g * P:(g + 1) * P], ul[:, g, :], ident)
                last.then_inc(pool_rows_turned, 1)

        took(pe, N0 - 1)
        took(pe, N0 - 2)
        pe.wait_ge(pool_rows_taken, 1)
        for c in range(C):
            pe.wait_ge(a_split, c + 1)
            if c >= 2:
                pe.wait_ge(pass1_masked, c - 1)
            for j in range(J):
                last = pe.matmul(bank[4 + c % 2][0:64, j * 128:(j + 1) * 128], BKp[:, j, c, 1, :], az[c % 2][:, j].rearrange("p q t -> p (q t)"), start=True, stop=True)
            last.then_inc(pass1_products, 1)
        for n in range(N0, N1):
            group(n)
        pe.wait_ge(inverses_loaded, 48)
        pe.wait_ge(inverse_buffer_set, 2)
        pe.wait_ge(pass1_masked, C)
        for r in range(4):
            if r >= 2:
                pe.wait_ge(offdiag_first_taken, r - 1)
            for n in range(16):
                i = 16 * r + n
                last = pe.matmul(bank[4 + r % 2][32:64, n * 32:n * 32 + 32], MOs[0:32, i, :], XA[0:32, i, :], start=True, stop=True)
            last.then_inc(offdiag_first_product, 1)
        for r in range(4):
            pe.wait_ge(offdiag_first_taken, r + 1)
            if r >= 2:
                pe.wait_ge(offdiag_taken, r - 1)
            for n in range(16):
                i = 16 * r + n
                last = pe.matmul(bank[6 + r % 2][0:32, n * 32:n * 32 + 32], P2T[32:64, i, :], XT[32:64, i, 32:64], start=True, stop=True)
            last.then_inc(offdiag_ready, 1)

        def prepare(c):
            pe.wait_ge(ar_split, c + 1)
            if c:
                pe.wait_ge(gram_masked, 2 * c)
            else:
                pe.wait_ge(offdiag_first_taken, 4)
            for j in range(J):
                last = pe.matmul(bank[4 + j // 2][:, (j % 2) * 256:(j % 2) * 256 + 256], BK[:, j, c * 128:(c + 1) * 128],
                                 ARZ[c % 2][:, j].rearrange("p q x t -> p (q x t)"), start=True, stop=True)
                if j % 2:
                    last.then_inc(gram_ready, 1)
            if c:
                pe.wait_ge(bk_taken, c)
            else:
                pe.wait_ge(offdiag_taken, 4)
            for j in range(J):
                last = pe.transpose(bank[6][:, j * 128:(j + 1) * 128], BK[:, j, c * 128:(c + 1) * 128], ident)
            last.then_inc(bk_turned, 1)
            if c:
                pe.wait_ge(values_taken, c)
            for j in range(J):
                last = pe.transpose(bank[7][0:64, j * 128:(j + 1) * 128], V[:, j, c * L:(c + 1) * L], ident)
            last.then_inc(values_turned, 1)

        prepare(0)
        took(pe, N1 - 1)
        took(pe, N1 - 2)

        def from_values(c):
            k = c % 2
            pe.wait_ge(gram_masked, 2 * c + 2)
            pe.wait_ge(values_taken, c + 1)
            if c:
                pe.wait_ge(rhs_taken, c)
            for h in range(H):
                pe.matmul(bank[0][0:64, h * 64:h * 64 + 64], Gs[k][0:64, h, 0:64], SAV[k][0:64, h * 64:h * 64 + 64],
                          start=(h == 0), stop=False, skip_group_check=True)

        from_values(0)
        for c in range(C):
            k = c % 2
            pe.wait_ge(state_ready, c + 1)
            for j in range(J):
                last = pe.matmul(bank[0][0:64, j * 128:(j + 1) * 128], ARp[:, j, c, 0, :], S0z[:, j].rearrange("p q v -> p (q v)"),
                                 start=False, stop=True, skip_group_check=True)
            last.then_inc(rhs_ready, 1)
            if c + 1 < C:
                prepare(c + 1)
            pe.wait_ge(rhs_taken, c + 1)
            if c:
                pe.wait_ge(solution_taken, c)
            for h in range(H):
                last = pe.matmul(bank[1][64:128, h * 64:h * 64 + 64], XT[0:64, c * H + h, :], RHS[:, h * 64:h * 64 + 64], start=True, stop=True)
            last.then_inc(solution_ready, 1)
            if c:
                pe.wait_ge(chunk_output_taken, c)
            for j in range(J):
                pe.matmul(bank[3][:, j * 64:j * 64 + 64], S0z[:, j].rearrange("p q v -> p (q v)"), ARp[:, j, c, 1, :],
                          start=(j == 0), stop=False, skip_group_check=True)
            pe.wait_ge(solution_taken, c + 1)
            pe.wait_ge(bk_taken, c + 1)
            for h in range(H):
                j, q = h // 2, h % 2
                last = pe.matmul(bank[2][64 * q:64 * q + 64, j * 64:j * 64 + 64], BKt[k][:, h * 64:h * 64 + 64], SAV[k][:, h * 64:h * 64 + 64], start=True, stop=True)
            last.then_inc(state_product_ready, 1)
            for h in range(H):
                j, q = h // 2, h % 2
                last = pe.matmul(bank[3][64 * q:64 * q + 64, j * 64:j * 64 + 64], SAV[k][:, h * 64:h * 64 + 64], Gs[k][:, h, 64:128],
                                 start=False, stop=True, skip_group_check=True)
            last.then_inc(chunk_output_ready, 1)
            if c + 1 < C:
                from_values(c + 1)
        pe.wait_ge(state_ready, C + 1)
        pe.wait_ge(bk_taken, C)
        for j in range(J):
            last = pe.transpose(bank[6][0:64, j * 128:(j + 1) * 128], SF[:, j, :], ident)
        last.then_inc(states_turned, 1)

        pe.wait_ge(chunk_output_taken, C)
        for j in range(J):
            last = pe.transpose(bank[3][0:32, j * 128:(j + 1) * 128], V[:, j, NPR:T], ident)
        last.then_inc(sample_values_turned, 1)
        for j in range(J):
            last = pe.transpose(bank[2][0:64, j * 128:(j + 1) * 128], BK[:, j, C * 128:CW], ident)
        last.then_inc(sample_bk_turned, 1)
        group(N1)
        pe.wait_ge(sample_states_loaded, 16)
        pe.wait_ge(gram_masked, 2 * C)
        for r in range(4):
            if r >= 2:
                pe.wait_ge(sample_states_split, r - 1)
            for n in range(8):
                x = (8 * r + n) * 128
                last = pe.transpose(bank[4 + r % 2][:, n * 64:n * 64 + 64], SL[:, x:x + 128], ident[0:64, 0:64])
            last.then_inc(sample_states_turned, 1)
        pe.wait_ge(sample_ar_spread, 2)
        pe.wait_ge(states_turned_taken, 1)
        for j in range(J):
            last = pe.matmul(bank[6][0:64, j * 128:(j + 1) * 128], BK[:, j, C * 128:CW], arzS[:, j].rearrange("p q x -> p (q x)"), start=True, stop=True)
        last.then_inc(sample_gram_ready, 1)
        pe.wait_ge(values_taken, C)
        for j in range(J):
            pe.matmul(bank[7][0:32, j * 64:j * 64 + 64].rearrange("p (q t) -> p q t", q=2), BKs[:, j, 1, :], arzS[:, j, :, 0:32], start=True, stop=True)
        for h in range(H):
            last = pe.matmul(bank[7][0:32, 256 + h * 32:288 + h * 32], arzS[:, h // 2, h % 2, 0:32], BKs[:, h // 2, 1, :], start=True, stop=True)
        last.then_inc(sample_triangles_ready, 1)
        pe.wait_ge(sample_triangles_masked, 1)
        pe.wait_ge(sample_states_split, 4)
        for h in range(H):
            last = pe.matmul(bank[4][0:32, h * 32:h * 32 + 32], Ms[:, h * 32:h * 32 + 32], MTs[:, h * 32:h * 32 + 32], start=True, stop=True)
        last.then_inc(sample_square_ready, 1)
        took(pe, N1)
        for b in range(NB):
            for j in range(J):
                pe.matmul(bank[0][0:64, j * 128:(j + 1) * 128], arB[:, j, b * 64:b * 64 + 64], S0S[:, b, j].rearrange("p q v -> p (q v)"),
                          start=(b == 0 and j == 0), stop=False, skip_group_check=True)
        pe.wait_ge(sample_square_taken, 1)
        for h in range(H):
            last = pe.matmul(bank[5][0:32, h * 32:h * 32 + 32], Ms[:, h * 32:h * 32 + 32], M2s[:, h * 32:h * 32 + 32], start=True, stop=True)
        last.then_inc(sample_cube_ready, 1)
        pe.wait_ge(sample_gram_masked, 1)
        pe.wait_ge(sample_values_taken, 1)
        for h in range(H):
            last = pe.matmul(bank[0][0:32, h * 64:h * 64 + 64], GsS[0:32, h, 0:32], SAVs[0:32, h * 64:h * 64 + 64], start=False, stop=True, skip_group_check=True)
        last.then_inc(sample_rhs_ready, 1)
        pe.wait_ge(sample_rhs_taken, 1)
        pe.wait_ge(sample_inverse_ready, 1)
        for h in range(H):
            last = pe.matmul(bank[1][32:64, h * 64:h * 64 + 64], Xs[:, h * 32:h * 32 + 32], RHSs[:, h * 64:h * 64 + 64], start=True, stop=True)
        last.then_inc(sample_solution_ready, 1)
        pe.wait_ge(sample_solution_taken, 1)
        for h in range(H):
            last = pe.matmul(bank[0][32:64, h * 64:h * 64 + 64], GsS[:, h, 32:64], SAVs[:, h * 64:h * 64 + 64], start=False, stop=True, skip_group_check=True)
        last.then_inc(sample_output_ready, 1)
        pe.wait_ge(sample_bk_taken, 1)
        group(N1 + 1)
        for h in range(H):
            j, q = h // 2, h % 2
            pe.wait_ge(sample_values_spread, h + 1)
            if h == 0:
                pe.wait_ge(sample_gram_masked, 1)
            if h >= 4:
                pe.wait_ge(sample_state_summed, h - 3)
            pe.matmul(bank[6 + j % 2][64 * q:64 * q + 64, :], BKtS[:, h * 64:h * 64 + 64], SAVm[h % 2].rearrange("p b v -> p (b v)"), start=True, stop=True).then_inc(sample_state_product, 1)
        pe.wait_ge(sample_output_taken, 1)
        for j in range(J):
            last = pe.transpose(bank[4][:, j * 32:j * 32 + 32], OsS[32:64, j * 128:(j + 1) * 128], ident[32:64, 32:64])
        last.then_inc(sample_output_turned, 1)
        group(N1 + 2)
        pe.wait_ge(sample_state_summed, 2 * J)
        pe.wait_ge(chunk_output_taken, C + 1)
        for b in range(NB):
            if b >= 2:
                pe.wait_ge(states_turned_taken, b)
            for j in range(J):
                last = pe.transpose(bank[4 + b % 2][0:64, j * 128:(j + 1) * 128], Sn[:, j, b, :], ident)
            last.then_inc(states_turned, 1)
        for n in range(N1 + 3, len(plan)):
            group(n)
        pe.wait_ge(merged_ready, KD)
        pe.wait_ge(w_out_loaded, 16)
        pe.wait_ge(states_turned_taken, WT_N)
        for g in range(2 * NTILE):
            n, q = g // 2, g % 2
            r = ROWS[n]
            if g >= 4:
                pe.wait_ge(x1_ready, g - 3)
            for k in range(KD):
                last = pe.matmul(bank[4 + g % 4][0:r, :], merged[:, k, n * P:n * P + r], WO[:, k, 512 * q:512 * q + 512], start=(k == 0), stop=(k == KD - 1))
            last.then_inc(w_out_product, 1)


E_ALL, G_ALL, EPG = 32, 4, 8
DE = 256
CAP = 64
NOV = 16
NBLK = E_ALL + NOV
U = 4
PLE = 256


def const_layout_moe():
    at, out = 0, {}
    for name, n in (("ident", 128), ("ones", 128), ("tri", 128), ("valid", 5), ("rev4", 4), ("rev8", 8), ("idx32", 32),
                    ("thr8", 8), ("thr4", 4), ("idx16", 16)):
        out[name] = (at, n)
        at += n
    return out, at

CONST2, NCONST2 = const_layout_moe()


def make_consts_moe():
    c = np.zeros((P, NCONST2), np.float32)
    p = np.arange(P)
    def put(name, a):
        at, n = CONST2[name]
        c[:, at:at + n] = a
    put("ident", np.eye(P))
    put("ones", 1.0)
    put("tri", (p[:, None] < p[None, :]).astype(np.float32))
    valid = np.ones((P, 5))
    valid[NSM:, 4] = 0
    put("valid", valid)
    put("rev4", np.arange(4, 0, -1))
    put("rev8", np.arange(8, 0, -1))
    put("idx32", np.arange(32))
    put("thr8", CAP * np.arange(1, 9))
    put("thr4", 4 * np.arange(4))
    put("idx16", np.arange(16))
    return c


def emb_views(BIG):
    w = NTILE * D
    pin = BIG[:, w:w + NTILE * PLE].rearrange("p (n d) -> p n d", n=NTILE)
    w += NTILE * PLE
    return pin, BIG[:, w:w + 2 * D].rearrange("p (k m) -> p k m", k=2)


def load_for_experts(sp, a, kept, done):
    cst, wr, gffn, gple, bias = kept
    sp.dma_start(cst[:, :], a["consts2"]).then_inc(done, 16)
    sp.dma_start(gffn[:, :], a["norm_ffn"][0].rearrange("(p k) -> p k", k=KD)).then_inc(done, 16)
    sp.dma_start(gple[:, :], a["norm_ple"][0].rearrange("(p k) -> p k", k=KD)).then_inc(done, 16)
    sp.dma_start(wr[:, :, 0:4], a["w_route_group"][0].rearrange("(p k) e -> p k e", k=KD)).then_inc(done, 16)
    sp.dma_start(wr[:, :, 4:36], a["w_route_expert"][0].rearrange("(p k) e -> p k e", k=KD)).then_inc(done, 16)
    sp.dma_start(bias[:, 0:4], a["b_route_group"][0].partition_broadcast(P)).then_inc(done, 16)
    sp.dma_start(bias[:, 4:36], a["b_route_expert"][0].partition_broadcast(P)).then_inc(done, 16)
    return 7 * 16


def load_embeddings(sp, a, BIG, done):
    pin, wproj = emb_views(BIG)
    for n in range(NTILE):
        src = a["p_prompt"][0, 0, n * P:(n + 1) * P, :] if n < 4 else a["p_sample"][0].rearrange("b t d -> (b t) d")
        sp.dma_start(pin[0:ROWS[n], n, :], src).then_inc(done, 16)
    sp.dma_start(wproj, a["w_ple_proj"][0].rearrange("(k p) m -> p k m", p=P)).then_inc(done, 16)
    return (NTILE + 1) * 16


def experts(nc, a, o, ctx, BIG, bank, kept):
    def sb(name, shape, dt=F32):
        return ctx.enter_context(nc.sbuf_tensor(name, shape, dt))

    def sem(name):
        return ctx.enter_context(nc.semaphore("m_" + name))

    EARLY = 4
    U32 = mybir.dt.uint32
    W8 = 4 * T
    X1 = BIG[:, 5 * W8:5 * W8 + NTILE * D].rearrange("p (n d) -> p n d", n=NTILE)
    HN = BIG[:, 0:NTILE * D].rearrange("p (n d) -> p n d", n=NTILE)
    PP = HN
    W0 = NTILE * D
    yb = [BIG[0:64, W0 + 2048 + 1024 * k:W0 + 3072 + 1024 * k] for k in range(2)]
    xgT = [BIG[:, W0 + 4096 + 512 * k:W0 + 4608 + 512 * k].rearrange("p (k t) -> p k t", k=KD) for k in range(2)]
    W1 = 5 * W8 + NTILE * D
    sg = [BIG[0:64, W1 + 256 * k:W1 + 256 * k + 256] for k in range(2)]
    hid = [BIG[0:64, W1 + 512 + 256 * k:W1 + 768 + 256 * k] for k in range(2)]
    hidT = [BIG[:, W1 + 1024 + 128 * k:W1 + 1152 + 128 * k].rearrange("p (k t) -> p k t", k=2) for k in range(2)]
    pin, wproj = emb_views(BIG)
    pT = BIG[:, W0 + 3328:W0 + 3328 + 2 * T].rearrange("p (k t) -> p k t", k=2)
    yg = [BIG[:, W0 + 1024 * k:W0 + 1024 * k + 1024] for k in range(4)]
    hT = sb("mhT", [P, KD, T])
    xg = [hT[:, :, :].rearrange("p k t -> p (k t)")[0:64, D * k:D * k + D] for k in range(U)]
    wexp = sb("wexp", [P, U, 3 * 2048])
    wf = wexp[:, :, :].rearrange("p u x -> p (u x)")
    WG = wf[:, 0:KD * D].rearrange("p (k m) -> p k m", k=KD)
    xn = [wf[:, KD * D + 4096 + 1024 * k:KD * D + 5120 + 1024 * k] for k in range(2)]
    sq = wf[:, KD * D + 6144:KD * D + 6144 + NTILE * 1024].rearrange("p (n d) -> p n d", n=NTILE)
    gf = wf[:, KD * D + 11264:KD * D + 12288]
    sgp = [wf[:, KD * D + 12288 + 512 * k:KD * D + 12800 + 512 * k] for k in range(2)]
    cst, wr, gffn, gple, bias = kept
    c_ = lambda name: cst[:, CONST2[name][0]:CONST2[name][0] + CONST2[name][1]]
    ident = c_("ident")
    LT = sb("LT", [36, T])
    rt = sb("rt", [P, 2450])
    at = [0]

    def small(n, dt=None, **dims):
        x = rt[:, at[0]:at[0] + n]
        at[0] += n
        return x
    Lg = small(180).rearrange("p (n x) -> p n x", n=5)
    E1, E2, EE, RR, TT, ET = [small(160).rearrange("p (n x) -> p n x", n=5) for _ in range(6)]
    g4a, g4b, ohg = [small(20).rearrange("p (n x) -> p n x", n=5) for _ in range(3)]
    els, t8, oh1, oh2, th = [small(40).rearrange("p (n x) -> p n x", n=5) for _ in range(5)]
    gmax, mx, pg, m1, m2, dd, p1, p2, ssq = [small(5) for _ in range(9)]
    rank, eid, ovb, rq, isov, blk, pos, row = [small(5) for _ in range(8)]
    acc, nov, incl, excl = [small(32) for _ in range(4)]
    ov8 = small(256).rearrange("p (e j) -> p e j", e=32)
    eo16 = small(512).rearrange("p (o e) -> p o e", o=16)
    q4, nbj, eo = small(4), small(1), small(16)
    ints = sb("ints", [P, 64], U32)
    ipos = [ints[:, 0:5], ints[:, 5:10]]
    irow = [ints[:, 10:15], ints[:, 15:20]]
    tok = ints[:, 20:25]
    inb, ieo = ints[:, 25:26], ints[:, 26:42]
    idxT = sb("idxT", [CAP, NBLK], U32)
    idxc = sb("idxc", [CAP, U], U32)

    hd = nc.dram_tensor("hd", (T, D), F32, kind="Internal").ap()
    tabd = nc.dram_tensor("tabd", (CAP * NBLK, 1), U32, kind="Internal").ap()
    yd = nc.dram_tensor("yd", (NBLK * CAP, D), F32, kind="Internal").ap()

    names = ("block_ready block_taken choices_ready counts_ready dve_wrote emb_added emb_projected emb_projection_taken "
             "emb_taken emb_turned expert_exp_ready expert_gap_ready final_gain_loaded gate_ready "
             "gate_sigmoid_ready gate_up_ready gate_weights_loaded gather_may_start group_exp_ready group_gap_ready "
             "hidden_may_turn hidden_ready hidden_taken hidden_turned indices_copied iota_ready last_mean_square last_root "
             "last_squares_summed logits_ready logits_taken logits_turned mean_square_ready normed_taken normed_turned "
             "plan_ready root_ready row_added rows_may_turn rows_taken rows_turned sigmoid_ready silu_ready slots_ready "
             "squares_summed table_filled table_loaded table_zeroed unused_rows_filled x_normed x_stored x_turned "
             "x_turned_taken y_ready y_stored zeros_written").split()
    S = {n: sem(n) for n in names}
    expert_loaded = [sem(f"expert_loaded{k}") for k in range(U)]
    rows_gathered = [sem(f"rows_gathered{k}") for k in range(U)]
    rows_stored = [sem(f"rows_stored{k}") for k in range(2)]
    rows_fetched = [sem(f"rows_fetched{k}") for k in range(4)]

    block = ctx.enter_context(nc.Block())

    def load_expert(sp, k, e):
        gu = wexp[:, k, 0:4096].rearrange("p (k q f) -> p k q f", k=KD, q=2)
        src = lambda name: a[name][0][bass.ds(e, 1)] if not isinstance(e, int) else a[name][0][e:e + 1]
        sp.dma_start(gu[:, :, 0, :], src("expert_gate").rearrange("o (p k) f -> p (o k) f", k=KD)).then_inc(expert_loaded[k], 16)
        sp.dma_start(gu[:, :, 1, :], src("expert_up").rearrange("o (p k) f -> p (o k) f", k=KD)).then_inc(expert_loaded[k], 16)
        sp.dma_start(wexp[:, k, 4096:6144].rearrange("p (k m) -> p k m", k=2),
                     src("expert_down").rearrange("o (p k) m -> p (o k) m", k=2)).then_inc(expert_loaded[k], 16)

    @block.sync
    def _(sp):
        for n in range(NTILE):
            sp.dma_start(hd[n * P:n * P + ROWS[n], :], HN[0:ROWS[n], n, :]).then_inc(S["x_stored"], 16)
        for k in range(U):
            load_expert(sp, k, k)
        with sp.Fori(1, E_ALL // U) as i:
            for k in range(U):
                sp.wait_ge(S["block_ready"], U * i + k - U + 1)
                load_expert(sp, k, i * U + k)
        sp.wait_ge(S["plan_ready"], 1)
        more_turns = sp.value_load(inb[0:1, :], min_val=0, max_val=NOV // U)
        n_turns, last_turn = more_turns + E_ALL // U, more_turns + (E_ALL // U - 1)
        with sp.If(more_turns > 0):
            with sp.Fori(E_ALL // U, n_turns) as i:
                for k in range(U):
                    sp.wait_ge(S["block_ready"], U * i + k - U + 1)
                    e = sp.value_load(ieo[0:1, bass.ds(U * i + k - E_ALL, 1)], min_val=0, max_val=E_ALL - 1)
                    load_expert(sp, k, e)
        sp.wait_ge(S["block_ready"], U * last_turn + 2)
        sp.dma_start(WG, a["w_ple_gate"][0].rearrange("(p k) m -> p k m", k=KD)).then_inc(S["gate_weights_loaded"], 16)
        sp.wait_ge(S["block_ready"], U * n_turns)
        sp.dma_start(gf, a["norm_final"].partition_broadcast(P)).then_inc(S["final_gain_loaded"], 16)
        for n in range(NTILE):
            sp.wait_ge(S["y_ready"], n + 1)
            dst = o["y_prompt"][0, n * P:(n + 1) * P, :] if n < 4 else o["y_sample"].rearrange("b t d -> (b t) d")
            sp.dma_start(dst, X1[0:ROWS[n], n, :]).then_inc(S["y_stored"], 16)
        sp.wait_ge(S["y_stored"], 16 * NTILE)

    @block.gpsimd
    def _(pool):
        pool.dma_start(yd[E_ALL * CAP:, :], a["w_ple_gate"][0]).then_inc(S["unused_rows_filled"], 16)
        pool.iota(tok, pattern=[[P, NTILE]], base=0, channel_multiplier=1).then_inc(S["iota_ready"], 1)
        pool.memset(idxT[:, :], 0).then_inc(S["zeros_written"], 1)
        pool.wait_ge(S["zeros_written"], 1)
        pool.dma_start(tabd.rearrange("(r b) o -> r (b o)", r=CAP), idxT[:, :]).then_inc(S["table_zeroed"], 16)
        pool.wait_ge(S["table_zeroed"], 16)
        pool.wait_ge(S["iota_ready"], 1)
        for i in range(2):
            pool.wait_ge(S["slots_ready"], i + 1)
            for n in range(NTILE):
                pool.indirect_dma_start(tabd, bass.IndirectOffsetOnAxis(ap=ipos[i][0:ROWS[n], n:n + 1], axis=0), tok[0:ROWS[n], n:n + 1], None).then_inc(S["table_filled"], 16)
        pool.wait_ge(S["table_filled"], 16 * 2 * NTILE)
        pool.dma_start(idxT[:, :], tabd.rearrange("(r b) o -> r (b o)", r=CAP)).then_inc(S["table_loaded"], 16)
        pool.wait_ge(S["table_loaded"], 16)
        pool.wait_ge(S["x_stored"], 16 * NTILE)
        pool.wait_ge(S["emb_projected"], 2 * NTILE)
        pool.wait_ge(S["plan_ready"], 1)
        more_turns = pool.value_load(inb[0:1, :], min_val=0, max_val=NOV // U)
        n_turns, last_turn = more_turns + E_ALL // U, more_turns + (E_ALL // U - 1)
        with pool.Fori(0, n_turns) as i:
            for k in range(U):
                x = k
                pool.wait_ge(S["rows_turned"], U * i + k + 1)
                pool.tensor_copy(idxc[:, x:x + 1], idxT[:, bass.ds(U * i + k, 1)]).then_inc(S["indices_copied"], 1)
                pool.wait_ge(S["indices_copied"], U * i + k + 1)
                pool.nop().then_inc(S["gather_may_start"], 1)
                pool.indirect_dma_start(xg[x], None, hd, bass.IndirectOffsetOnAxis(ap=idxc[:, x:x + 1], axis=0)).then_inc(rows_gathered[x], 16)
        pool.wait_ge(S["unused_rows_filled"], 16)
        pool.wait_ge(rows_stored[0], 16 * 2 * n_turns)
        pool.wait_ge(rows_stored[1], 16 * 2 * n_turns)
        pool.nop().then_inc(S["gather_may_start"], 1)
        for n in range(NTILE):
            for i in range(2):
                g = 2 * n + i
                if g >= 4:
                    pool.wait_ge(S["row_added"], g - 3)
                pool.indirect_dma_start(yg[g % 4][0:ROWS[n]], None, yd, bass.IndirectOffsetOnAxis(ap=irow[i][0:ROWS[n], n:n + 1], axis=0)).then_inc(rows_fetched[g % 4], 16)

    @block.scalar
    def _(act):
        A_ = nc.scalar.activation

        def take_embedding(n):
            act.wait_ge(S["emb_turned"], n + 1)
            A_(pT[:, :, n * P:n * P + ROWS[n]], bank[4 + n % 2][:, 0:256].rearrange("p (k t) -> p k t", k=2)[:, :, 0:ROWS[n]], ACT.Copy).then_inc(S["emb_taken"], 1)

        def take_projection(g):
            n, q = g // 2, g % 2
            act.wait_ge(S["emb_projected"], g + 1)
            A_(PP[0:ROWS[n], n, 512 * q:512 * q + 512], bank[4 + g % 4][0:ROWS[n], :], ACT.Copy).then_inc(S["emb_projection_taken"], 1)

        take_embedding(0)
        act.wait_ge(S["logits_ready"], 1)
        for h in range(2):
            ins = A_(LT[:, h * HT:(h + 1) * HT], bank[2 + h][0:36, 0:HT], ACT.Copy)
        ins.then_inc(S["logits_taken"], 1)
        for n in range(1, NTILE):
            take_embedding(n)
        act.wait_ge(S["x_stored"], 16 * NTILE)
        act.wait_ge(S["x_turned"], 2 * NTILE)
        for g in range(EARLY):
            take_projection(g)
        act.wait_ge(S["group_gap_ready"], 1)
        A_(g4b, g4b, ACT.Exp).then_inc(S["group_exp_ready"], 1)
        act.wait_ge(S["expert_gap_ready"], 1)
        A_(dd, dd, ACT.Exp).then_inc(S["expert_exp_ready"], 1)
        for g in range(EARLY, 2 * NTILE):
            take_projection(g)
        act.wait_ge(S["plan_ready"], 1)
        more_turns = act.value_load(inb[0:1, :], min_val=0, max_val=NOV // U)
        n_turns, last_turn = more_turns + E_ALL // U, more_turns + (E_ALL // U - 1)

        def sigm(b, x):
            act.wait_ge(S["gate_up_ready"], b + 3)
            if not isinstance(b, int) or b:
                act.wait_ge(S["hidden_ready"], b)
            A_(sg[x], bank[2 + x][0:64, 0:DE], ACT.Sigmoid).then_inc(S["sigmoid_ready"], 1)

        def take_hidT(b, x):
            act.wait_ge(S["hidden_turned"], b + 1)
            A_(hidT[x], bank[1][:, 0:128].rearrange("p (k t) -> p k t", k=2), ACT.Copy).then_inc(S["hidden_taken"], 1)

        def take_y(b, x, turn):
            act.wait_ge(S["block_ready"], b + 1)
            if not isinstance(turn, int) or turn:
                act.wait_ge(rows_stored[x], turn)
            A_(yb[x][:, 0:512], bank[4 + 2 * x][0:64, :], ACT.Copy)
            A_(yb[x][:, 512:1024], bank[5 + 2 * x][0:64, :], ACT.Copy).then_inc(S["block_taken"], 1)

        def store_y(b, x):
            act.wait_ge(S["block_taken"], b + 1)
            act.dma_start(yd[bass.ds(b * CAP, CAP), :] if not isinstance(b, int) else yd[b * CAP:(b + 1) * CAP, :], yb[x]).then_inc(rows_stored[x], 16)

        act.wait_ge(S["unused_rows_filled"], 16)
        sigm(0, 0)
        take_hidT(0, 0)

        def step(i, k):
            b = U * i + k
            sigm(b, k % 2)
            take_y(b - 1, (k + 1) % 2, 16 * (2 * i + (k - 1) // 2))
            take_hidT(b, k % 2)
            store_y(b - 1, (k + 1) % 2)

        for k in range(1, U + 1):
            step(0, k)
        with act.Fori(1, last_turn) as i:
            for k in range(1, U + 1):
                step(i, k)
        for k in range(1, U):
            step(last_turn, k)
        last_b = U * last_turn + (U - 1)
        take_y(last_b, 1, 16 * (2 * last_turn + 1))
        store_y(last_b, 1)
        act.wait_ge(S["block_ready"], U * n_turns)
        for n in range(NTILE):
            act.wait_ge(S["row_added"], 2 * n + 2)
            A_(sq[0:ROWS[n], n, :], X1[0:ROWS[n], n, :], ACT.Square, accum_out=ssq[0:ROWS[n], n:n + 1]).then_inc(S["squares_summed"], 1)
            act.wait_ge(S["mean_square_ready"], n + 1)
            A_(ssq[0:ROWS[n], n:n + 1], ssq[0:ROWS[n], n:n + 1], ACT.Sqrt).then_inc(S["root_ready"], 1)

        def gate_sigmoid(g):
            n, r = g // 2, ROWS[g // 2]
            act.wait_ge(S["gate_ready"], g + 1)
            if g >= 2:
                act.wait_ge(S["emb_added"], g - 1)
            A_(sgp[g % 2][0:r], bank[4 + g % 4][0:r, :], ACT.Sigmoid).then_inc(S["gate_sigmoid_ready"], 1)

        def last_norm(n):
            r = ROWS[n]
            act.wait_ge(S["emb_added"], 2 * n + 2)
            A_(sq[0:r, n, :], X1[0:r, n, :], ACT.Square, accum_out=ssq[0:r, n:n + 1]).then_inc(S["last_squares_summed"], 1)
            act.wait_ge(S["last_mean_square"], n + 1)
            A_(ssq[0:r, n:n + 1], ssq[0:r, n:n + 1], ACT.Sqrt).then_inc(S["last_root"], 1)

        for n in range(NTILE):
            gate_sigmoid(2 * n)
            gate_sigmoid(2 * n + 1)
            if n:
                last_norm(n - 1)
        last_norm(NTILE - 1)

    @block.vector
    def _(dve):
        v = nc.vector
        done = [0]

        def link(ins):
            done[0] += 1
            ins.then_inc(S["dve_wrote"], 1)
            dve.wait_ge(S["dve_wrote"], done[0])

        def bc(x, *shape):
            return x.to_broadcast(list(shape))

        v.memset(Lg, 0.0)

        def take_turned(g, gain, first):
            n, q = g // 2, g % 2
            r = ROWS[n]
            dve.wait_ge(S["x_turned" if first else "normed_turned"], g + 1)
            v.tensor_tensor(hT[:, 4 * q:4 * q + 4, n * P:n * P + r], bank[g % 2].rearrange("p (k t) -> p k t", k=4)[:, :, 0:r],
                            bc(gain[:, 4 * q:4 * q + 4].unsqueeze(2), P, 4, r), ALU.mult).then_inc(S["x_turned_taken" if first else "normed_taken"], 1)

        for g in range(2 * NTILE):
            take_turned(g, gffn, True)
        dve.wait_ge(S["logits_turned"], 1)
        pl = bank[0][:, 0:180].rearrange("p (n x) -> p n x", n=5)
        v.tensor_tensor(Lg[:, 0:4], pl[:, 0:4], bc(bias[:, :].unsqueeze(1), P, 4, 36), ALU.add)
        link(v.tensor_tensor(Lg[0:NSM, 4], pl[0:NSM, 4], bias[0:NSM, :], ALU.add))
        gl, el = Lg[:, :, 0:4], Lg[:, :, 4:36]

        def first_best(x, best, hot, rev, n, work):
            link(v.tensor_reduce(best, x, AX.X, ALU.max))
            link(v.tensor_tensor(work, x, bc(best.unsqueeze(2), P, 5, n), ALU.is_equal))
            link(v.tensor_tensor(work, work, bc(rev.unsqueeze(1), P, 5, n), ALU.mult))
            link(v.tensor_reduce(mx, work, AX.X, ALU.max))
            link(v.tensor_tensor(hot, work, bc(mx.unsqueeze(2), P, 5, n), ALU.is_equal))

        first_best(gl, gmax, ohg, c_("rev4"), 4, g4a)
        link(v.tensor_tensor(ohg, ohg, bc(c_("valid").unsqueeze(2), P, 5, 4), ALU.mult))
        v.tensor_tensor(g4b, gl, bc(gmax.unsqueeze(2), P, 5, 4), ALU.subtract).then_inc(S["group_gap_ready"], 1)
        link(v.tensor_tensor(ET.rearrange("p n (g e) -> p n g e", g=4), el.rearrange("p n (g e) -> p n g e", g=4),
                             bc(ohg.unsqueeze(3), P, 5, 4, 8), ALU.mult))
        link(v.tensor_reduce(els, ET.rearrange("p n (g e) -> p n e g", g=4), AX.X, ALU.add))
        first_best(els, m1, oh1, c_("rev8"), 8, t8)
        link(v.scalar_tensor_tensor(els, oh1, -1e30, els, ALU.mult, ALU.add))
        first_best(els, m2, oh2, c_("rev8"), 8, t8)
        v.tensor_tensor(dd, m2, m1, ALU.subtract).then_inc(S["expert_gap_ready"], 1)
        for hot, E in ((oh1, E1), (oh2, E2)):
            last = v.tensor_tensor(E.rearrange("p n (g e) -> p n g e", g=4), bc(ohg.unsqueeze(3), P, 5, 4, 8), bc(hot.unsqueeze(2), P, 5, 4, 8), ALU.mult)
        link(last)
        v.tensor_tensor(EE, E1, E2, ALU.add).then_inc(S["choices_ready"], 1)
        dve.wait_ge(S["group_exp_ready"], 1)
        link(v.tensor_reduce(pg, g4b, AX.X, ALU.add))
        link(v.reciprocal(pg, pg))
        dve.wait_ge(S["expert_exp_ready"], 1)
        link(v.tensor_scalar(p1, dd, 1.0, None, ALU.add))
        link(v.reciprocal(p1, p1))
        link(v.tensor_tensor(p1, p1, pg, ALU.mult))
        link(v.tensor_tensor(p2, p1, dd, ALU.mult))
        dve.wait_ge(S["counts_ready"], 1)
        v.tensor_copy(TT, bank[1][:, 0:160].rearrange("p (n x) -> p n x", n=5))
        link(v.tensor_copy(RR, bank[0][:, 256:416].rearrange("p (n x) -> p n x", n=5)))
        link(v.tensor_copy(acc, TT[:, 0]))
        for n in range(1, 5):
            link(v.tensor_tensor(RR[:, n], RR[:, n], acc, ALU.add))
            link(v.tensor_tensor(acc, acc, TT[:, n], ALU.add))
        link(v.tensor_tensor(ov8, bc(acc.unsqueeze(2), P, 32, 8), bc(c_("thr8").unsqueeze(1), P, 32, 8), ALU.is_gt))
        link(v.tensor_reduce(nov, ov8, AX.X, ALU.add))
        link(v.tensor_tensor_scan(incl, c_("ones")[:, 0:32], nov, 0.0, ALU.mult, ALU.add))
        link(v.tensor_tensor(excl, incl, nov, ALU.subtract))
        link(v.tensor_tensor(q4, bc(incl[:, 31:32], P, 4), c_("thr4"), ALU.is_gt))
        link(v.tensor_reduce(nbj, q4, AX.X, ALU.add))
        link(v.tensor_tensor(eo16, bc(incl.unsqueeze(1), P, 16, 32), bc(c_("idx16").unsqueeze(2), P, 16, 32), ALU.is_le))
        link(v.tensor_reduce(eo, eo16, AX.X, ALU.add))
        link(v.tensor_scalar(eo, eo, float(E_ALL - 1), None, ALU.min))
        v.tensor_copy(inb, nbj)
        v.tensor_copy(ieo, eo)
        for i, E in ((0, E1), (1, E2)):
            for dst, x in ((rank, RR), (eid, bc(c_("idx32").unsqueeze(1), P, 5, 32)), (ovb, bc(excl.unsqueeze(1), P, 5, 32))):
                link(v.tensor_tensor(ET, E, x, ALU.mult))
                link(v.tensor_reduce(dst, ET, AX.X, ALU.add))
            link(v.tensor_tensor(th, bc(rank.unsqueeze(2), P, 5, 8), bc(c_("thr8").unsqueeze(1), P, 5, 8), ALU.is_ge))
            link(v.tensor_reduce(rq, th, AX.X, ALU.add))
            link(v.tensor_scalar(isov, rq, 1.0, None, ALU.min))
            link(v.tensor_tensor(blk, ovb, rq, ALU.add))
            link(v.scalar_tensor_tensor(blk, blk, float(E_ALL - 1), eid, ALU.add, ALU.subtract))
            link(v.tensor_tensor(blk, blk, isov, ALU.mult))
            link(v.tensor_tensor(blk, blk, eid, ALU.add))
            link(v.scalar_tensor_tensor(rank, rq, -float(CAP), rank, ALU.mult, ALU.add))
            link(v.scalar_tensor_tensor(pos, rank, float(NBLK), blk, ALU.mult, ALU.add))
            link(v.scalar_tensor_tensor(row, blk, float(CAP), rank, ALU.mult, ALU.add))
            v.tensor_copy(ipos[i], pos).then_inc(S["slots_ready"], 1)
            last = v.tensor_copy(irow[i], row)
            if i == 0:
                link(last)
            else:
                last.then_inc(S["plan_ready"], 1)
        dve.wait_ge(S["plan_ready"], 1)
        more_turns = dve.value_load(inb[0:1, :], min_val=0, max_val=NOV // U)
        n_turns, last_turn = more_turns + E_ALL // U, more_turns + (E_ALL // U - 1)

        def take_x(b, x):
            dve.wait_ge(S["rows_turned"], b + 1 + U)
            dve.wait_ge(S["gate_up_ready"], b + 1)
            v.tensor_tensor(xgT[x], bank[0].rearrange("p (k t) -> p k t", k=KD), bc(gffn[:, :].unsqueeze(2), P, KD, CAP), ALU.mult).then_inc(S["rows_taken"], 1)

        def swiglu(b, x):
            dve.wait_ge(S["sigmoid_ready"], b + 1)
            v.tensor_tensor(sg[x], sg[x], bank[2 + x][0:64, 0:DE], ALU.mult).then_inc(S["silu_ready"], 1)
            dve.wait_ge(S["silu_ready"], b + 1)
            v.tensor_tensor(hid[x], sg[x], bank[2 + x][0:64, DE:2 * DE], ALU.mult).then_inc(S["hidden_ready"], 1)

        take_x(0, 0)
        swiglu(0, 0)
        take_x(1, 1)

        def step(i, k, more):
            b = U * i + k
            swiglu(b, k % 2)
            if more:
                take_x(b + 1, (k + 1) % 2)

        with dve.Fori(0, last_turn) as i:
            for k in range(1, U + 1):
                step(i, k, True)
        for k in range(1, U):
            step(last_turn, k, k < U - 1)
        dve.wait_ge(S["block_ready"], U * n_turns)
        for n in range(NTILE):
            r = ROWS[n]
            for i in range(2):
                g = 2 * n + i
                dve.wait_ge(rows_fetched[g % 4], 16 * (g // 4 + 1))
                ins = v.scalar_tensor_tensor(X1[0:r, n, :], yg[g % 4][0:r], (p1, p2)[i][0:r, n:n + 1], X1[0:r, n, :], ALU.mult, ALU.add)
                ins.then_inc(S["row_added"], 1)
                dve.wait_ge(S["row_added"], g + 1)
            dve.wait_ge(S["squares_summed"], n + 1)
            v.tensor_scalar(ssq[0:r, n:n + 1], ssq[0:r, n:n + 1], 1.0 / D, RMS_EPS, ALU.mult, ALU.add).then_inc(S["mean_square_ready"], 1)
            dve.wait_ge(S["root_ready"], n + 1)
            link(v.reciprocal(ssq[0:r, n:n + 1], ssq[0:r, n:n + 1]))
            if n >= 2:
                dve.wait_ge(S["normed_turned"], 2 * n - 2)
            v.tensor_scalar(xn[n % 2][0:r], X1[0:r, n, :], ssq[0:r, n:n + 1], None, ALU.mult).then_inc(S["x_normed"], 1)
            if n:
                take_turned(2 * n - 2, gple, False)
                take_turned(2 * n - 1, gple, False)
        take_turned(8, gple, False)
        take_turned(9, gple, False)
        dve.wait_ge(S["final_gain_loaded"], 16)

        def add_embedding(g):
            n, q = g // 2, g % 2
            r = ROWS[n]
            dve.wait_ge(S["gate_sigmoid_ready"], g + 1)
            link(v.tensor_tensor(sgp[g % 2][0:r], sgp[g % 2][0:r], PP[0:r, n, 512 * q:512 * q + 512], ALU.mult))
            x = X1[0:r, n, 512 * q:512 * q + 512]
            v.tensor_tensor(x, x, sgp[g % 2][0:r], ALU.add).then_inc(S["emb_added"], 1)

        def last_norm(n):
            r = ROWS[n]
            dve.wait_ge(S["last_squares_summed"], n + 1)
            v.tensor_scalar(ssq[0:r, n:n + 1], ssq[0:r, n:n + 1], 1.0 / D, RMS_EPS, ALU.mult, ALU.add).then_inc(S["last_mean_square"], 1)
            dve.wait_ge(S["last_root"], n + 1)
            link(v.reciprocal(ssq[0:r, n:n + 1], ssq[0:r, n:n + 1]))
            v.scalar_tensor_tensor(X1[0:r, n, :], X1[0:r, n, :], ssq[0:r, n:n + 1], gf[0:r], ALU.mult, ALU.mult).then_inc(S["y_ready"], 1)

        for n in range(NTILE):
            add_embedding(2 * n)
            add_embedding(2 * n + 1)
            if n:
                last_norm(n - 1)
        last_norm(NTILE - 1)

    @block.tensor
    def _(pe):
        for g in range(2 * NTILE):
            n, q = g // 2, g % 2
            r = ROWS[n]
            if g >= 2:
                pe.wait_ge(S["x_turned_taken"], g - 1)
            for k in range(4):
                last = pe.transpose(bank[g % 2][:, k * P:k * P + r], HN[0:r, n, 4 * q + k:D:KD], ident[0:r, 0:r])
            last.then_inc(S["x_turned"], 1)

        def turn_embedding(n):
            r = ROWS[n]
            if n >= 2:
                pe.wait_ge(S["emb_taken"], n - 1)
            for k in range(2):
                last = pe.transpose(bank[4 + n % 2][:, k * P:k * P + r], pin[0:r, n, k * P:(k + 1) * P], ident[0:r, 0:r])
            last.then_inc(S["emb_turned"], 1)

        def project_embedding(g):
            n, q = g // 2, g % 2
            r = ROWS[n]
            if g >= 4:
                pe.wait_ge(S["emb_projection_taken"], g - 3)
            for k in range(2):
                last = pe.matmul(bank[4 + g % 4][0:r, :], pT[:, k, n * P:n * P + r], wproj[:, k, 512 * q:512 * q + 512], start=(k == 0), stop=(k == 1))
            last.then_inc(S["emb_projected"], 1)

        turn_embedding(0)
        pe.wait_ge(S["x_turned_taken"], 2 * NTILE)
        for h in range(2):
            for k in range(KD):
                last = pe.matmul(bank[2 + h][0:36, 0:HT], wr[:, k, :], hT[:, k, h * HT:(h + 1) * HT], start=(k == 0), stop=(k == KD - 1))
        last.then_inc(S["logits_ready"], 1)
        turn_embedding(1)
        pe.wait_ge(S["logits_taken"], 1)
        for m in range(NTILE):
            last = pe.transpose(bank[0][0:ROWS[m], m * 36:(m + 1) * 36], LT[:, m * P:m * P + ROWS[m]], ident[0:36, 0:36])
        last.then_inc(S["logits_turned"], 1)
        for n in range(2, NTILE):
            turn_embedding(n)
        pe.wait_ge(S["emb_taken"], NTILE)
        for g in range(EARLY):
            project_embedding(g)
        pe.wait_ge(S["choices_ready"], 1)
        ee = EE.rearrange("p n x -> p (n x)")
        pe.matmul(bank[0][:, 256:416], c_("tri"), ee, start=True, stop=True)
        pe.matmul(bank[1][:, 0:160], c_("ones"), ee, start=True, stop=True).then_inc(S["counts_ready"], 1)
        for g in range(EARLY, 2 * NTILE):
            project_embedding(g)
        for _ in range(U):
            pe.nop().then_inc(S["rows_turned"], 1)
        for _ in range(2):
            pe.nop().then_inc(S["gate_up_ready"], 1)
        pe.wait_ge(S["emb_projection_taken"], 2 * NTILE)
        pe.wait_ge(S["plan_ready"], 1)
        more_turns = pe.value_load(inb[0:1, :], min_val=0, max_val=NOV // U)
        n_turns, last_turn = more_turns + E_ALL // U, more_turns + (E_ALL // U - 1)

        def turn(b, x, w, turn_no):
            pe.wait_ge(rows_gathered[w], turn_no)
            if not isinstance(b, int) or b:
                pe.wait_ge(S["rows_taken"], b)
            pe.nop().then_inc(S["rows_may_turn"], 1)
            for k in range(KD):
                last = pe.transpose(bank[0][:, k * CAP:(k + 1) * CAP], xg[w][:, k:D:KD], ident[0:CAP, 0:CAP])
            last.then_inc(S["rows_turned"], 1)

        def gate_up(b, x, w, turn_no):
            pe.wait_ge(S["rows_taken"], b + 1)
            pe.wait_ge(expert_loaded[w], turn_no)
            gu = wexp[:, w, 0:4096].rearrange("p (k f) -> p k f", k=KD)
            for k in range(KD):
                last = pe.matmul(bank[2 + x][0:CAP, :], xgT[x][:, k, :], gu[:, k, :], start=(k == 0), stop=(k == KD - 1))
            last.then_inc(S["gate_up_ready"], 1)
            
        def turn_hidden(b, x):
            pe.wait_ge(S["hidden_ready"], b + 1)
            if not isinstance(b, int) or b:
                pe.wait_ge(S["hidden_taken"], b)
            pe.nop().then_inc(S["hidden_may_turn"], 1)
            for k in range(2):
                last = pe.transpose(bank[1][:, k * CAP:(k + 1) * CAP], hid[x][:, k:DE:2], ident[0:CAP, 0:CAP])
            last.then_inc(S["hidden_turned"], 1)

        def down(b, x, w, first):
            pe.wait_ge(S["hidden_taken"], b + 1)
            if not first:
                pe.wait_ge(S["block_taken"], b - 1)
            dn = wexp[:, w, 4096:6144].rearrange("p (k m) -> p k m", k=2)
            for q in range(2):
                for k in range(2):
                    last = pe.matmul(bank[4 + 2 * x + q][0:CAP, :], hidT[x][:, k, :], dn[:, k, 512 * q:512 * q + 512], start=(k == 0), stop=(k == 1))
            last.then_inc(S["block_ready"], 1)

        turn(0, 0, 0, 16)
        gate_up(0, 0, 0, 48)
        turn(1, 1, 1, 16)
        turn_hidden(0, 0)

        def step(i, k, more, first=False):
            b = U * i + k
            gate_up(b, k % 2, k % U, 48 * (i + k // U + 1))
            if more:
                turn(b + 1, (k + 1) % 2, (k + 1) % U, 16 * (i + (k + 1) // U + 1))
            down(b - 1, (k + 1) % 2, k - 1, first)
            turn_hidden(b, k % 2)

        for k in range(1, U + 1):
            step(0, k, True, first=(k <= 2))
        with pe.Fori(1, last_turn) as i:
            for k in range(1, U + 1):
                step(i, k, True)
        for k in range(1, U):
            step(last_turn, k, k < U - 1)
        down(U * last_turn + (U - 1), 1, U - 1, False)
        def turn_normed(n):
            r = ROWS[n]
            pe.wait_ge(S["x_normed"], n + 1)
            for g in (2 * n, 2 * n + 1):
                if g >= 2:
                    pe.wait_ge(S["normed_taken"], g - 1)
                for k in range(4):
                    last = pe.transpose(bank[g % 2][:, k * P:k * P + r], xn[n % 2][0:r, 4 * (g % 2) + k:D:KD], ident[0:r, 0:r])
                last.then_inc(S["normed_turned"], 1)

        def gate(n):
            r = ROWS[n]
            pe.wait_ge(S["normed_taken"], 2 * n + 2)
            for g in (2 * n, 2 * n + 1):
                if g >= 4:
                    pe.wait_ge(S["gate_sigmoid_ready"], g - 3)
                for k in range(KD):
                    last = pe.matmul(bank[4 + g % 4][0:r, :], hT[:, k, n * P:n * P + r], WG[:, k, 512 * (g % 2):512 * (g % 2) + 512], start=(k == 0), stop=(k == KD - 1))
                last.then_inc(S["gate_ready"], 1)

        turn_normed(0)
        turn_normed(1)
        pe.wait_ge(S["gate_weights_loaded"], 16)
        pe.wait_ge(S["block_taken"], U * n_turns)
        gate(0)
        turn_normed(2)
        turn_normed(3)
        gate(1)
        turn_normed(4)
        gate(2)
        gate(3)
        gate(4)


def program(nc, a, o):
    with ExitStack() as ctx:
        BIG = ctx.enter_context(nc.sbuf_tensor("BIG", [P, 8 * 4 * T], F32))
        kept = [ctx.enter_context(nc.sbuf_tensor(n, s, F32)) for n, s in
                (("cst2", [P, NCONST2]), ("wr", [P, KD, 36]), ("gffn", [P, KD]), ("gple", [P, KD]), ("bias", [P, 36]))]
        PB = [ctx.enter_context(nc.psum_tensor(f"PB{i}", [P, 2, 512], F32)) for i in range(2)]
        PQ = [ctx.enter_context(nc.psum_tensor(f"PQ{i}", [P, 512], F32)) for i in range(4)]
        bank = [PB[0][:, 0, :], PB[0][:, 1, :], PB[1][:, 0, :], PB[1][:, 1, :]] + [q[:, :] for q in PQ]
        with nc.cleanup_on_exit():
            with ExitStack() as half:
                mixer(nc, a, o, half, BIG[:, :], PB, PQ, bank, kept)
        with ExitStack() as half:
            experts(nc, a, o, half, BIG[:, :], bank, kept)


def kernel(**inputs):
    import concourse.bacc as _bacc
    from concourse.bass_utils import run_bass_kernel_spmd as _run
    nc = _bacc.Bacc("TRN2", target_bir_lowering=False, num_devices=1)
    arrays, a = {}, {}
    for n, x in dict(inputs, consts=make_consts(), consts2=make_consts_moe()).items():
        x = np.ascontiguousarray(x)
        arrays["in_" + n] = x
        a[n] = nc.dram_tensor("in_" + n, x.shape, mybir.dt.from_np(x.dtype), kind="ExternalInput").ap()
    o = {}
    for n, s in (("y_prompt", (1, NPR, D)), ("y_sample", (NB, TS, D)), ("pool_prompt", (1, 1, 15, 512)), ("shift_prompt", (1, 1, 1792)),
                 ("wkv_prompt", (1, 1, 8, 64, 64)), ("pool_sample", (1, 8, 15, 512)), ("shift_sample", (1, 8, 1792)), ("wkv_sample", (1, 8, 8, 64, 64))):
        o[n] = nc.dram_tensor("out_" + n, s, F32, kind="ExternalOutput").ap()
    program(nc, a, o)
    r = _run(nc, [arrays], core_ids=[0]).results[0]
    return tuple(r["out_" + n] for n in o)
```
